# Optimizing a Trainium2 kernel written in Bass

```python
import math
import jax, jax.numpy as jnp
from jax import lax
import numpy as np

D_MODEL = 1024
BATCH = 1
SEQ = 512
DEPTH = 2
DEC_BATCH = 8
DEC_SEQ = 4
PAST_LEN = 4096
PAGE_SIZE = 128

N_HEADS = 4
HEAD_K = 128
HEAD_V = 128
MIX_K = N_HEADS * HEAD_K
MIX_V = N_HEADS * HEAD_V
CONV_W = 4
CONV_DIM = 2 * MIX_K + MIX_V
CHUNK = 64
N_BRANCH = 3
D_FF = -(-8 * D_MODEL // (3 * 256)) * 256
ROPE_BASE = 10000.0
EPS = 1e-6
F_TINY = 1e-30

_SPLITS = (('gdn_q', MIX_K), ('gdn_k', MIX_K), ('gdn_v', MIX_V), ('gdn_z', MIX_V),
           ('gdn_a', N_HEADS), ('gdn_b', N_HEADS),
           ('ret_q', MIX_K), ('ret_k', MIX_K), ('ret_v', MIX_V), ('ret_g', MIX_V),
           ('hg_q', MIX_K), ('hg_f', MIX_K), ('hg_i', MIX_V), ('hg_g', MIX_V),
           ('merge', N_BRANCH * D_MODEL))
N_IN = sum(s for _, s in _SPLITS)

kernel_name = 'hybrid_gdn_retnet_hgrn2_gated_merge_step'

def _split_cols(proj):
    cols, off = {}, 0
    for name, size in _SPLITS:
        cols[name] = proj[..., off:off + size]
        off += size
    return cols

def _rmsnorm(x, g):
    xf = x.astype(jnp.float32)
    y = xf * lax.rsqrt(jnp.mean(xf * xf, axis=-1, keepdims=True) + EPS)
    return (y * g.astype(jnp.float32)).astype(x.dtype)

def _l2norm(x):
    return x * lax.rsqrt(jnp.sum(x * x, axis=-1, keepdims=True) + EPS)

def _heads(t, d):
    B, L, _ = t.shape
    return t.reshape(B, L, N_HEADS, d).transpose(0, 2, 1, 3)

def _rope(x, pos):
    half = x.shape[-1] // 2
    inv = ROPE_BASE ** (-jnp.arange(half, dtype=jnp.float32) / half)
    ang = pos.astype(jnp.float32)[:, None] * inv[None, :]
    cos, sin = jnp.cos(ang), jnp.sin(ang)
    x1, x2 = x[..., :half], x[..., half:]
    return jnp.concatenate([x1 * cos - x2 * sin, x1 * sin + x2 * cos], axis=-1)

def _masked_exp(mask, z):
    return jnp.where(mask, jnp.exp(jnp.where(mask, z, 0.0)), 0.0)

def _to_chunks(t, n, C):
    B, H = t.shape[0], t.shape[1]
    return jnp.moveaxis(t.reshape(B, H, n, C, *t.shape[3:]), 2, 0)

def _from_chunks(o):
    n, B, H, C, d = o.shape
    return jnp.moveaxis(o, 0, 2).reshape(B, H, n * C, d)

def _gated_delta_chunked(q, k, v, g, beta, S0):
    L = q.shape[2]
    dv = v.shape[-1]
    C = math.gcd(L, CHUNK)
    n = L // C
    incl = jnp.tril(jnp.ones((C, C), bool))
    strict = jnp.tril(jnp.ones((C, C), bool), -1)
    eye = jnp.eye(C, dtype=jnp.float32)

    def step(S, inp):
        qi, ki, vi, gi, bi = inp
        G = jnp.cumsum(gi, axis=-1)
        decay = _masked_exp(incl, G[..., :, None] - G[..., None, :])
        A = jnp.where(strict, bi[..., None] * jnp.einsum('bhtd,bhsd->bhts', ki, ki) * decay, 0.0)
        rhs = jnp.concatenate([bi[..., None] * vi, (bi * jnp.exp(G))[..., None] * ki], axis=-1)
        sol = lax.linalg.triangular_solve(eye + A, rhs, left_side=True, lower=True, unit_diagonal=True)
        u = sol[..., :dv] - jnp.einsum('bhtk,bhkv->bhtv', sol[..., dv:], S)
        scores = jnp.einsum('bhtd,bhsd->bhts', qi, ki) * decay
        o = (jnp.exp(G)[..., None] * jnp.einsum('bhtk,bhkv->bhtv', qi, S)
             + jnp.einsum('bhts,bhsv->bhtv', scores, u))
        k_end = ki * jnp.exp(G[..., -1:] - G)[..., None]
        S_new = jnp.exp(G[..., -1])[..., None, None] * S + jnp.einsum('bhsk,bhsv->bhkv', k_end, u)
        return S_new, o

    xs = tuple(_to_chunks(t, n, C) for t in (q, k, v, g, beta))
    S, o = lax.scan(step, S0, xs)
    return _from_chunks(o), S

def _retention_chunked(q, k, v, log_gamma, S0):
    L = q.shape[2]
    C = math.gcd(L, CHUNK)
    n = L // C
    idx = jnp.arange(C, dtype=jnp.float32)
    rel = idx[:, None] - idx[None, :]
    lg = log_gamma[:, None, None]
    D = _masked_exp(rel >= 0, lg * rel)
    inner = jnp.exp(log_gamma[:, None] * (idx + 1.0))
    to_end = jnp.exp(log_gamma[:, None] * (C - 1.0 - idx))
    chunk_dec = jnp.exp(log_gamma * C)

    def step(S, inp):
        qi, ki, vi = inp
        scores = jnp.einsum('bhtd,bhsd->bhts', qi, ki) * D
        o = (jnp.einsum('bhts,bhsv->bhtv', scores, vi)
             + inner[..., None] * jnp.einsum('bhtk,bhkv->bhtv', qi, S))
        S_new = chunk_dec[:, None, None] * S + jnp.einsum('bhsk,bhsv->bhkv', ki * to_end[..., None], vi)
        return S_new, o

    xs = tuple(_to_chunks(t, n, C) for t in (q, k, v))
    S, o = lax.scan(step, S0, xs)
    return _from_chunks(o), S

def _hgrn2_chunked(q, k, v, log_f, S0):
    L = q.shape[2]
    C = math.gcd(L, CHUNK)
    n = L // C
    incl = jnp.tril(jnp.ones((C, C), bool))[:, :, None]

    def step(S, inp):
        qi, ki, vi, gi = inp
        A = jnp.cumsum(gi, axis=2)
        w = _masked_exp(incl, A[:, :, :, None, :] - A[:, :, None, :, :])
        scores = jnp.einsum('bhtd,bhsd,bhtsd->bhts', qi, ki, w)
        o = (jnp.einsum('bhts,bhsv->bhtv', scores, vi)
             + jnp.einsum('bhtk,bhkv->bhtv', qi * jnp.exp(A), S))
        S_new = (jnp.exp(A[:, :, -1])[..., None] * S
                 + jnp.einsum('bhsk,bhsv->bhkv', ki * jnp.exp(A[:, :, -1:] - A), vi))
        return S_new, o

    xs = tuple(_to_chunks(t, n, C) for t in (q, k, v, log_f))
    S, o = lax.scan(step, S0, xs)
    return _from_chunks(o), S

def _token_mixers(h, s_gdn, s_conv, s_ret, s_hg, pos, lb, w_in, conv_w, a_log, dt_bias,
                  gdn_g, hg_g, w_branch, w_out):
    B, L, _ = h.shape
    f32 = jnp.float32
    proj = h @ w_in
    cols = _split_cols(proj)

    xpad = jnp.concatenate([s_conv.astype(proj.dtype), proj[..., :CONV_DIM]], axis=1)
    conv = xpad[:, 0:L] * conv_w[0]
    for j in range(1, CONV_W):
        conv = conv + xpad[:, j:j + L] * conv_w[j]
    qkv = jax.nn.silu(conv.astype(f32))
    new_conv = xpad[:, L:]
    q_a = _l2norm(_heads(qkv[..., :MIX_K], HEAD_K)) * HEAD_K ** -0.5
    k_a = _l2norm(_heads(qkv[..., MIX_K:2 * MIX_K], HEAD_K))
    v_a = _heads(qkv[..., 2 * MIX_K:], HEAD_V)
    g_a = -jnp.exp(a_log.astype(f32)) * jax.nn.softplus(cols['gdn_a'].astype(f32) + dt_bias.astype(f32))
    beta = jax.nn.sigmoid(cols['gdn_b'].astype(f32))
    o_a, new_gdn = _gated_delta_chunked(q_a, k_a, v_a, g_a.transpose(0, 2, 1), beta.transpose(0, 2, 1),
                                        s_gdn.astype(f32))
    o_a = _rmsnorm(o_a.transpose(0, 2, 1, 3), gdn_g) * jax.nn.silu(
        cols['gdn_z'].astype(f32).reshape(B, L, N_HEADS, HEAD_V))
    o_a = o_a.reshape(B, L, MIX_V)

    q_b = _rope(_heads(cols['ret_q'].astype(f32), HEAD_K), pos)
    k_b = _rope(_heads(cols['ret_k'].astype(f32), HEAD_K), pos) * HEAD_K ** -0.5
    v_b = _heads(cols['ret_v'].astype(f32), HEAD_V)
    log_gamma = jnp.log1p(-jnp.exp2(-5.0 - jnp.arange(N_HEADS, dtype=f32)))
    o_b, new_ret = _retention_chunked(q_b, k_b, v_b, log_gamma, s_ret.astype(f32))
    o_b = o_b.transpose(0, 2, 1, 3)
    mu = jnp.mean(o_b, axis=-1, keepdims=True)
    var = jnp.mean(jnp.square(o_b - mu), axis=-1, keepdims=True)
    o_b = (o_b - mu) * lax.rsqrt(var + EPS) * jax.nn.silu(
        cols['ret_g'].astype(f32).reshape(B, L, N_HEADS, HEAD_V))
    o_b = o_b.reshape(B, L, MIX_V)

    z_f = _heads(cols['hg_f'].astype(f32), HEAD_K)
    lb_h = lb.reshape(N_HEADS, 1, HEAD_K)
    f_gate = jax.nn.sigmoid(z_f) + lb_h * jax.nn.sigmoid(-z_f)
    log_f = jnp.log(jnp.maximum(f_gate, F_TINY))
    k_c = (1.0 - lb_h) * jax.nn.sigmoid(-z_f)
    q_c = _heads(cols['hg_q'].astype(f32), HEAD_K)
    v_c = _heads(cols['hg_i'].astype(f32), HEAD_V)
    o_c, new_hg = _hgrn2_chunked(q_c, k_c, v_c, log_f, s_hg.astype(f32))
    o_c = _rmsnorm(o_c.transpose(0, 2, 1, 3), hg_g) * jax.nn.sigmoid(
        cols['hg_g'].astype(f32).reshape(B, L, N_HEADS, HEAD_V))
    o_c = o_c.reshape(B, L, MIX_V)

    ob = jnp.stack([o_a, o_b, o_c], axis=2).astype(h.dtype)
    branch = jnp.einsum('blnv,nvd->blnd', ob, w_branch)
    gates = jax.nn.sigmoid(cols['merge'].reshape(B, L, N_BRANCH, D_MODEL))
    merged = jnp.sum(gates * branch, axis=2)
    return merged @ w_out, (new_gdn, new_conv, new_ret, new_hg)

def _swiglu(h, w_gate_up, w_down):
    gu = h @ w_gate_up
    return (jax.nn.silu(gu[..., :D_FF]) * gu[..., D_FF:]) @ w_down

def _trunk(x, c, s_gdn, s_conv, s_ret, s_hg, pos0, params):
    (w_in, conv_w, gdn_a_log, gdn_dt_bias, gdn_norm, hgrn_lb, hgrn_norm, w_branch, w_out,
     w_ada, b_ada, norm_mix, norm_ffn, w_gate_up, w_down, final_norm) = params
    L = x.shape[1]
    pos = pos0 + jnp.arange(L, dtype=jnp.int32)
    lb_w = jax.nn.softmax(hgrn_lb.astype(jnp.float32), axis=0)
    lb_all = jnp.cumsum(lb_w, axis=0) - lb_w[0:1]
    cs = jax.nn.silu(c)
    out_gdn, out_conv, out_ret, out_hg = [], [], [], []
    for l in range(DEPTH):
        mod = (cs @ w_ada[l] + b_ada[l])[:, None, :]
        sh_m, sc_m, gt_m, sh_f, sc_f, gt_f = jnp.split(mod, 6, axis=-1)
        h = _rmsnorm(x, norm_mix[l]) * (1.0 + sc_m) + sh_m
        mix, (ng, nc, nr, nh) = _token_mixers(
            h, s_gdn[l], s_conv[l], s_ret[l], s_hg[l], pos, lb_all[l], w_in[l], conv_w[l],
            gdn_a_log[l], gdn_dt_bias[l], gdn_norm[l], hgrn_norm[l], w_branch[l], w_out[l])
        x = x + gt_m * mix.astype(x.dtype)
        h = _rmsnorm(x, norm_ffn[l]) * (1.0 + sc_f) + sh_f
        x = x + gt_f * _swiglu(h, w_gate_up[l], w_down[l])
        out_gdn.append(ng.astype(s_gdn.dtype))
        out_conv.append(nc.astype(s_conv.dtype))
        out_ret.append(nr.astype(s_ret.dtype))
        out_hg.append(nh.astype(s_hg.dtype))
    y = _rmsnorm(x, final_norm)
    return y, (jnp.stack(out_gdn), jnp.stack(out_conv), jnp.stack(out_ret), jnp.stack(out_hg))

def setup_inputs(seed: int = 0) -> dict:
    key = jax.random.key(seed)
    ks = jax.random.split(key, 32)
    f32 = jnp.float32

    def nrm(k, shape, s):
        return jax.random.normal(k, shape, f32) * s

    return {
        'x_prompt': nrm(ks[0], (BATCH, SEQ, D_MODEL), 1.0),
        'x_sample': nrm(ks[1], (DEC_BATCH, DEC_SEQ, D_MODEL), 1.0),
        'state_gdn': nrm(ks[2], (DEPTH, DEC_BATCH, N_HEADS, HEAD_K, HEAD_V), 0.1),
        'state_gdn_conv': nrm(ks[3], (DEPTH, DEC_BATCH, CONV_W - 1, CONV_DIM), 1.0),
        'state_ret': nrm(ks[4], (DEPTH, DEC_BATCH, N_HEADS, HEAD_K, HEAD_V), 0.1),
        'state_hgrn': nrm(ks[5], (DEPTH, DEC_BATCH, N_HEADS, HEAD_K, HEAD_V), 0.1),
        'c_prompt': nrm(ks[6], (BATCH, D_MODEL), 1.0),
        'c_sample': nrm(ks[7], (DEC_BATCH, D_MODEL), 1.0),
        'w_in': nrm(ks[8], (DEPTH, D_MODEL, N_IN), D_MODEL ** -0.5),
        'conv_w': nrm(ks[9], (DEPTH, CONV_W, CONV_DIM), CONV_W ** -0.5),
        'gdn_a_log': jnp.log(jax.random.uniform(ks[10], (DEPTH, N_HEADS), f32, 1.0, 16.0)),
        'gdn_dt_bias': nrm(ks[11], (DEPTH, N_HEADS), 0.1),
        'gdn_norm': 1.0 + nrm(ks[12], (DEPTH, HEAD_V), 0.02),
        'hgrn_lb': nrm(ks[13], (DEPTH, MIX_K), 0.5),
        'hgrn_norm': 1.0 + nrm(ks[14], (DEPTH, HEAD_V), 0.02),
        'w_branch': nrm(ks[15], (DEPTH, N_BRANCH, MIX_V, D_MODEL), MIX_V ** -0.5),
        'w_out': nrm(ks[16], (DEPTH, D_MODEL, D_MODEL), D_MODEL ** -0.5),
        'w_ada': nrm(ks[17], (DEPTH, D_MODEL, 6 * D_MODEL), 0.5 * D_MODEL ** -0.5),
        'b_ada': nrm(ks[18], (DEPTH, 6 * D_MODEL), 0.01),
        'norm_mix': 1.0 + nrm(ks[19], (DEPTH, D_MODEL), 0.02),
        'norm_ffn': 1.0 + nrm(ks[20], (DEPTH, D_MODEL), 0.02),
        'w_gate_up': nrm(ks[21], (DEPTH, D_MODEL, 2 * D_FF), D_MODEL ** -0.5),
        'w_down': nrm(ks[22], (DEPTH, D_FF, D_MODEL), D_FF ** -0.5),
        'final_norm': 1.0 + nrm(ks[23], (D_MODEL,), 0.02),
    }

def reference(x_prompt, x_sample, state_gdn, state_gdn_conv, state_ret, state_hgrn, c_prompt, c_sample,
              w_in, conv_w, gdn_a_log, gdn_dt_bias, gdn_norm, hgrn_lb, hgrn_norm, w_branch, w_out,
              w_ada, b_ada, norm_mix, norm_ffn, w_gate_up, w_down, final_norm):
    params = (w_in, conv_w, gdn_a_log, gdn_dt_bias, gdn_norm, hgrn_lb, hgrn_norm, w_branch, w_out,
              w_ada, b_ada, norm_mix, norm_ffn, w_gate_up, w_down, final_norm)
    Bp = x_prompt.shape[0]
    zs = jnp.zeros((DEPTH, Bp, N_HEADS, HEAD_K, HEAD_V), state_gdn.dtype)
    zc = jnp.zeros((DEPTH, Bp, CONV_W - 1, CONV_DIM), state_gdn_conv.dtype)
    y_prompt, (gdn_p, conv_p, ret_p, hg_p) = _trunk(x_prompt, c_prompt, zs, zc, zs, zs, 0, params)
    y_sample, (gdn_s, conv_s, ret_s, hg_s) = _trunk(x_sample, c_sample, state_gdn, state_gdn_conv,
                                                    state_ret, state_hgrn, PAST_LEN, params)
    return (y_prompt, y_sample, gdn_p, conv_p, ret_p, hg_p, gdn_s, conv_s, ret_s, hg_s)


_drawn_inputs = setup_inputs


def setup_inputs(seed=0):
    import zlib

    import numpy as np

    out = dict(_drawn_inputs(seed))
    spreads = {}
    factors = {'gdn_dt_bias': 4.085,
     'gdn_norm': 30.067,
     'hgrn_norm': 25.355,
     'norm_ffn': 7.09,
     'final_norm': 8.391}
    for name, (base, spread) in spreads.items():
        noise = np.random.default_rng([zlib.crc32(name.encode()), seed]).standard_normal(out[name].shape)
        drawn = base * np.exp(spread * noise) if base else spread * noise
        out[name] = __import__('jax').numpy.asarray(drawn.astype(out[name].dtype))
    for name, factor in factors.items():
        out[name] = (out[name] * factor).astype(out[name].dtype)
    return out
```

```python
from contextlib import ExitStack

import numpy as np

import concourse.bass as bass
from concourse import mybir

F32 = mybir.dt.float32
F32R = mybir.dt.float32r
ALU = mybir.AluOpType
ACT = mybir.ActivationFunctionType
AX = mybir.AxisListType

P = 128
D = 1024
DEPTH = 2
SEQ = 512
NS, LS = 8, 4
H = 4
DFF = 2816
CONV_W = 4
PAST = 4096
EPS = 1e-6
F_TINY = 1e-30
LN_CUT = 2.0 ** -50
KD = D // P
HALF, PH, SH = 272, 256, 16
T = 2 * HALF
NCH = SEQ // P
SW = NS * LS
LEVELS = 8
S_LEVELS = 3
KF = 11
SLAB = KF * P
NCQ = 12

P_CONV = 0
P_NMIX = P_CONV + NCQ * CONV_W
P_NFFN = P_NMIX + KD
P_BADA = P_NFFN + KD
P_GNORM = P_BADA + 6 * KD
P_HNORM = P_GNORM + 1
P_ALOG = P_HNORM + 1
P_DT = P_ALOG + 1
P_W = P_DT + 1

C_ID = 0
C_MASK = C_ID + P
C_COS = C_MASK + LEVELS * P
C_SIN = C_COS + T
C_DRET = C_SIN + T
C_IRET = C_DRET + H * P
C_DRETS = C_IRET + H * P
C_IRETS = C_DRETS + H * SW
C_END = C_IRETS + H * SW
C_ENDS = C_END + H
C_RESET = C_ENDS + H
C_INCL = C_RESET + T
C_INCLS = C_INCL + P
C_SEQ = C_INCLS + SW
C_HOT = C_SEQ + NS
C_SEL = C_HOT + 64
C_ONE = C_SEL + 8 * P
C_W = C_ONE + P


def constants():
    f = np.float32
    c = np.zeros((P, C_W), f)
    c[:, C_ID:C_ID + P] = np.eye(P)
    s, t = np.arange(P)[:, None], np.arange(P)[None, :]
    masks = [s == t] + [(s // (2 * m) == t // (2 * m)) & (s // m % 2 == 0) & (t // m % 2 == 1)
                        for m in (1 << i for i in range(LEVELS - 1))]
    c[:, C_MASK:C_COS] = np.stack(masks, 1).reshape(P, -1)
    pos = np.concatenate([np.concatenate([np.arange(h * PH, (h + 1) * PH), PAST + np.tile(np.arange(LS), NS // 2)])
                          for h in range(2)]).astype(f)
    half = P // 2
    inv = (10000.0 ** (-np.arange(half) / half)).astype(f)
    ang = (inv[:, None] * pos[None, :]).astype(f)
    c[:, C_COS:C_SIN] = np.tile(np.cos(ang), (2, 1))
    c[:, C_SIN:C_DRET] = np.concatenate([-np.sin(ang), np.sin(ang)])
    lg = np.log1p(-np.exp2(-5.0 - np.arange(H)))
    scale = P ** -0.5
    for h in range(H):
        decay = np.where(s <= t, np.exp(lg[h] * (t - s)), 0.0) * scale
        c[:, C_DRET + h * P:C_DRET + (h + 1) * P] = decay
        c[:SW, C_DRETS + h * SW:C_DRETS + (h + 1) * SW] = (decay * (s // LS == t // LS))[:SW, :SW]
        c[:, C_IRET + h * P:C_IRET + (h + 1) * P] = np.exp(lg[h] * (t + 1))
        c[:, C_IRETS + h * SW:C_IRETS + (h + 1) * SW] = np.exp(lg[h] * (t[:, :SW] % LS + 1))
        c[:, C_END + h] = np.exp(lg[h] * (P - 1 - s[:, 0])) * scale
        c[:, C_ENDS + h] = np.exp(lg[h] * (LS - 1 - s[:, 0] % LS)) * scale
    reset = np.ones(T)
    for h in range(2):
        reset[[h * HALF, h * HALF + P]] = 0
        reset[h * HALF + PH:(h + 1) * HALF:LS] = 0
    c[:, C_RESET:C_INCL] = reset
    c[:, C_INCL:C_INCLS] = s <= t
    c[:SW, C_INCLS:C_SEQ] = ((s <= t) & (s // LS == t // LS))[:SW, :SW]
    c[:, C_SEQ:C_HOT] = s // LS == np.arange(NS)
    for i in range(8):
        c[:, C_HOT + 8 * i + i] = 1
        c[i, C_SEL + i * P:C_SEL + (i + 1) * P] = 1
        c[32 + i, C_SEL + i * P:C_SEL + (i + 1) * P] = 1
    c[:, C_ONE:C_W] = 1
    return c


class Counts:

    def __init__(self, eng, own):
        self.eng, self.own, self.n = eng, own, {}
        self.reg, self.per, self.before = None, {}, {}

    def value(self, sem, n):
        return n if self.reg is None else n + self.reg * self.per[sem]

    def next(self, sem, n=1):
        self.n[sem] = self.n.get(sem, 0) + n
        self.eng.wait_ge(sem, self.value(sem, self.n[sem]))

    def peek(self, sem, ahead=1):
        self.eng.wait_ge(sem, self.value(sem, self.n.get(sem, 0) + ahead))

    def skip(self, sem, n=1):
        self.n[sem] = self.n.get(sem, 0) + n

    def link(self, ins):
        self.n[self.own] = self.n.get(self.own, 0) + 1
        ins.then_inc(self.own, 1)

    def settle(self):
        self.eng.wait_ge(self.own, self.value(self.own, self.n[self.own]))

    def begin(self, reg, per):
        self.reg, self.per, self.before = reg, per, dict(self.n)

    def end(self, passes):
        for sem, k in self.per.items():
            got = self.n.get(sem, 0) - self.before.get(sem, 0)
            assert got == k, (sem, got, k)
            self.n[sem] += k * (passes - 1)
        assert all(self.n[s] == self.before.get(s, 0) for s in self.n if s not in self.per)
        self.reg, self.per = None, {}


def trunk(nc, consts_in, x_in, c_in, params_in, fnorm_in, lb_in, conv_in, w_first, w_ret, w_hg, w_mrg, w_brn, w_out,
          w_gu, w_dn, w_ada, s_gdn, s_ret, s_hg, y_out, gdn_p, conv_out, ret_p, hg_p, gdn_s, ret_s, hg_s):
    ctx = ExitStack()

    def sb(name, shape, dt=F32):
        return ctx.enter_context(nc.sbuf_tensor(name, shape, dt))

    sems = {}

    def sig(name):
        if name not in sems:
            sems[name] = ctx.enter_context(nc.semaphore(name))
        return sems[name]

    X = sb("x", [P, KD, T])
    HH = sb("h_hi_lo", [P, 2, KD, T], F32R)
    raw = sb("w_raw", [P, 2, SLAB])
    whl = sb("w_hi_lo", [P, 2, 2, SLAB], F32R)
    C = sb("consts", [P, C_W])
    PR = sb("params", [P, P_W])
    MOD = sb("mod", [P, 6 * KD, 1 + NS])
    LB = sb("lb", [P, DEPTH, H])
    LBC = sb("lb_layer", [P, 2, H])
    CS = sb("silu_c", [P, KD, 1 + NS])
    CONV0 = sb("conv_state", [P, NCQ, NS * 3])
    CONV1 = sb("conv_new", [P, NCQ, 3 + NS * 3])
    ST = sb("state", [P, H, P])
    FN = sb("final_norm", [P, KD])
    MISC = sb("misc", [P, 64])
    GTB = sb("gate_sample", [P, KD, NS])
    GTP = sb("gate_prompt", [P, KD])
    SCT = sb("gated_sample", [P, SW])
    SCG = sb("scale_gain", [P, KD, 1 + NS])
    SMP = sb("sample_cols", [P, 16, SW])
    CSM = sb("conv_sample", [P, SW])

    M1W = 7680
    XPW = 3 + SEQ + NS * (3 + LS)
    BRW = 20 * T
    with ExitStack() as mix:
        M1 = mix.enter_context(nc.sbuf_tensor("mix_temps", [P, M1W], F32))
        BR = mix.enter_context(nc.sbuf_tensor("branch", [P, BRW], F32))
        MG = mix.enter_context(nc.sbuf_tensor("merged", [P, KD, T], F32))
    MG_flat = MG[:, :, :].rearrange("p k t -> p (k t)")
    with ExitStack() as mix:
        OH = mix.enter_context(nc.sbuf_tensor("o_hi_lo", [P, 2, H, T], F32R))
        OT = mix.enter_context(nc.sbuf_tensor("o_temps", [P, M1W - 2 * H * T], F32))
    with ExitStack() as ffn:
        AH = ffn.enter_context(nc.sbuf_tensor("ffn_hi_lo", [P, 2, KF, T], F32R))
        FT = ffn.enter_context(nc.sbuf_tensor("ffn_temps", [P, 4, T], F32))
    GP = ctx.enter_context(nc.psum_tensor("gemm_psum", [P, 4, 512], F32))
    B = ctx.enter_context(nc.psum_tensor("mix_psum", [P, 4, 512], F32))

    brt = BR[:, :].rearrange("p (i t) -> p i t", t=T)

    def halves(ap):
        return ap.rearrange("p (a b) -> p a b", a=2)

    def prompt(ap):
        return halves(ap)[:, :, 0:PH]

    def sample(ap):
        return halves(ap)[:, :, PH:HALF]

    def by_seq(ap):
        return ap.rearrange("p a (b t) -> p a b t", t=LS)

    def cols(c):
        o = c // 2 * HALF + c % 2 * P
        return slice(o, o + P)

    ident = C[:, C_ID:C_ID + P]
    mask = C[:, C_MASK:C_COS].rearrange("p (l t) -> p l t", l=LEVELS)
    hot = C[:, C_HOT:C_SEL].rearrange("p (i j) -> p i j", i=8)
    sel = C[:, C_SEL:C_ONE].rearrange("p (i j) -> p i j", i=8)
    ones = C[:, C_ONE:C_W]
    reset = C[:, C_RESET:C_INCL]
    neg_a = MISC[0:H, 1:2]
    epsc = MISC[:, 2:3]
    onec = MISC[:, 3:4]

    def heads(o, w):
        return M1[:, o:o + H * w].rearrange("p (h t) -> p h t", h=H)

    BLK = H * P
    big = {n: heads(i * BLK, P) for i, n in enumerate(
        ("bgk", "kend", "v", "eg", "dt", "sc", "a", "l0", "l1", "t", "u", "x", "w", "uv", "qg"))}
    hgb = {n: heads((9 + i) * BLK, P) for i, n in enumerate(("qg", "ked", "eg", "kend", "v", "sc"))}
    hgb["xl"] = M1[:, 0:7 * BLK].rearrange("p (l h t) -> p l h t", l=LEVELS - 1, h=H)
    hgb["prod"] = M1[:, 7 * BLK:9 * BLK].rearrange("p (l t) -> p l t", l=LEVELS)
    NAR = H * SW
    names = ("eg", "dt", "sc", "a", "l0", "l1", "t", "u", "x", "w", "qg", "ut", "us", "ked")
    small = {n: heads(i * NAR, SW) for i, n in enumerate(names)}
    small["xl"] = M1[:, 3 * NAR:5 * NAR].rearrange("p (l h t) -> p l h t", l=S_LEVELS - 1, h=H)
    small["prod"] = M1[:, 6 * NAR:6 * NAR + S_LEVELS * SW].rearrange("p (l t) -> p l t", l=S_LEVELS)
    o = len(names) * NAR
    for i, n in enumerate(("bgk", "kend", "v")):
        small[n] = heads(o + i * BLK, P)
    o += 3 * BLK
    UM = M1[:, o:o + NS * P].rearrange("p (b v) -> p b v", b=NS)
    o += NS * P
    NSL = (M1W - o) // (NS * P)
    S8 = [M1[:, o + i * NS * P:o + (i + 1) * NS * P].rearrange("p (b v) -> p b v", b=NS) for i in range(NSL)]
    US = small["us"][0:SW, :, :].rearrange("p h t -> p (h t)")
    sq_m = [M1[:, i * T:(i + 1) * T] for i in range(2)]
    wide = [M1[:, i * T:(i + 1) * T] for i in range(2, 8)]
    sq_o = [OT[:, i * T:(i + 1) * T] for i in range(2)]
    RWO, VAL, SG = (OT[:, i * T:(i + 1) * T] for i in (2, 3, 4))
    RW = wide[0]
    LN1, LN2 = (M1[:, i * H * T:(i + 1) * H * T] for i in range(2))

    o = 16 * T
    XP = [BR[:, o + i * XPW:o + (i + 1) * XPW] for i in range(2)]
    ROW = BR[:, o:o + T]
    ROWS = BR[:, o + T:o + T + SW]
    o += T + SW
    COL = BR[:, o:o + 5 * 96].rearrange("p (c j) -> p c j", c=5)
    o += 5 * 96
    CE = BR[:, o:o + 5 * 12].rearrange("p (c j) -> p c j", c=5)
    CSMP = [MISC[:, 32:64], CSM[:, :]]
    ABROW = MG[0:64, 0, :]
    ADG = 4
    ada_group = [x[:, o:o + ADG * D].rearrange("p (n k) -> p n k", n=ADG) for x, o in ((BR, 0), (BR, ADG * D), (MG_flat, 0))]
    ada_slot = [M1[:, M1W - (i + 1) * D:M1W - i * D] for i in range(2)]

    stream = [("first", 17, 8, 8)]
    for n in range(3):
        if n:
            stream.append(("ret" if n == 1 else "hg", 16, 8, 8))
        stream.append((f"merge{n}", 16, 8, 4))
    stream += [("out", 8, 8, 8)]
    for f in range(2):
        stream += [(f"gu{f}", 22, 8, 8), (f"dn{f}", 8, KF, KF)]
    ADA_FIRST = {"ret": 2 * KD, "hg": 4 * KD}
    base, at = {}, 0
    for name, count, _, _ in stream:
        base[name] = at
        at += count

    def source(name, l, i, odd):
        if name == "first":
            return w_first[l, i]
        if name.startswith("merge"):
            n = int(name[-1])
            return (w_brn if odd else w_mrg)[l, n, i]
        if name in ("ret", "hg"):
            return {"ret": w_ret, "hg": w_hg}[name][l, i]
        if name == "out":
            return w_out[l, i]
        return {"gu": w_gu, "dn": w_dn}[name[:2]][l, int(name[-1]), i]

    landed = [sig("slab_landed_0"), sig("slab_landed_1")]
    hi_done, split_done, tile_done = sig("weights_hi"), sig("weights_split"), sig("gemm_tile_done")
    buf_free = [sig("gemm_buffer_0_free"), sig("gemm_buffer_1_free")]
    full = [sig(f"bank_{i}_full") for i in range(4)]
    free = [sig(f"bank_{i}_free") for i in range(4)]
    own = {e: sig(f"{e}_steps") for e in ("vector", "scalar", "gpsimd", "tensor")}

    def each_slab(eng, name, body, k=None, per=None, extra=None):
        _, count, _, _ = next(s for s in stream if s[0] == name)
        n0 = base[name]
        step = name.startswith("merge")
        first = 3 if name == "first" else 0
        for n in range(first):
            body(n0 + n, n, None)
        with eng.Fori(0, (count - first) // 2) as g:
            if extra:
                k.begin(g, per)
            for j in range(2):
                i = (g if step else 2 * g + first + j)
                body(n0 + first + j, i, g)
            if extra:
                extra(g)
                k.end((count - first) // 2)

    with nc.Block() as block:
        @block.sync
        def _(sp):
            sp.dma_start(C[:, :], consts_in[:, :]).then_inc(sig("consts_landed"), 16)
            sp.dma_start(X[:, :, :], x_in[:, :, :]).then_inc(sig("x_landed"), 16)
            sp.dma_start(CS[:, :, :], c_in[:, :, :]).then_inc(sig("c_landed"), 16)
            sp.dma_start(LB[:, :, :], lb_in[:, :, :]).then_inc(sig("lb_landed"), 16)
            sp.dma_start(FN[:, :], fnorm_in[:, :]).then_inc(sig("fnorm_landed"), 16)
            for s in ("consts_landed", "x_landed", "fnorm_landed"):
                sp.wait_ge(sig(s), 16)

        @block.scalar
        def _(act):
            act.wait_ge(sig("c_landed"), 16)
            act.activation(CS[:, :, :], CS[:, :, :], ACT.Silu)
            act.wait_ge(sig("lb_shifted"), 1)
            act.activation(LB[:, :, :], LB[:, :, :], ACT.Exp).then_inc(sig("lb_exp"), 1)

        @block.vector
        def _(dve):
            k = Counts(dve, own["vector"])
            k.link(dve.memset(MISC[:, :], 0.0))
            k.settle()
            k.link(dve.memset(epsc, EPS))
            k.link(dve.memset(onec, 1.0))
            dve.wait_ge(sig("lb_landed"), 16)
            top, tot = MISC[:, 8:8 + H], MISC[:, 12:12 + H]
            k.settle()
            k.link(dve.tensor_copy(top, LB[:, 0, :]))
            for l in range(1, DEPTH):
                k.settle()
                k.link(dve.tensor_tensor(top, top, LB[:, l, :], ALU.max))
            k.settle()
            dve.tensor_tensor(LB[:, :, :], LB[:, :, :], top.unsqueeze(1).broadcast_to([P, DEPTH, H]),
                              ALU.subtract).then_inc(sig("lb_shifted"), 1)
            dve.wait_ge(sig("lb_exp"), 1)
            k.link(dve.tensor_copy(tot, LB[:, 0, :]))
            for l in range(1, DEPTH):
                k.settle()
                k.link(dve.tensor_tensor(tot, tot, LB[:, l, :], ALU.add))
            k.settle()
            k.link(dve.reciprocal(tot, tot))
            k.settle()
            k.link(dve.tensor_tensor(LB[:, :, :], LB[:, :, :], tot.unsqueeze(1).broadcast_to([P, DEPTH, H]), ALU.mult))
            k.settle()
            k.link(dve.tensor_copy(top, LB[:, 0, :]))
            for l in range(1, DEPTH):
                k.settle()
                k.link(dve.tensor_tensor(LB[:, l, :], LB[:, l, :], LB[:, l - 1, :], ALU.add))
            k.settle()
            k.link(dve.tensor_tensor(LB[:, :, :], LB[:, :, :], top.unsqueeze(1).broadcast_to([P, DEPTH, H]),
                                     ALU.subtract))
            k.settle()

    def clear():
        for s in sems.values():
            nc.sync.sem_clear(s)
        nc.all_engine_barrier()

    clear()

    with nc.Fori(0, DEPTH) as l:
        with nc.Block() as block:
            @block.sync
            def _(sp):
                k = Counts(sp, None)
                sp.dma_start(PR[:, :], params_in[l]).then_inc(sig("params_landed"), 16)
                sp.dma_start(CONV0[:, :, :], conv_in[l]).then_inc(sig("conv_landed"), 16)
                for i in range(2 * KD // ADG):
                    if i >= 3:
                        sp.wait_ge(sig("ada_group_used"), i - 2)
                    sp.dma_start(ada_group[i % 3], w_ada[l, i * ADG:(i + 1) * ADG].rearrange("n p k -> p n k")
                                 ).then_inc(sig(f"ada_group_landed_{i}"), 16)

                def ada_pair(first):
                    def load(g):
                        for j in range(2):
                            k.next(sig(f"ada_slot_{j}_free"))
                            sp.dma_start(ada_slot[j], w_ada[l, 2 * g + first + j]).then_inc(sig(f"ada_landed_{j}"), 16)
                    return load

                def states(n):
                    s_in, s_out, p_out = ((s_gdn, gdn_s, gdn_p), (s_ret, ret_s, ret_p), (s_hg, hg_s, hg_p))[n]
                    k.next(sig("prompt_state_done"))
                    sp.dma_start(p_out[l].rearrange("h k v -> k h v"), ST[:, :, :]).then_inc(sig("stored_prompt"), 16)

                    def load(h):
                        sp.dma_start(S8[h % NSL], s_in[l, :, h].rearrange("b k v -> k b v")
                                     ).then_inc(sig(f"state_landed_{h % NSL}"), 16)

                    for h in range(min(NSL, H)):
                        load(h)
                    for h in range(H):
                        k.next(sig("sample_state_done"))
                        sp.dma_start(s_out[l, :, h].rearrange("b k v -> k b v"), S8[h % NSL]
                                     ).then_inc(sig(f"stored_sample_{h % NSL}"), 16)
                        if h + NSL < H:
                            k.next(sig(f"stored_sample_{h % NSL}"), 16)
                            load(h + NSL)

                for seg in stream:
                    def load_slab(n, i, g):
                        odd = (n - base[seg[0]]) % 2 == 1
                        words = seg[3 if odd else 2] * P
                        if n >= 2:
                            sp.wait_ge(split_done, n - 1 if g is None else n - 1 + 2 * g)
                        sp.dma_start(raw[:, n % 2, 0:words], source(seg[0], l, i, odd)).then_inc(landed[n % 2], 16)

                    if seg[0] in ADA_FIRST:
                        each_slab(sp, seg[0], load_slab, k, {sig("ada_slot_0_free"): 1, sig("ada_slot_1_free"): 1},
                                  ada_pair(ADA_FIRST[seg[0]]))
                        for j in range(2):
                            k.skip(sig(f"ada_slot_{j}_free"))
                    else:
                        each_slab(sp, seg[0], load_slab)
                    if seg[0] in ("first", "ret", "hg"):
                        states(("first", "ret", "hg").index(seg[0]))
                sp.wait_ge(sig("conv_saved"), 1)
                sp.dma_start(conv_out[l], CONV1[:, :, :]).then_inc(sig("stored_conv"), 16)
                sp.wait_ge(sig("stored_conv"), 16)
                sp.wait_ge(sig("stored_prompt"), 16 * 3)
                for i in range(NSL):
                    sp.wait_ge(sig(f"stored_sample_{i}"), 16 * 3 * len(range(i, H, NSL)))

            @block.gpsimd
            def _(pool):
                for seg in stream:
                    def split(n, i, g):
                        odd = (n - base[seg[0]]) % 2 == 1
                        words = seg[3 if odd else 2] * P

                        def at(v, per):
                            return v if g is None else v + per * g
                        if n >= 2:
                            pool.wait_ge(tile_done, at(n - 1, 2))
                        pool.wait_ge(landed[n % 2], at(16 * (n // 2 + 1), 16))
                        src, hi, lo = raw[:, n % 2, 0:words], whl[:, n % 2, 0, 0:words], whl[:, n % 2, 1, 0:words]
                        pool.tensor_tensor(hi, src, ones[:, 0:1].broadcast_to([P, words]), ALU.mult).then_inc(hi_done, 1)
                        pool.wait_ge(hi_done, at(n + 1, 2))
                        pool.tensor_tensor(lo, src, hi.bitcast(F32), ALU.subtract).then_inc(split_done, 1)

                    each_slab(pool, seg[0], split)

            @block.tensor
            def _(pe):
                k = Counts(pe, own["tensor"])
                pe.nop().then_inc(sig("square_slot_free"), 2)

                def acquire(b):
                    k.next(free[b])

                def ada(weights, out):
                    w = weights.rearrange("p (k m) -> p k m", k=KD)
                    for kk in range(KD):
                        mm = pe.matmul(out, w[:, kk, :], CS[:, kk, :], start=kk == 0, stop=kk == KD - 1)
                    return mm

                def ada_pair(g):
                    for j in range(2):
                        k.next(sig(f"ada_landed_{j}"), 16)
                        ada(ada_slot[j], B[:, 0, bass.ds((2 * g + j) * (1 + NS), 1 + NS)]).then_inc(sig(f"ada_slot_{j}_free"), 1)

                def gemm(n, g, kt, rhs):
                    slot = n % 2
                    pe.wait_ge(split_done, n + 1 if g is None else n + 1 + 2 * g)
                    if n >= 2:
                        pe.wait_ge(buf_free[slot], n // 2 if g is None else n // 2 + g)
                    for kk in range(kt):
                        for p, (a, b) in enumerate(((0, 0), (0, 1), (1, 0))):
                            for h in range(2):
                                mm = pe.matmul(GP[:, 2 * slot + h, 0:HALF], whl[:, slot, a, kk * P:(kk + 1) * P],
                                               rhs[:, b, kk, h * HALF:(h + 1) * HALF],
                                               start=kk == 0 and p == 0, stop=kk == kt - 1 and p == 2)
                    mm.then_inc(tile_done, 1)

                def segment(name, rhs, kt_even, kt_odd=None, rhs_odd=None):
                    def tile(n, i, g):
                        odd = (n - base[name]) % 2 == 1 and rhs_odd is not None
                        gemm(n, g, kt_odd if odd else kt_even, rhs_odd if odd else rhs)
                    if name in ADA_FIRST:
                        acquire(0)
                        each_slab(pe, name, tile, k, {sig("ada_landed_0"): 16, sig("ada_landed_1"): 16}, ada_pair)
                        pe.wait_ge(sig("ada_slot_1_free"), 1 + KD + (KD if name == "hg" else 0) + (name == "hg"))
                        pe.nop().then_inc(full[0], 1)
                    else:
                        each_slab(pe, name, tile)

                def feature_sums(count, lhs, rows, sq):
                    acquire(0)
                    acquire(1)
                    for i in range(count):
                        k.next(sig("square_ready"))
                        for h in range(2):
                            mm = pe.matmul(B[0:rows, h, 0:HALF], lhs(i), sq[i % 2][:, h * HALF:(h + 1) * HALF],
                                           start=i == 0, stop=i == count - 1)
                        mm.then_inc(sig("square_slot_free"), 1)

                def spread(rows, count):
                    k.next(sig("rows_ready"))
                    for i in range(count):
                        for h in range(2):
                            b = 2 * (i % 2) + h
                            acquire(b)
                            pe.matmul(B[:, b, 0:HALF], sel[0:8, i, :], rows[0:8, h * HALF:(h + 1) * HALF],
                                      start=True, stop=True).then_inc(full[b], 1)

                def operands(c):
                    if c < NCH:
                        return P, [[brt[:, g * H + h, cols(c)] for h in range(H)] for g in range(3)]
                    return SW, [[SMP[:, g * H + h, :] for h in range(H)] for g in range(3)]

                def hcol(bank, w, h, parts=P):
                    return B[0:parts, bank, h * w:(h + 1) * w]

                def per_head(bank, product):
                    acquire(bank)
                    for h in range(H):
                        mm = product(h)
                    mm.then_inc(full[bank], 1)

                def turn(bank, tiles, w):
                    per_head(bank, lambda h: pe.transpose(hcol(bank, P, h, w), tiles[h], ident))

                def out_and_state(t, val):
                    k.peek(free[3])
                    acquire(2)
                    for h in range(H):
                        pe.matmul(hcol(2, P, h), ST[:, h, :], t["qg"][:, h, :], start=True, stop=False)
                        mm = pe.matmul(hcol(2, P, h), val[:, h, :], t["sc"][:, h, :], start=False, stop=True)
                    mm.then_inc(full[2], 1)
                    per_head(3, lambda h: pe.matmul(hcol(3, P, h), t["kend"][:, h, :], val[:, h, :],
                                                    start=True, stop=True))

                def sample_heads(delta):
                    t = small
                    for h in range(H):
                        k.next(sig(f"state_landed_{h % NSL}"), 16)
                        st = S8[h % NSL]
                        val = t["v"][0:SW, h, :]
                        if delta:
                            acquire(1)
                            pe.matmul(B[:, 1, 0:SW], val, t["u"][0:SW, h, :], start=True, stop=False,
                                      skip_group_check=True)
                            for b in range(NS):
                                mm = pe.matmul(B[:, 1, b * LS:(b + 1) * LS], st[:, b, :],
                                               t["w"][:, h, b * LS:(b + 1) * LS], start=False, stop=b == NS - 1,
                                               skip_group_check=True)
                            mm.then_inc(full[1], 1)
                            acquire(1)
                            pe.transpose(B[0:SW, 1, 0:P], t["ut"][:, 0, :], ident).then_inc(full[1], 1)
                            k.peek(free[1])
                            val = US
                        acquire(2)
                        pe.matmul(B[:, 2, 0:SW], val, t["sc"][0:SW, h, :], start=True, stop=False,
                                  skip_group_check=True)
                        for b in range(NS):
                            mm = pe.matmul(B[:, 2, b * LS:(b + 1) * LS], st[:, b, :],
                                           t["qg"][:, h, b * LS:(b + 1) * LS], start=False, stop=b == NS - 1,
                                           skip_group_check=True)
                        mm.then_inc(full[2], 1)
                        k.next(sig("masked_values"))
                        for half, bank in ((0, 0), (1, 3)):
                            acquire(bank)
                            pe.matmul(B[:, bank, :], t["kend"][0:SW, h, :], UM[0:SW, 4 * half:4 * half + 4, :],
                                      start=True, stop=True).then_inc(full[bank], 1)

                def gdn(c):
                    w, (q, kk, v) = operands(c)
                    sm = c == NCH
                    t = small if sm else big
                    turn(0, kk, w)
                    turn(1, v, w)
                    for bank, r in ((2, kk), (3, q)):
                        per_head(bank, lambda h: pe.matmul(hcol(bank, w, h, w), kk[h], r[h], start=True, stop=True))
                    rows = ROWS if sm else ROW[:, cols(c)]
                    for bank, p0, m in ((0, 0, P), (1, 32, w)):
                        per_head(bank, lambda h: pe.matmul(hcol(bank, w, h, m), sel[p0:p0 + H, h, 0:m],
                                                           rows[p0:p0 + H, :], start=True, stop=True))
                    levels = S_LEVELS if sm else LEVELS
                    tt = uu = [ident[0:w, 0:w]] * H
                    for lv in range(1, levels):
                        k.next(sig("level_ready"))
                        if lv > 1:
                            k.peek(free[1])
                        al, xs = t["l0" if lv % 2 else "l1"], t["x"]
                        per_head(0, lambda h: pe.matmul(hcol(0, w, h, w), al[0:w, h, :], tt[h], start=True, stop=True))
                        k.peek(free[0])
                        if lv > 1:
                            k.peek(free[2])
                        if lv < levels - 1:
                            per_head(1, lambda h: pe.matmul(hcol(1, w, h, w), uu[h], xs[0:w, h, :],
                                                            start=True, stop=True))
                        per_head(2, lambda h: pe.matmul(hcol(2, w, h, w), xs[0:w, h, :], uu[h], start=True, stop=True))
                        tt = [t["t"][0:w, h, :] for h in range(H)]
                        uu = [t["u"][0:w, h, :] for h in range(H)]
                    k.peek(free[2])
                    per_head(0, lambda h: pe.matmul(hcol(0, w, h), t["bgk"][0:w, h, :], uu[h], start=True, stop=True))
                    k.peek(free[0])
                    k.next(sig("gated_q_ready"))
                    if sm:
                        sample_heads(True)
                        return
                    k.peek(free[3])
                    acquire(1)
                    for h in range(H):
                        pe.matmul(hcol(1, P, h), uu[h], t["v"][:, h, :], start=True, stop=False)
                        mm = pe.matmul(hcol(1, P, h), t["w"][:, h, :], ST[:, h, :], start=False, stop=True)
                    mm.then_inc(full[1], 1)
                    k.peek(free[1])
                    out_and_state(t, t["uv"])

                def ret(c):
                    w, (q, kk, v) = operands(c)
                    turn(0, kk, w)
                    turn(1, v, w)
                    per_head(3, lambda h: pe.matmul(hcol(3, w, h, w), kk[h], q[h], start=True, stop=True))
                    k.next(sig("chunk_ready"))
                    if c == NCH:
                        sample_heads(False)
                    else:
                        out_and_state(big, big["v"])

                def hg(c):
                    w, (q, kk, v) = operands(c)
                    t = small if c == NCH else hgb
                    levels = S_LEVELS if c == NCH else LEVELS
                    k.next(sig("kend_ready"))
                    turn(0, [t["ked"][:, h, :] for h in range(H)], w)
                    turn(1, v, w)
                    k.next(sig("levels_ready"))
                    for h in range(H):
                        for lv in range(levels):
                            bank = 2 + lv // 4
                            if lv % 4 == 0:
                                acquire(bank)
                            a, b = (kk[h], q[h]) if lv == 0 else (t["xl"][:, lv - 1, h, :],) * 2
                            mm = pe.matmul(hcol(bank, P, lv % 4, w)[:, 0:w], a, b, start=True, stop=True)
                            if lv % 4 == 3 or lv == levels - 1:
                                mm.then_inc(full[bank], 1)
                    k.next(sig("chunk_ready"))
                    if c == NCH:
                        sample_heads(False)
                    else:
                        out_and_state(t, t["v"])

                def out_norm(n):
                    if n == 1:
                        k.next(sig("outputs_ready"))
                        for i in range(H):
                            for h in range(2):
                                b = 2 * (i % 2) + h
                                acquire(b)
                                pe.matmul(B[:, b, 0:HALF], ones, brt[:, i, h * HALF:(h + 1) * HALF],
                                          start=True, stop=True).then_inc(full[b], 1)
                    feature_sums(H, lambda i: hot[:, i, :], 8, sq_o)
                    spread(RWO, H)

                feature_sums(KD, lambda i: ones, P, sq_m)
                acquire(2)
                for i in range(2 * KD // ADG):
                    k.next(sig(f"ada_group_landed_{i}"), 16)
                    for j in range(ADG):
                        mm = ada(ada_group[i % 3][:, j, :], B[:, 2, (i * ADG + j) * (1 + NS):(i * ADG + j + 1) * (1 + NS)])
                    mm.then_inc(sig("ada_group_used"), 1)
                k.next(sig("h_ready"))
                segment("first", HH, 8)
                feature_sums(2 * H, lambda i: hot[:, i, :], 8, sq_m)
                spread(RW, 2 * H)
                k.next(sig("gate_rows_ready"))
                per_head(0, lambda c: pe.transpose(B[:, 0, c * P:(c + 1) * P], ROW[:, cols(c)], ident))
                acquire(1)
                pe.transpose(B[0:SW, 1, 0:P], ROWS, ident).then_inc(full[1], 1)
                for n, (name, mixer) in enumerate((("first", gdn), ("ret", ret), ("hg", hg))):
                    if n:
                        segment(name, HH, 8)
                    k.next(sig("branch_ready"))
                    for c in range(NCH + 1):
                        mixer(c)
                    out_norm(n)
                    k.next(sig("o_ready"))
                    segment(f"merge{n}", HH, 8, 4, OH)
                k.next(sig("h_ready"))
                segment("out", HH, 8)
                feature_sums(KD, lambda i: ones, P, sq_m)
                k.next(sig("h_ready"))
                for f in range(2):
                    segment(f"gu{f}", HH, 8)
                    k.next(sig("act_ready"))
                    segment(f"dn{f}", AH, KF)

            @block.vector
            def _(dve):
                k = Counts(dve, own["vector"])

                def release(*banks):
                    k.settle()
                    for b in banks:
                        dve.nop().then_inc(free[b], 1)

                def say(name):
                    k.settle()
                    dve.nop().then_inc(sig(name), 1)

                def bc(ap, shape):
                    return ap.broadcast_to(shape)

                def norm_and_modulate(shift, scale, gain):
                    k.link(dve.scalar_tensor_tensor(
                        out=SCG[:, :, :], in0=MOD[:, scale:scale + KD, :], scalar=1.0,
                        in1=bc(PR[:, gain:gain + KD].unsqueeze(2), [P, KD, 1 + NS]), op0=ALU.add, op1=ALU.mult))
                    rstd, t, y = wide[0], wide[1], wide[2]
                    k.next(sig("root_ready"))
                    release(0, 1)
                    k.link(dve.reciprocal(rstd, rstd))
                    for i in range(KD):
                        k.settle()
                        k.link(dve.tensor_tensor(t, X[:, i, :], rstd, ALU.mult))
                        k.settle()
                        k.link(dve.tensor_scalar(prompt(y), prompt(t), SCG[:, i, 0:1], MOD[:, shift + i, 0:1],
                                                 ALU.mult, ALU.add))
                        g4 = SCG[:, i, 1:].rearrange("p (a b) -> p a b", a=2).unsqueeze(3)
                        s4 = MOD[:, shift + i, 1:].rearrange("p (a b) -> p a b", a=2).unsqueeze(3)
                        k.link(dve.tensor_tensor(by_seq(sample(y)), by_seq(sample(t)), bc(g4, [P, 2, 4, LS]), ALU.mult))
                        k.settle()
                        k.link(dve.tensor_tensor(by_seq(sample(y)), by_seq(sample(y)), bc(s4, [P, 2, 4, LS]), ALU.add))
                        k.settle()
                        k.link(dve.tensor_copy(HH[:, 0, i, :], y))
                        k.settle()
                        k.link(dve.tensor_tensor(HH[:, 1, i, :], y, HH[:, 0, i, :].bitcast(F32), ALU.subtract))
                    say("h_ready")

                def pairs(name, first, count, body, per):
                    n0 = base[name] + first
                    with dve.Fori(0, count // 2) as g:
                        k.begin(g, per)
                        for j in range(2):
                            body(n0 + j, g, j)
                        k.end(count // 2)

                def wait_tile(n, g):
                    dve.wait_ge(tile_done, n + 1 if g is None else n + 1 + 2 * g)

                def gp(n):
                    return GP[:, n % 2 * 2:n % 2 * 2 + 2, 0:HALF]

                def add_gated(name, gate):
                    def body(n, g, j):
                        wait_tile(n, g)
                        xi = X[:, 2 * g + j, :]
                        src, tmp = gp(n), SCT[:, :]
                        g4 = GTB[:, 2 * g + j, :].rearrange("p (a b) -> p a b", a=2)
                        k.link(dve.tensor_tensor(tmp.rearrange("p (a b t) -> p a b t", a=2, b=4),
                                                 by_seq(src[:, :, PH:HALF]), bc(g4.unsqueeze(3), [P, 2, 4, LS]), ALU.mult))
                        k.settle()
                        k.link(dve.tensor_tensor(sample(xi), sample(xi), tmp.rearrange("p (a b) -> p a b", a=2), ALU.add))
                        k.link(dve.scalar_tensor_tensor(
                            out=prompt(xi), in0=src[:, :, 0:PH], scalar=GTP[:, bass.ds(2 * g + j, 1)],
                            in1=prompt(xi), op0=ALU.mult, op1=ALU.add))
                        k.settle()
                        dve.nop().then_inc(buf_free[n % 2], 1)
                    k.link(dve.tensor_copy(GTB[:, :, :], MOD[:, gate:gate + KD, 1:]))
                    k.link(dve.tensor_copy(GTP[:, :], MOD[:, gate:gate + KD, 0]))
                    k.settle()
                    pairs(name, 0, 8, body, {own["vector"]: 6})

                for b in range(4):
                    dve.nop().then_inc(free[b], 1)
                dve.wait_ge(sig("params_landed"), 16)
                k.link(dve.tensor_copy(LBC[:, 0, :], LB[:, l, :]))
                k.settle()
                k.link(dve.tensor_scalar(LBC[:, 1, :], LBC[:, 0, :], -1.0, 1.0, ALU.mult, ALU.add))
                k.next(sig("a_exp"))
                k.link(dve.tensor_scalar(neg_a, neg_a, -1.0, None, ALU.mult))
                for i in range(2):
                    k.link(dve.memset(XP[i][:, 0:3], 0.0))

                def modulation(bank, first):
                    k.link(dve.tensor_tensor(
                        MOD[:, first:first + 2 * KD, :],
                        B[:, bank, 0:2 * KD * (1 + NS)].rearrange("p (i j) -> p i j", j=1 + NS),
                        bc(PR[:, P_BADA + first:P_BADA + first + 2 * KD].unsqueeze(2), [P, 2 * KD, 1 + NS]), ALU.add))
                    release(bank)

                dve.wait_ge(sig("ada_group_used"), 2 * KD // ADG)
                modulation(2, 0)
                norm_and_modulate(0, KD, P_NMIX)

                wait_tile(0, None)
                dve.tensor_copy(halves(ABROW), GP[0:64, 0:2, 0:HALF]).then_inc(buf_free[0], 1)
                dve.wait_ge(sig("conv_landed"), 16)

                def conv(n, g, j):
                    i = n - 1 if g is None else 2 * g + (n - 1)
                    xp = XP[n % 2]
                    xs = xp[:, 3 + SEQ:].rearrange("p (b t) -> p b t", b=NS)
                    cs = CSMP[n % 2].rearrange("p (b t) -> p b t", b=NS)
                    wait_tile(n, g)
                    k.link(dve.tensor_copy(halves(xp[:, 3:3 + SEQ]), gp(n)[:, :, 0:PH]))
                    dve.tensor_copy(xs[:, :, 3:].rearrange("p (a b) t -> p a b t", a=2),
                                    by_seq(gp(n)[:, :, PH:HALF])).then_inc(buf_free[n % 2], 1)
                    c0 = CONV0[:, i, :].rearrange("p (b t) -> p b t", b=NS)
                    k.link(dve.tensor_copy(xs[:, :, 0:3], c0))
                    k.settle()
                    c1 = CONV1[:, i, :]
                    k.link(dve.tensor_copy(c1[:, 0:3], xp[:, SEQ:SEQ + 3]))
                    k.link(dve.tensor_copy(c1[:, 3:].rearrange("p (b t) -> p b t", b=NS), xs[:, :, 4:7]))
                    k.next(sig("conv_slot_free"))
                    out = prompt(brt[:, i, :])
                    for tap in range(CONV_W):
                        wt = PR[:, bass.ds(i * CONV_W + tap, 1)]
                        xin = halves(xp[:, tap:tap + SEQ])
                        if tap == 0:
                            k.link(dve.tensor_scalar(out, xin, wt, None, ALU.mult))
                            k.link(dve.tensor_scalar(cs, xs[:, :, 0:LS], wt, None, ALU.mult))
                            k.settle()
                            continue
                        k.link(dve.scalar_tensor_tensor(out=out, in0=xin, scalar=wt, in1=out, op0=ALU.mult, op1=ALU.add))
                        ins = dve.scalar_tensor_tensor(out=cs, in0=xs[:, :, tap:tap + LS], scalar=wt, in1=cs,
                                                       op0=ALU.mult, op1=ALU.add)
                        if tap < CONV_W - 1:
                            k.link(ins)
                            k.settle()
                        else:
                            ins.then_inc(sig("conv_done"), 1)
                            k.settle()

                for n in (1, 2):
                    conv(n, None, n - 1)
                pairs("first", 3, 10, conv, {own["vector"]: 2 * 11, sig("conv_slot_free"): 2})
                say("conv_saved")

                def rows_of(rw, scale_q):
                    k.next(sig("root_ready"))
                    release(0, 1)
                    k.link(dve.reciprocal(rw[0:8, :], rw[0:8, :]))
                    if scale_q:
                        k.settle()
                        k.link(dve.tensor_scalar(rw[0:H, :], rw[0:H, :], float(P) ** -0.5, None, ALU.mult))
                    say("rows_ready")

                def bank_pair(i):
                    b = 2 * (i % 2)
                    k.next(full[b])
                    k.next(full[b + 1])
                    return B[:, b:b + 2, 0:HALF], b

                rows_of(RW, True)
                for i in range(2 * H):
                    src, b = bank_pair(i)
                    k.link(dve.tensor_tensor(halves(brt[:, i, :]), src, halves(brt[:, i, :]), ALU.mult))
                    release(b, b + 1)

                a1, a2 = wide[1][0:H, :], wide[2][0:H, :]
                k.link(dve.memset(ROW, 0.0))
                k.link(dve.memset(COL[:, NCH, :], 0.0))
                k.link(dve.tensor_scalar(a1, ABROW[0:H, :], PR[0:H, P_DT:P_DT + 1], None, ALU.add))
                k.settle()
                k.link(dve.tensor_scalar(a2, a1, -1.0, None, ALU.mult))
                k.settle()
                k.link(dve.tensor_tensor(a2, a1, a2, ALU.min))
                say("gate_args")
                k.next(sig("gate_logs"))
                k.link(dve.scalar_tensor_tensor(out=a1, in0=a1, scalar=0.0, in1=a2, op0=ALU.max, op1=ALU.add))
                k.settle()
                k.link(dve.tensor_scalar(a1, a1, neg_a, None, ALU.mult))
                k.settle()
                k.link(dve.tensor_tensor_scan(ROW[0:H, :], reset[0:H, :], a1, 0.0, ALU.mult, ALU.add))
                k.settle()
                k.link(dve.tensor_copy(ROW[32:32 + H, :], wide[3][32:32 + H, :]))
                g4 = prompt(ROW[0:H, :]).rearrange("p a (c t) -> p a c t", c=2)
                e4 = prompt(ROW[64:64 + H, :]).rearrange("p a (c t) -> p a c t", c=2)
                k.link(dve.tensor_tensor(e4, bc(g4[:, :, :, P - 1:P], [H, 2, 2, P]), g4, ALU.subtract))
                g4, e4 = by_seq(sample(ROW[0:H, :])), by_seq(sample(ROW[64:64 + H, :]))
                k.link(dve.tensor_tensor(e4, bc(g4[:, :, :, LS - 1:LS], [H, 2, 4, LS]), g4, ALU.subtract))
                k.settle()
                k.link(dve.tensor_copy(halves(ROWS), sample(ROW)))
                say("gate_rows_ready")
                k.next(full[0])
                k.link(dve.tensor_copy(COL[:, 0:NCH, :], B[:, 0, :].rearrange("p (c j) -> p c j", c=NCH)[:, :, 0:96]))
                release(0)
                k.next(full[1])
                k.link(dve.tensor_copy(COL[0:SW, NCH, :], B[0:SW, 1, 0:96]))
                release(1)
                say("gate_cols")
                k.next(sig("gate_exps"))
                k.link(dve.tensor_tensor(CE[:, :, 8:12], CE[:, :, 0:4], COL[:, :, 32:36], ALU.mult))

                def start_branch(tiles):
                    for i in range(0, tiles, H):
                        src = 16 if i == 12 else i
                        k.settle()
                        k.link(dve.tensor_copy(SMP[:, i:i + H, :].rearrange("p i (a b) -> p i a b", a=2),
                                               brt[:, src:src + H, :].rearrange("p i (a b) -> p i a b", a=2)[:, :, :, PH:]))
                    k.link(dve.memset(ST[:, :, :], 0.0))
                    say("branch_ready")

                def bank4(b, w=P, parts=P, inner=P):
                    return B[0:parts, b, 0:H * w].rearrange("p (h t) -> p h t", h=H)[:, :, 0:inner]

                def by_token(col, parts, w=P):
                    return bc(col.unsqueeze(2), [parts, H, w])

                def finish_chunk(eg, t, c):
                    k.next(full[2])
                    k.link(dve.tensor_copy(brt[:, 0:H, cols(c)], bank4(2)))
                    release(2)
                    k.next(full[3])
                    for h in range(H):
                        k.link(dve.scalar_tensor_tensor(out=ST[:, h, :], in0=ST[:, h, :], scalar=eg[:, h, P - 1:P],
                                                        in1=bank4(3)[:, h, :], op0=ALU.mult, op1=ALU.add))
                    release(3)
                    if c == NCH - 1:
                        dve.nop().then_inc(sig("prompt_state_done"), 1)

                def sample_heads(delta, eg):
                    t = small
                    seqs = bc(C[0:SW, C_SEQ:C_SEQ + NS].unsqueeze(2), [SW, NS, P])
                    for h in range(H):
                        st = S8[h % NSL]
                        val = t["v"][0:SW, h, :]
                        if delta:
                            k.next(sig("ut_copied"))
                            dve.nop().then_inc(free[1], 1)
                            k.next(full[1], 2)
                            k.link(dve.tensor_copy(US, B[0:SW, 1, 0:P]))
                            release(1)
                            val = US
                        k.settle()
                        k.link(dve.tensor_tensor(UM[0:SW, :, :], bc(val.unsqueeze(1), [SW, NS, P]), seqs, ALU.mult))
                        say("masked_values")
                        k.next(full[2])
                        k.link(dve.tensor_copy(sample(brt[:, h, :]), halves(B[:, 2, 0:SW])))
                        release(2)
                        dec = eg[:, h, :].rearrange("p (b t) -> p b t", b=NS)[:, :, LS - 1:LS]
                        k.next(sig(f"state_landed_{h % NSL}"), 16)
                        k.link(dve.tensor_tensor(st, st, bc(dec, [P, NS, P]), ALU.mult))
                        for half, bank in ((0, 0), (1, 3)):
                            k.next(full[bank])
                            k.settle()
                            part = st[:, 4 * half:4 * half + 4, :]
                            k.link(dve.tensor_tensor(part, B[:, bank, :].rearrange("p (b v) -> p b v", b=4), part, ALU.add))
                            release(bank)
                        say("sample_state_done")

                def gdn(c):
                    sm = c == NCH
                    w, t = (SW, small) if sm else (P, big)
                    q = SMP[:, 0:H, :] if sm else brt[:, 0:H, cols(c)]
                    incl = C[0:w, C_INCLS:C_INCLS + SW] if sm else C[:, C_INCL:C_INCL + P]
                    k.next(full[0])
                    k.link(dve.tensor_tensor(t["bgk"][0:w], bank4(0, P, w), by_token(CE[0:w, c, 8:12], w), ALU.mult))
                    k.link(dve.tensor_tensor(t["kend"][0:w], bank4(0, P, w), by_token(CE[0:w, c, 4:8], w), ALU.mult))
                    release(0)
                    k.next(full[1])
                    k.link(dve.tensor_tensor(t["v"][0:w], bank4(1, P, w), by_token(COL[0:w, c, 32:36], w), ALU.mult))
                    release(1)
                    k.next(sig("eg_ready"))
                    k.next(full[0])
                    k.link(dve.tensor_tensor(t["dt"][0:w], bank4(0, w, w, w), by_token(COL[0:w, c, 0:4], w, w), ALU.subtract))
                    release(0)
                    k.link(dve.tensor_scalar(t["dt"][0:w], t["dt"][0:w], 0.0, None, ALU.min))
                    say("decay_args")
                    k.link(dve.tensor_tensor(t["qg"], q, t["eg"], ALU.mult))
                    say("gated_q_ready")
                    k.next(sig("decay_ready"))
                    k.link(dve.tensor_tensor(t["dt"][0:w], t["dt"][0:w], bc(incl.unsqueeze(1), [w, H, w]), ALU.mult))
                    k.settle()
                    k.next(full[2])
                    k.link(dve.tensor_tensor(t["a"][0:w], bank4(2, w, w, w), t["dt"][0:w], ALU.mult))
                    release(2)
                    k.next(full[1])
                    k.link(dve.tensor_tensor(t["a"][0:w], bank4(1, w, w, w), t["a"][0:w], ALU.mult))
                    release(1)
                    k.next(full[3])
                    k.link(dve.tensor_tensor(t["sc"][0:w], bank4(3, w, w, w), t["dt"][0:w], ALU.mult))
                    release(3)
                    levels = S_LEVELS if sm else LEVELS
                    k.skip(full[0], levels)

                    def level(lv):
                        m = bc(mask[0:w, lv, 0:w].unsqueeze(1), [w, H, w])
                        k.link(dve.tensor_tensor(t["l0" if lv % 2 else "l1"][0:w], t["a"][0:w], m, ALU.mult))
                        say("level_ready")

                    level(1)
                    for lv in range(1, levels):
                        if lv + 1 < levels:
                            level(lv + 1)
                        for bank, name in ((1, "t"), (2, "u")):
                            if bank == 1 and lv == levels - 1:
                                continue
                            k.next(full[bank])
                            old = bc(ident[0:w, 0:w].unsqueeze(1), [w, H, w]) if lv == 1 else t[name][0:w]
                            k.link(dve.tensor_tensor(t[name][0:w], old, bank4(bank, w, w, w), ALU.subtract))
                            release(bank)
                    if sm:
                        sample_heads(True, t["eg"])
                    else:
                        k.skip(full[1])
                        finish_chunk(t["eg"], t, c)

                def ret(c):
                    sm = c == NCH
                    w, t = (SW, small) if sm else (P, big)
                    q = SMP[:, 0:H, :] if sm else brt[:, 0:H, cols(c)]
                    heads_of = lambda o, w: C[:, o:o + H * w].rearrange("p (h t) -> p h t", h=H)
                    dec = heads_of(C_DRETS if sm else C_DRET, w)
                    inner = heads_of(C_IRETS if sm else C_IRET, w)
                    ends = C[0:w, C_ENDS:C_ENDS + H] if sm else C[:, C_END:C_END + H]
                    k.next(full[0])
                    k.link(dve.tensor_tensor(t["kend"][0:w], bank4(0, P, w), by_token(ends, w), ALU.mult))
                    release(0)
                    k.next(full[1])
                    k.link(dve.tensor_copy(t["v"][0:w], bank4(1, P, w)))
                    release(1)
                    k.link(dve.tensor_tensor(t["qg"], q, inner, ALU.mult))
                    k.next(full[3])
                    k.link(dve.tensor_tensor(t["sc"][0:w], bank4(3, w, w, w), dec[0:w], ALU.mult))
                    release(3)
                    say("chunk_ready")
                    if sm:
                        sample_heads(False, inner)
                    else:
                        finish_chunk(inner, t, c)

                def hg(c):
                    sm = c == NCH
                    w, t = (SW, small) if sm else (P, hgb)
                    q, kk, acc = ((SMP[:, i:i + H, :] for i in (0, 4, 12)) if sm else
                                  (brt[:, i:i + H, cols(c)] for i in (0, 4, 16)))
                    levels = S_LEVELS if sm else LEVELS
                    blk = LS if sm else P
                    nb = w // blk
                    a4, d4 = (x.rearrange("p h (n t) -> p h n t", n=nb) for x in (acc, t["ked"]))
                    if nb == 1:
                        k.link(dve.tensor_tensor(t["ked"], bc(acc[:, :, P - 1:P], [P, H, P]), acc, ALU.subtract))
                    else:
                        k.link(dve.tensor_tensor(d4, bc(a4[:, :, :, blk - 1:blk], [P, H, nb, blk]), a4, ALU.subtract))
                    say("kend_args")
                    for lv in range(1, levels):
                        m = 1 << (lv - 1)
                        a5, x5 = (x.rearrange("p h (n u t) -> p h n u t", u=2, t=m) for x in (acc, t["xl"][:, lv - 1]))
                        mid = bc(a5[:, :, :, 0, m - 1:m], [P, H, w // (2 * m), m])
                        k.link(dve.tensor_tensor(x5[:, :, :, 0, :], mid, a5[:, :, :, 0, :], ALU.subtract))
                        k.link(dve.tensor_tensor(x5[:, :, :, 1, :], a5[:, :, :, 1, :], mid, ALU.subtract))
                    say("level_args")
                    k.next(sig("kend_exps"))
                    k.link(dve.tensor_tensor(t["ked"], t["ked"], kk, ALU.mult))
                    say("kend_ready")
                    k.link(dve.tensor_tensor(t["qg"], q, t["eg"], ALU.mult))
                    k.next(full[0])
                    k.link(dve.tensor_copy(t["kend"][0:w], bank4(0, P, w)))
                    release(0)
                    k.next(full[1])
                    k.link(dve.tensor_copy(t["v"][0:w], bank4(1, P, w)))
                    release(1)
                    k.next(sig("level_exps"))
                    for lv in range(1, levels):
                        m = 1 << (lv - 1)
                        q5, k5, x5 = (x.rearrange("p h (n u t) -> p h n u t", u=2, t=m) for x in (q, kk, t["xl"][:, lv - 1]))
                        k.link(dve.tensor_tensor(x5[:, :, :, 0, :], x5[:, :, :, 0, :], k5[:, :, :, 0, :], ALU.mult))
                        k.link(dve.tensor_tensor(x5[:, :, :, 1, :], x5[:, :, :, 1, :], q5[:, :, :, 1, :], ALU.mult))
                    say("levels_ready")
                    prod = t["prod"]
                    for h in range(H):
                        for b in range((levels + 3) // 4):
                            n = min(4, levels - 4 * b)
                            k.next(full[2 + b])
                            k.link(dve.tensor_tensor(
                                prod[0:w, 4 * b:4 * b + n, 0:w],
                                B[0:w, 2 + b, :].rearrange("p (l t) -> p l t", l=4)[:, 0:n, 0:w],
                                mask[0:w, 4 * b:4 * b + n, 0:w], ALU.mult))
                            release(2 + b)
                        k.link(dve.tensor_reduce(t["sc"][0:w, h, :], prod[0:w].rearrange("p l t -> p t l"), AX.X, ALU.add))
                        k.settle()
                    say("chunk_ready")
                    if sm:
                        sample_heads(False, t["eg"])
                    else:
                        finish_chunk(t["eg"], t, c)

                def out_norm(n):
                    k.settle()
                    for i in range(NSL):
                        dve.wait_ge(sig(f"stored_sample_{i}"), 16 * (n + 1) * len(range(i, H, NSL)))
                    if n == 1:
                        say("outputs_ready")
                        for i in range(H):
                            src, b = bank_pair(i)
                            o = halves(brt[:, i, :])
                            k.link(dve.scalar_tensor_tensor(out=o, in0=src, scalar=-1.0 / P, in1=o, op0=ALU.mult, op1=ALU.add))
                            release(b, b + 1)
                    say("outputs_final")
                    rows_of(RWO, False)
                    gain = {0: PR[:, P_GNORM:P_GNORM + 1], 1: 1.0, 2: PR[:, P_HNORM:P_HNORM + 1]}[n]
                    for i in range(H):
                        src, b = bank_pair(i)
                        k.settle()
                        k.link(dve.scalar_tensor_tensor(out=halves(VAL), in0=src, scalar=gain, in1=halves(brt[:, i, :]),
                                                        op0=ALU.mult, op1=ALU.mult))
                        release(b, b + 1)
                        k.link(dve.tensor_tensor(VAL, VAL, brt[:, 12 + i, :], ALU.mult))
                        k.settle()
                        k.link(dve.tensor_copy(OH[:, 0, i, :], VAL))
                        k.settle()
                        k.link(dve.tensor_tensor(OH[:, 1, i, :], VAL, OH[:, 0, i, :].bitcast(F32), ALU.subtract))
                    say("o_ready")

                def merge(n):
                    def body(s, g, j):
                        if j == 0:
                            k.next(sig("merge_gate"))
                            dve.nop().then_inc(buf_free[s % 2], 1)
                            return
                        wait_tile(s, g)
                        dst = MG[:, g, :] if n == 0 else VAL
                        k.link(dve.tensor_tensor(halves(dst), gp(s), halves(SG), ALU.mult))
                        k.settle()
                        dve.nop().then_inc(buf_free[s % 2], 1)
                        dve.nop().then_inc(sig("merge_slot_free"), 1)
                        if n:
                            k.link(dve.tensor_tensor(MG[:, g, :], MG[:, g, :], VAL, ALU.add))
                            k.settle()
                    pairs(f"merge{n}", 0, 16, body, {own["vector"]: 2 if n else 1, sig("merge_gate"): 1})

                def copy_tiles(name, first, count, dst):
                    def body(n, g, j):
                        wait_tile(n, g)
                        dve.tensor_copy(halves(brt[:, 2 * g + j + dst, :]), gp(n)).then_inc(buf_free[n % 2], 1)
                    pairs(name, first, count, body, {})

                def rope(n, g, j):
                    k.next(sig("swapped"))
                    out = brt[:, 2 * g + j, :]
                    dve.tensor_tensor(halves(out), gp(n), halves(C[:, C_COS:C_SIN]), ALU.mult).then_inc(buf_free[n % 2], 1)
                    k.link(dve.tensor_tensor(wide[j], wide[j], C[:, C_SIN:C_DRET], ALU.mult))
                    k.settle()
                    k.link(dve.tensor_tensor(out, out, wide[j], ALU.add))
                    say("rope_slot_free")

                def forget(n, g, j):
                    k.next(sig("sigmoids"))
                    dve.nop().then_inc(buf_free[n % 2], 1)
                    i = 2 * g + j
                    f, kk = brt[:, i + 16, :], brt[:, i + 4, :]
                    k.link(dve.scalar_tensor_tensor(out=f, in0=kk, scalar=LBC[:, 0, bass.ds(i, 1)], in1=f,
                                                    op0=ALU.mult, op1=ALU.add))
                    k.settle()
                    k.link(dve.tensor_scalar(kk, kk, LBC[:, 1, bass.ds(i, 1)], None, ALU.mult))

                start_branch(12)
                for c in range(NCH + 1):
                    gdn(c)
                out_norm(0)
                dve.nop().then_inc(sig("merge_slot_free"), 1)
                merge(0)

                for j in range(2):
                    dve.nop().then_inc(sig(f"ada_slot_{j}_free"), 1)
                dve.nop().then_inc(sig("rope_slot_free"), 2)
                pairs("ret", 0, 8, rope, {own["vector"]: 4, sig("swapped"): 2})
                copy_tiles("ret", 8, 4, 8)
                k.next(full[0])
                modulation(0, 2 * KD)
                k.next(sig("gates_in"))
                dve.wait_ge(sig("stored_prompt"), 16)
                start_branch(12)
                for c in range(NCH + 1):
                    ret(c)
                out_norm(1)
                merge(1)

                for j in range(2):
                    dve.nop().then_inc(sig(f"ada_slot_{j}_free"), 1)
                copy_tiles("hg", 0, 4, 0)
                pairs("hg", 4, 4, forget, {own["vector"]: 4, sig("sigmoids"): 2})
                f4 = BR[:, 16 * T:20 * T]
                k.settle()
                k.link(dve.tensor_scalar(LN1, f4, LN_CUT, None, ALU.max))
                k.link(dve.tensor_scalar(LN2, f4, F_TINY, LN_CUT, ALU.max, ALU.min))
                say("log_args")
                copy_tiles("hg", 8, 4, 8)
                k.next(sig("logs"))
                k.link(dve.tensor_tensor(LN1, LN1, LN2, ALU.add))
                k.settle()
                for h in range(H):
                    k.link(dve.tensor_tensor_scan(brt[:, 16 + h, :], reset, LN1[:, h * T:(h + 1) * T], 0.0,
                                                  ALU.mult, ALU.add))
                k.next(full[0])
                modulation(0, 4 * KD)
                k.next(sig("gates_in"))
                dve.wait_ge(sig("stored_prompt"), 32)
                start_branch(16)
                for c in range(NCH + 1):
                    hg(c)
                out_norm(2)
                merge(2)

                dve.wait_ge(tile_done, base["out"])
                for i in range(KD):
                    k.link(dve.tensor_copy(HH[:, 0, i, :], MG[:, i, :]))
                k.settle()
                for i in range(KD):
                    k.link(dve.tensor_tensor(HH[:, 1, i, :], MG[:, i, :], HH[:, 0, i, :].bitcast(F32), ALU.subtract))
                say("h_ready")
                add_gated("out", 2 * KD)
                say("x_ready")

                dve.wait_ge(tile_done, base["gu0"])
                norm_and_modulate(3 * KD, 4 * KD, P_NFFN)
                dve.nop().then_inc(sig("ffn_slot_free"), 1)
                for f in range(2):
                    def act_tile(s, g, j):
                        if j == 0:
                            k.next(sig("ffn_gate"))
                            dve.nop().then_inc(buf_free[s % 2], 1)
                            return
                        wait_tile(s, g)
                        k.link(dve.tensor_tensor(halves(FT[:, 1, :]), gp(s), halves(FT[:, 0, :]), ALU.mult))
                        k.settle()
                        dve.nop().then_inc(buf_free[s % 2], 1)
                        dve.nop().then_inc(sig("ffn_slot_free"), 1)
                        k.link(dve.tensor_copy(AH[:, 0, g, :], FT[:, 1, :]))
                        k.settle()
                        k.link(dve.tensor_tensor(AH[:, 1, g, :], FT[:, 1, :], AH[:, 0, g, :].bitcast(F32), ALU.subtract))
                        k.settle()
                    pairs(f"gu{f}", 0, 22, act_tile, {own["vector"]: 3, sig("ffn_gate"): 1})
                    say("act_ready")
                    add_gated(f"dn{f}", 5 * KD)

            @block.scalar
            def _(act):
                k = Counts(act, own["scalar"])

                def f(out, in_, func, **kw):
                    return act.activation(out, in_, func, **kw)

                def pairs(name, first, count, body, per):
                    n0 = base[name] + first
                    with act.Fori(0, count // 2) as g:
                        k.begin(g, per)
                        for j in range(2):
                            body(n0 + j, g, j)
                        k.end(count // 2)

                def wait_tile(n, g):
                    act.wait_ge(tile_done, n + 1 if g is None else n + 1 + 2 * g)

                def gp(n, p0=0, p1=P):
                    return GP[p0:p1, n % 2 * 2:n % 2 * 2 + 2, 0:HALF]

                def squares(tiles, sq, rows, out, scale):
                    for i, tile in enumerate(tiles):
                        k.next(sig("square_slot_free"))
                        f(sq[i % 2], tile, ACT.Square).then_inc(sig("square_ready"), 1)
                    k.peek(sig("square_slot_free"), 2)
                    f(halves(out[0:rows, :]), B[0:rows, 0:2, 0:HALF], ACT.Sqrt, scale=scale, bias=epsc[0:rows, :]
                      ).then_inc(sig("root_ready"), 1)

                act.wait_ge(sig("params_landed"), 16)
                f(neg_a, PR[0:H, P_ALOG:P_ALOG + 1], ACT.Exp).then_inc(sig("a_exp"), 1)
                squares([X[:, i, :] for i in range(KD)], sq_m, P, wide[0], 1.0 / D)

                act.nop().then_inc(sig("conv_slot_free"), 2)

                def conv(n, g, j):
                    i = n - 1 if g is None else 2 * g + (n - 1)
                    k.next(sig("conv_done"))
                    tile = brt[:, i, :]
                    k.link(f(prompt(tile), prompt(tile), ACT.Silu))
                    f(sample(tile), halves(CSMP[n % 2]), ACT.Silu).then_inc(sig("conv_slot_free"), 1)

                for n in (1, 2):
                    conv(n, None, n - 1)
                pairs("first", 3, 10, conv, {own["scalar"]: 2, sig("conv_done"): 2})

                def gate_tiles(name, first, func):
                    def body(n, g, j):
                        wait_tile(n, g)
                        k.link(f(halves(brt[:, 2 * g + j + 12, :]), gp(n), func))
                        k.settle()
                        act.nop().then_inc(buf_free[n % 2], 1)
                    pairs(name, first, 4, body, {own["scalar"]: 2})

                gate_tiles("first", 13, ACT.Silu)
                k.next(sig("conv_slot_free"), NCQ)
                squares([brt[:, i, :] for i in range(2 * H)], sq_m, 8, RW, 1.0)

                a2 = wide[2][0:H, :]
                k.next(sig("gate_args"))
                k.link(f(a2, a2, ACT.Exp))
                k.settle()
                k.link(f(a2, a2, ACT.Ln, bias=onec[0:H, :]))
                k.settle()
                f(wide[3][32:32 + H, :], ABROW[32:32 + H, :], ACT.Sigmoid).then_inc(sig("gate_logs"), 1)
                k.next(sig("gate_cols"))
                k.link(f(CE[:, :, 0:4], COL[:, :, 0:4], ACT.Exp))
                f(CE[:, :, 4:8], COL[:, :, 64:68], ACT.Exp).then_inc(sig("gate_exps"), 1)

                def bank4(b, w=P, parts=P, inner=P):
                    return B[0:parts, b, 0:H * w].rearrange("p (h t) -> p h t", h=H)[:, :, 0:inner]

                fills = {b: 0 for b in range(4)}

                def filled(b, n=1):
                    fills[b] += n
                    act.wait_ge(full[b], fills[b])

                def skip(b, n=1):
                    fills[b] += n

                for b in range(4):
                    skip(b, H)
                skip(0)
                skip(1)

                def gdn(c):
                    sm = c == NCH
                    w, t = (SW, small) if sm else (P, big)
                    skip(0)
                    filled(0)
                    f(t["eg"], bank4(0, w, P, w), ACT.Exp).then_inc(sig("eg_ready"), 1)
                    k.next(sig("decay_args"))
                    f(t["dt"][0:w], t["dt"][0:w], ACT.Exp).then_inc(sig("decay_ready"), 1)
                    skip(1, 2)
                    levels = S_LEVELS if sm else LEVELS
                    for lv in range(1, levels):
                        filled(0)
                        f(t["x"][0:w], bank4(0, w, w, w), ACT.Copy).then_inc(free[0], 1)
                    skip(1, levels - 2)
                    filled(0)
                    f(t["w"], bank4(0, w, P, w), ACT.Copy, scale=-1.0).then_inc(free[0], 1)
                    if sm:
                        for h in range(H):
                            filled(1)
                            f(t["ut"][:, 0, :], B[:, 1, 0:SW], ACT.Copy).then_inc(sig("ut_copied"), 1)
                            skip(1)
                            skip(0)
                    else:
                        filled(1)
                        f(t["uv"], bank4(1), ACT.Copy).then_inc(free[1], 1)

                for c in range(NCH + 1):
                    gdn(c)

                def out_norm():
                    k.next(sig("outputs_final"))
                    squares([brt[:, i, :] for i in range(H)], sq_o, 8, RWO, 1.0 / P)

                def merge(n):
                    def body(s, g, j):
                        if j == 0:
                            k.next(sig("merge_slot_free"))
                            wait_tile(s, g)
                            f(halves(SG), gp(s), ACT.Sigmoid).then_inc(sig("merge_gate"), 1)
                    pairs(f"merge{n}", 0, 16, body, {sig("merge_slot_free"): 1})

                out_norm()
                merge(0)

                def swap(n, g, j):
                    k.next(sig("rope_slot_free"))
                    wait_tile(n, g)
                    k.link(f(halves(wide[j][0:64, :]), gp(n, 64, P), ACT.Copy))
                    f(halves(wide[j][64:P, :]), gp(n, 0, 64), ACT.Copy).then_inc(sig("swapped"), 1)

                pairs("ret", 0, 8, swap, {own["scalar"]: 2, sig("rope_slot_free"): 2})
                gate_tiles("ret", 12, ACT.Silu)
                act.nop().then_inc(sig("gates_in"), 1)
                out_norm()
                merge(1)

                def forget(n, g, j):
                    wait_tile(n, g)
                    k.link(f(halves(brt[:, 2 * g + j + 16, :]), gp(n), ACT.Sigmoid))
                    f(halves(brt[:, 2 * g + j + 4, :]), gp(n), ACT.Sigmoid, scale=-1.0).then_inc(sig("sigmoids"), 1)

                pairs("hg", 4, 4, forget, {own["scalar"]: 2})
                k.next(sig("log_args"))
                k.link(f(LN1, LN1, ACT.Ln))
                f(LN2, LN2, ACT.Ln, scale=1.0 / LN_CUT).then_inc(sig("logs"), 1)
                gate_tiles("hg", 12, ACT.Sigmoid)
                act.nop().then_inc(sig("gates_in"), 1)
                for c in range(NCH + 1):
                    t = small if c == NCH else hgb
                    acc = SMP[:, 12:16, :] if c == NCH else brt[:, 16:20, cols(c)]
                    k.next(sig("kend_args"))
                    k.link(f(t["eg"], acc, ACT.Exp))
                    f(t["ked"], t["ked"], ACT.Exp).then_inc(sig("kend_exps"), 1)
                    k.next(sig("level_args"))
                    f(t["xl"], t["xl"], ACT.Exp).then_inc(sig("level_exps"), 1)
                out_norm()
                merge(2)

                k.next(sig("x_ready"))
                squares([X[:, i, :] for i in range(KD)], sq_m, P, wide[0], 1.0 / D)
                for half in range(2):
                    def gate(s, g, j):
                        if j == 0:
                            k.next(sig("ffn_slot_free"))
                            wait_tile(s, g)
                            f(halves(FT[:, 0, :]), gp(s), ACT.Silu).then_inc(sig("ffn_gate"), 1)
                    pairs(f"gu{half}", 0, 22, gate, {sig("ffn_slot_free"): 1})
        clear()

    with nc.Block() as block:
        @block.scalar
        def _(act):
            for i in range(KD):
                if i >= 2:
                    act.wait_ge(sig("square_slot_free"), i - 1)
                act.activation(sq_m[i % 2], X[:, i, :], ACT.Square).then_inc(sig("square_ready"), 1)
            act.wait_ge(sig("square_slot_free"), KD)
            act.activation(halves(wide[0]), B[:, 0:2, 0:HALF], ACT.Sqrt, scale=1.0 / D, bias=epsc
                           ).then_inc(sig("root_ready"), 1)

        @block.tensor
        def _(pe):
            for i in range(KD):
                pe.wait_ge(sig("square_ready"), i + 1)
                for h in range(2):
                    mm = pe.matmul(B[:, h, 0:HALF], ones, sq_m[i % 2][:, h * HALF:(h + 1) * HALF],
                                   start=i == 0, stop=i == KD - 1)
                mm.then_inc(sig("square_slot_free"), 1)

        @block.vector
        def _(dve):
            k = Counts(dve, own["vector"])
            dve.wait_ge(sig("root_ready"), 1)
            k.link(dve.reciprocal(wide[0], wide[0]))
            k.settle()
            for i in range(KD):
                dve.scalar_tensor_tensor(out=X[:, i, :], in0=X[:, i, :], scalar=FN[:, i:i + 1], in1=wide[0],
                                         op0=ALU.mult, op1=ALU.mult).then_inc(sig("y_ready"), 1)

        @block.sync
        def _(sp):
            for i in range(KD):
                sp.wait_ge(sig("y_ready"), i + 1)
                sp.dma_start(y_out[:, i, :], X[:, i, :]).then_inc(sig("stored_y"), 16)
            sp.wait_ge(sig("stored_y"), 16 * KD)

    ctx.close()


def _halves(prompt, sample):
    s = sample.reshape((SW,) + sample.shape[2:])
    return np.concatenate([prompt[:PH], s[:SH], prompt[PH:], s[SH:]])


def _tiles(w):
    L, K, N = w.shape
    return np.ascontiguousarray(w.reshape(L, K // P, P, N // P, P).transpose(0, 3, 2, 1, 4)).reshape(L, N // P, P, K)


def _cols(a):
    return np.swapaxes(a.reshape(a.shape[:-1] + (-1, P)), -1, -2)


def kernel(**inputs):
    import concourse.bacc as bacc
    from concourse.bass_utils import run_bass_kernel_spmd

    i = {n: np.asarray(a) for n, a in inputs.items()}
    f = np.float32
    arrays = {"consts": constants()}
    x = _halves(i["x_prompt"][0], i["x_sample"])
    arrays["x"] = np.ascontiguousarray(x.reshape(T, KD, P).transpose(2, 1, 0))
    cc = np.concatenate([i["c_prompt"], i["c_sample"]])
    arrays["c"] = np.ascontiguousarray(cc.reshape(1 + NS, KD, P).transpose(2, 1, 0))
    par = np.zeros((DEPTH, P, P_W), f)
    par[:, :, P_CONV:P_NMIX] = i["conv_w"].reshape(DEPTH, CONV_W, NCQ, P).transpose(0, 3, 2, 1).reshape(DEPTH, P, -1)
    par[:, :, P_NMIX:P_NFFN] = _cols(i["norm_mix"])
    par[:, :, P_NFFN:P_BADA] = _cols(i["norm_ffn"])
    par[:, :, P_BADA:P_GNORM] = _cols(i["b_ada"])
    par[:, :, P_GNORM] = i["gdn_norm"]
    par[:, :, P_HNORM] = i["hgrn_norm"]
    par[:, 0:H, P_ALOG] = i["gdn_a_log"]
    par[:, 0:H, P_DT] = i["gdn_dt_bias"]
    arrays["params"] = par
    arrays["fnorm"] = np.ascontiguousarray(_cols(i["final_norm"]))
    arrays["lb"] = np.ascontiguousarray(_cols(i["hgrn_lb"]).transpose(1, 0, 2))
    arrays["conv"] = np.ascontiguousarray(
        i["state_gdn_conv"].reshape(DEPTH, NS, 3, NCQ, P).transpose(0, 4, 3, 1, 2)).reshape(DEPTH, P, NCQ, NS * 3)
    w = i["w_in"]
    mk = H * P
    ab = np.zeros((DEPTH, D, P), f)
    ab[:, :, 0:H] = w[:, :, 4 * mk:4 * mk + H]
    ab[:, :, 32:32 + H] = w[:, :, 4 * mk + H:4 * mk + 2 * H]
    o = 4 * mk + 2 * H
    arrays["w_first"] = _tiles(np.concatenate([ab, w[:, :, :4 * mk]], 2))
    arrays["w_ret"] = _tiles(w[:, :, o:o + 4 * mk])
    arrays["w_hg"] = _tiles(w[:, :, o + 4 * mk:o + 8 * mk])
    arrays["w_mrg"] = _tiles(w[:, :, o + 8 * mk:]).reshape(DEPTH, 3, KD, P, D)
    arrays["w_brn"] = _tiles(i["w_branch"].reshape(DEPTH * 3, mk, D)).reshape(DEPTH, 3, KD, P, mk)
    arrays["w_out"] = _tiles(i["w_out"])
    gu = _tiles(i["w_gate_up"]).reshape(DEPTH, 2, 2, KF, P, D)
    arrays["w_gu"] = np.ascontiguousarray(gu.transpose(0, 2, 3, 1, 4, 5)).reshape(DEPTH, 2, 2 * KF, P, D)
    dn = _tiles(i["w_down"]).reshape(DEPTH, KD, P, 2, KF * P)
    arrays["w_dn"] = np.ascontiguousarray(dn.transpose(0, 3, 1, 2, 4))
    arrays["w_ada"] = _tiles(i["w_ada"])
    for n, s in (("s_gdn", "state_gdn"), ("s_ret", "state_ret"), ("s_hg", "state_hgrn")):
        arrays[n] = np.ascontiguousarray(i[s])

    outs = {"y": (P, KD, T), "gdn_p": (DEPTH, H, P, P), "conv_new_": (DEPTH, P, NCQ, 3 + NS * 3), "ret_p": (DEPTH, H, P, P),
            "hg_p": (DEPTH, H, P, P), "gdn_s": (DEPTH, NS, H, P, P), "ret_s": (DEPTH, NS, H, P, P),
            "hg_s": (DEPTH, NS, H, P, P)}
    nc = bacc.Bacc("TRN2", target_bir_lowering=False, num_devices=1)
    args = [nc.dram_tensor(f"in_{n}", a.shape, F32, kind="ExternalInput").ap() for n, a in arrays.items()]
    args += [nc.dram_tensor(f"out_{n}", s, F32, kind="ExternalOutput").ap() for n, s in outs.items()]
    trunk(nc, *args)
    r = run_bass_kernel_spmd(nc, [{f"in_{n}": a for n, a in arrays.items()}], core_ids=[0])
    got = {n: np.asarray(r.results[0][f"out_{n}"]) for n in outs}
    y = got["y"].transpose(2, 1, 0).reshape(2, HALF, D)
    y_prompt = np.ascontiguousarray(y[:, :PH]).reshape(1, SEQ, D)
    y_sample = np.ascontiguousarray(y[:, PH:]).reshape(NS, LS, D)
    cv = got["conv_new_"].transpose(0, 3, 2, 1).reshape(DEPTH, 3 + NS * 3, NCQ * P)
    conv_p = np.ascontiguousarray(cv[:, :3]).reshape(DEPTH, 1, 3, NCQ * P)
    conv_s = np.ascontiguousarray(cv[:, 3:]).reshape(DEPTH, NS, 3, NCQ * P)
    one = {n: got[n].reshape(DEPTH, 1, H, P, P) for n in ("gdn_p", "ret_p", "hg_p")}
    return (y_prompt, y_sample, one["gdn_p"], conv_p, one["ret_p"], one["hg_p"],
            got["gdn_s"], conv_s, got["ret_s"], got["hg_s"])
```

```python
from contextlib import ExitStack

import numpy as np

import concourse.bass as bass
from concourse import mybir

F32 = mybir.dt.float32
F32R = mybir.dt.float32r
ALU = mybir.AluOpType
ACT = mybir.ActivationFunctionType
AX = mybir.AxisListType

P = 128
D = 1024
DEPTH = 2
SEQ = 512
NS, LS = 8, 4
H = 4
DFF = 2816
CONV_W = 4
PAST = 4096
EPS = 1e-6
F_TINY = 1e-30
LN_CUT = 2.0 ** -50
KD = D // P
HALF, PH, SH = 272, 256, 16
T = 2 * HALF
NCH = SEQ // P
SW = NS * LS
LEVELS = 8
S_LEVELS = 3
KF = 11
SLAB = KF * P
NCQ = 12

P_CONV = 0
P_NMIX = P_CONV + NCQ * CONV_W
P_NFFN = P_NMIX + KD
P_BADA = P_NFFN + KD
P_GNORM = P_BADA + 6 * KD
P_HNORM = P_GNORM + 1
P_ALOG = P_HNORM + 1
P_DT = P_ALOG + 1
P_W = P_DT + 1

C_ID = 0
C_MASK = C_ID + P
C_COS = C_MASK + LEVELS * P
C_SIN = C_COS + T
C_DRET = C_SIN + T
C_IRET = C_DRET + H * P
C_DRETS = C_IRET + H * P
C_IRETS = C_DRETS + H * SW
C_END = C_IRETS + H * SW
C_ENDS = C_END + H
C_RESET = C_ENDS + H
C_INCL = C_RESET + T
C_INCLS = C_INCL + P
C_SEQ = C_INCLS + SW
C_HOT = C_SEQ + NS
C_SEL = C_HOT + 64
C_ONE = C_SEL + 8 * P
C_W = C_ONE + P


def constants():
    f = np.float32
    c = np.zeros((P, C_W), f)
    c[:, C_ID:C_ID + P] = np.eye(P)
    s, t = np.arange(P)[:, None], np.arange(P)[None, :]
    masks = [s == t] + [(s // (2 * m) == t // (2 * m)) & (s // m % 2 == 0) & (t // m % 2 == 1)
                        for m in (1 << i for i in range(LEVELS - 1))]
    c[:, C_MASK:C_COS] = np.stack(masks, 1).reshape(P, -1)
    pos = np.concatenate([np.concatenate([np.arange(h * PH, (h + 1) * PH), PAST + np.tile(np.arange(LS), NS // 2)])
                          for h in range(2)]).astype(f)
    half = P // 2
    inv = (10000.0 ** (-np.arange(half) / half)).astype(f)
    ang = (inv[:, None] * pos[None, :]).astype(f)
    c[:, C_COS:C_SIN] = np.tile(np.cos(ang), (2, 1))
    c[:, C_SIN:C_DRET] = np.concatenate([-np.sin(ang), np.sin(ang)])
    lg = np.log1p(-np.exp2(-5.0 - np.arange(H)))
    scale = P ** -0.5
    for h in range(H):
        decay = np.where(s <= t, np.exp(lg[h] * (t - s)), 0.0) * scale
        c[:, C_DRET + h * P:C_DRET + (h + 1) * P] = decay
        c[:SW, C_DRETS + h * SW:C_DRETS + (h + 1) * SW] = (decay * (s // LS == t // LS))[:SW, :SW]
        c[:, C_IRET + h * P:C_IRET + (h + 1) * P] = np.exp(lg[h] * (t + 1))
        c[:, C_IRETS + h * SW:C_IRETS + (h + 1) * SW] = np.exp(lg[h] * (t[:, :SW] % LS + 1))
        c[:, C_END + h] = np.exp(lg[h] * (P - 1 - s[:, 0])) * scale
        c[:, C_ENDS + h] = np.exp(lg[h] * (LS - 1 - s[:, 0] % LS)) * scale
    reset = np.ones(T)
    for h in range(2):
        reset[[h * HALF, h * HALF + P]] = 0
        reset[h * HALF + PH:(h + 1) * HALF:LS] = 0
    c[:, C_RESET:C_INCL] = reset
    c[:, C_INCL:C_INCLS] = s <= t
    c[:SW, C_INCLS:C_SEQ] = ((s <= t) & (s // LS == t // LS))[:SW, :SW]
    c[:, C_SEQ:C_HOT] = s // LS == np.arange(NS)
    for i in range(8):
        c[:, C_HOT + 8 * i + i] = 1
        c[i, C_SEL + i * P:C_SEL + (i + 1) * P] = 1
        c[32 + i, C_SEL + i * P:C_SEL + (i + 1) * P] = 1
    c[:, C_ONE:C_W] = 1
    return c


class Counts:

    def __init__(self, eng, own):
        self.eng, self.own, self.n = eng, own, {}
        self.reg, self.per, self.before = None, {}, {}

    def value(self, sem, n):
        return n if self.reg is None else n + self.reg * self.per[sem]

    def next(self, sem, n=1):
        self.n[sem] = self.n.get(sem, 0) + n
        self.eng.wait_ge(sem, self.value(sem, self.n[sem]))

    def peek(self, sem, ahead=1):
        self.eng.wait_ge(sem, self.value(sem, self.n.get(sem, 0) + ahead))

    def skip(self, sem, n=1):
        self.n[sem] = self.n.get(sem, 0) + n

    def link(self, ins):
        self.n[self.own] = self.n.get(self.own, 0) + 1
        ins.then_inc(self.own, 1)

    def settle(self):
        self.eng.wait_ge(self.own, self.value(self.own, self.n[self.own]))

    def begin(self, reg, per):
        self.reg, self.per, self.before = reg, per, dict(self.n)

    def end(self, passes):
        for sem, k in self.per.items():
            got = self.n.get(sem, 0) - self.before.get(sem, 0)
            assert got == k, (sem, got, k)
            self.n[sem] += k * (passes - 1)
        assert all(self.n[s] == self.before.get(s, 0) for s in self.n if s not in self.per)
        self.reg, self.per = None, {}


def trunk(nc, consts_in, x_in, c_in, params_in, fnorm_in, lb_in, conv_in, w_first, w_ret, w_hg, w_merge, w_out,
          w_gu, w_dn, w_ada, s_gdn, s_ret, s_hg, y_out, gdn_p, conv_out, ret_p, hg_p, gdn_s, ret_s, hg_s):
    ctx = ExitStack()

    def sb(name, shape, dt=F32):
        return ctx.enter_context(nc.sbuf_tensor(name, shape, dt))

    sems = {}

    def sig(name):
        if name not in sems:
            sems[name] = ctx.enter_context(nc.semaphore(name))
        return sems[name]

    X = sb("x", [P, KD, T])
    HH = sb("h_hi_lo", [P, 2, KD, T], F32R)
    raw = sb("w_raw", [P, 2, SLAB])
    whl = sb("w_hi_lo", [P, 2, 2, SLAB], F32R)
    C = sb("consts", [P, C_W])
    PR = sb("params", [P, P_W])
    MOD = sb("mod", [P, 6 * KD, 1 + NS])
    LB = sb("lb", [P, DEPTH, H])
    LBC = sb("lb_layer", [P, 2, H])
    CS = sb("silu_c", [P, KD, 1 + NS])
    CONV0 = sb("conv_state", [P, NCQ, NS * 3])
    CONV1 = sb("conv_new", [P, NCQ, 3 + NS * 3])
    ST = sb("state", [P, H, P])
    FN = sb("final_norm", [P, KD])
    MISC = sb("misc", [P, 64])
    GTB = sb("gate_sample", [P, KD, NS])
    GTP = sb("gate_prompt", [P, KD])
    SCT = sb("gated_sample", [P, SW])
    SCG = sb("scale_gain", [P, KD, 1 + NS])
    SMP = sb("sample_cols", [P, 16, SW])
    CSM = sb("conv_sample", [P, SW])

    M1W = 7680
    XPW = 3 + SEQ + NS * (3 + LS)
    BRW = 20 * T
    with ExitStack() as mix:
        M1 = mix.enter_context(nc.sbuf_tensor("mix_temps", [P, M1W], F32))
        BR = mix.enter_context(nc.sbuf_tensor("branch", [P, BRW], F32))
        MG = mix.enter_context(nc.sbuf_tensor("merged", [P, KD, T], F32))
    X_flat = X[:, :, :].rearrange("p k t -> p (k t)")
    MG_flat = MG[:, :, :].rearrange("p k t -> p (k t)")
    with ExitStack() as mix:
        OH = mix.enter_context(nc.sbuf_tensor("o_hi_lo", [P, 2, H, T], F32R))
        OT = mix.enter_context(nc.sbuf_tensor("o_temps", [P, M1W - 2 * H * T], F32))
    with ExitStack() as ffn:
        AH = ffn.enter_context(nc.sbuf_tensor("ffn_hi_lo", [P, 2, KF, T], F32R))
        FT = ffn.enter_context(nc.sbuf_tensor("ffn_temps", [P, 4, T], F32))
    GP = ctx.enter_context(nc.psum_tensor("gemm_psum", [P, 4, 512], F32))
    B = ctx.enter_context(nc.psum_tensor("mix_psum", [P, 4, 512], F32))

    brt = BR[:, :].rearrange("p (i t) -> p i t", t=T)

    def halves(ap):
        return ap.rearrange("p (a b) -> p a b", a=2)

    def prompt(ap):
        return halves(ap)[:, :, 0:PH]

    def sample(ap):
        return halves(ap)[:, :, PH:HALF]

    def by_seq(ap):
        return ap.rearrange("p a (b t) -> p a b t", t=LS)

    def cols(c):
        o = c // 2 * HALF + c % 2 * P
        return slice(o, o + P)

    ident = C[:, C_ID:C_ID + P]
    mask = C[:, C_MASK:C_COS].rearrange("p (l t) -> p l t", l=LEVELS)
    hot = C[:, C_HOT:C_SEL].rearrange("p (i j) -> p i j", i=8)
    sel = C[:, C_SEL:C_ONE].rearrange("p (i j) -> p i j", i=8)
    ones = C[:, C_ONE:C_W]
    seqs = C[0:SW, C_SEQ:C_SEQ + NS].unsqueeze(2).broadcast_to([SW, NS, P])
    reset = C[:, C_RESET:C_INCL]
    neg_a = MISC[0:H, 1:2]
    epsc = MISC[:, 2:3]
    onec = MISC[:, 3:4]
    EGE = MISC[:, 16:16 + 2 * H].rearrange("p (c h) -> p c h", c=2)

    def heads(o, w):
        return M1[:, o:o + H * w].rearrange("p (h t) -> p h t", h=H)

    BLK = H * P
    order = ("bgk", "kend", "v", "qg", "sc", "a", "t", "u", "x", "l0", "l1")
    flat = [(M1[:, :], i * BLK) for i in range(15)] + [(MG_flat, i * BLK) for i in range(7)]
    sets = []
    for p in range(2):
        where = flat[p * len(order):(p + 1) * len(order)]
        t = {n: m[:, a:a + BLK].rearrange("p (h t) -> p h t", h=H) for n, (m, a) in zip(order, where)}
        t.update(eg=t["qg"], dt=t["x"], w=t["l1"], uv=t["x"])
        sets.append(t)
    big = sets[0]
    hgb = {n: heads((9 + i) * BLK, P) for i, n in enumerate(("qg", "ked", "eg", "kend", "v", "sc"))}
    hgb["xl"] = M1[:, 0:7 * BLK].rearrange("p (l h t) -> p l h t", l=LEVELS - 1, h=H)
    hgb["prod"] = M1[:, 7 * BLK:9 * BLK].rearrange("p (l t) -> p l t", l=LEVELS)
    NAR = H * SW
    names = ("eg", "dt", "sc", "a", "l0", "l1", "t", "u", "x", "w", "qg", "ut", "ked")
    small = {n: heads(i * NAR, SW) for i, n in enumerate(names)}
    small["xl"] = M1[:, 3 * NAR:5 * NAR].rearrange("p (l h t) -> p l h t", l=S_LEVELS - 1, h=H)
    small["prod"] = M1[:, 6 * NAR:6 * NAR + S_LEVELS * SW].rearrange("p (l t) -> p l t", l=S_LEVELS)
    o = len(names) * NAR
    for i, n in enumerate(("bgk", "kend", "v")):
        small[n] = heads(o + i * BLK, P)
    o += 3 * BLK
    UM = M1[:, o:o + H * NS * P].rearrange("p (h b v) -> p h b v", h=H, b=NS)
    US = small["bgk"][0:SW]
    S8 = X_flat[:, 0:H * NS * P].rearrange("p (h b v) -> p h b v", h=H, b=NS)
    sq_m = [M1[:, i * T:(i + 1) * T] for i in range(2)]
    wide = [M1[:, i * T:(i + 1) * T] for i in range(2, 8)]
    sq_o = [OT[:, i * T:(i + 1) * T] for i in range(2)]
    RWO, VAL, SG = (OT[:, i * T:(i + 1) * T] for i in (2, 3, 4))
    RW = wide[0]
    RSTD = wide[0]
    TN = M1[:, 3 * T:11 * T].rearrange("p (i t) -> p i t", i=KD)
    YP = [M1[:, i * T:(i + 1) * T] for i in (11, 12)]
    YS = M1[:, 13 * T:13 * T + KD * SW].rearrange("p (a i t) -> p a i t", a=2, i=KD)
    SQ8 = M1[:, 6 * T:14 * T].rearrange("p (i t) -> p i t", i=8)
    LN1, LN2 = (M1[:, i * H * T:(i + 1) * H * T] for i in range(2))

    o = 16 * T
    XP = [BR[:, o + i * XPW:o + (i + 1) * XPW] for i in range(2)]
    ROW = BR[:, o:o + T]
    ROWS = BR[:, o + T:o + T + SW]
    o += T + SW
    COL = BR[:, o:o + 5 * 96].rearrange("p (c j) -> p c j", c=5)
    o += 5 * 96
    CE = BR[:, o:o + 5 * 12].rearrange("p (c j) -> p c j", c=5)
    CSMP = [MISC[:, 32:64], CSM[:, :]]
    ABROW = MG[0:64, 0, :]
    ADG = 4
    ada_group = [x[:, o:o + ADG * D].rearrange("p (n k) -> p n k", n=ADG) for x, o in ((BR, 0), (BR, ADG * D), (MG_flat, 0))]
    ada_slot = [M1[:, M1W - (i + 1) * D:M1W - i * D] for i in range(2)]

    CHUNKS = [(c, c + 1) for c in range(0, NCH, 2)] + [(NCH,)]

    stream = [("first", 17, 8)]
    for n in range(3):
        if n:
            stream.append(("ret" if n == 1 else "hg", 16, 8))
        stream.append((f"merge{n}", 16, 6))
    stream += [("out", 8, 8)]
    for f in range(2):
        stream += [(f"gu{f}", 22, 8), (f"dn{f}", 8, KF)]
    ADA_FIRST = {"ret": 2 * KD, "hg": 4 * KD}
    base, at = {}, 0
    for name, count, _ in stream:
        base[name] = at
        at += count

    def source(name, l, i, odd):
        if name == "first":
            return w_first[l, i]
        if name.startswith("merge"):
            return w_merge[l, int(name[-1]), i, int(odd)]
        if name in ("ret", "hg"):
            return {"ret": w_ret, "hg": w_hg}[name][l, i]
        if name == "out":
            return w_out[l, i]
        return {"gu": w_gu, "dn": w_dn}[name[:2]][l, int(name[-1]), i]

    landed = [sig("slab_landed_0"), sig("slab_landed_1")]
    hi_done, split_done, tile_done = sig("weights_hi"), sig("weights_split"), sig("gemm_tile_done")
    buf_free = [sig("gemm_buffer_0_free"), sig("gemm_buffer_1_free")]
    full = [sig(f"bank_{i}_full") for i in range(8)]
    free = [sig(f"bank_{i}_free") for i in range(8)]

    def psum(b):
        return (B if b < 4 else GP)[:, b % 4, :]

    def banks_of(c):
        return 4 * (c % 2) if c < NCH else 0

    own = {e: sig(f"{e}_steps") for e in ("vector", "scalar", "gpsimd", "tensor")}

    def slab_pairs(eng, name, first, count, body, k=None, per=None):
        step = name.startswith("merge")
        with eng.Fori(0, count // 2) as g:
            if k:
                k.begin(g, per)
            for j in range(2):
                body(base[name] + first + j, g if step else 2 * g + first + j, g)
            if k:
                k.end(count // 2)

    def each_slab(eng, name, body, k=None, per=None):
        _, count, _ = next(s for s in stream if s[0] == name)
        first = 3 if count % 2 else 0
        for n in range(first):
            body(base[name] + n, n, None)
        slab_pairs(eng, name, first, count - first, body, k, per)

    with nc.Block() as block:
        @block.sync
        def _(sp):
            sp.dma_start(C[:, :], consts_in[:, :]).then_inc(sig("consts_landed"), 16)
            sp.dma_start(X[:, :, :], x_in[:, :, :]).then_inc(sig("x_landed"), 16)
            sp.dma_start(CS[:, :, :], c_in[:, :, :]).then_inc(sig("c_landed"), 16)
            sp.dma_start(LB[:, :, :], lb_in[:, :, :]).then_inc(sig("lb_landed"), 16)
            sp.dma_start(FN[:, :], fnorm_in[:, :]).then_inc(sig("fnorm_landed"), 16)
            for s in ("consts_landed", "x_landed", "fnorm_landed"):
                sp.wait_ge(sig(s), 16)

        @block.scalar
        def _(act):
            act.wait_ge(sig("c_landed"), 16)
            act.activation(CS[:, :, :], CS[:, :, :], ACT.Silu)
            act.wait_ge(sig("lb_shifted"), 1)
            act.activation(LB[:, :, :], LB[:, :, :], ACT.Exp).then_inc(sig("lb_exp"), 1)

        @block.vector
        def _(dve):
            k = Counts(dve, own["vector"])
            k.link(dve.memset(MISC[:, :], 0.0))
            k.settle()
            k.link(dve.memset(epsc, EPS))
            k.link(dve.memset(onec, 1.0))
            dve.wait_ge(sig("lb_landed"), 16)
            top, tot = MISC[:, 8:8 + H], MISC[:, 12:12 + H]
            k.settle()
            k.link(dve.tensor_copy(top, LB[:, 0, :]))
            for l in range(1, DEPTH):
                k.settle()
                k.link(dve.tensor_tensor(top, top, LB[:, l, :], ALU.max))
            k.settle()
            dve.tensor_tensor(LB[:, :, :], LB[:, :, :], top.unsqueeze(1).broadcast_to([P, DEPTH, H]),
                              ALU.subtract).then_inc(sig("lb_shifted"), 1)
            dve.wait_ge(sig("lb_exp"), 1)
            k.link(dve.tensor_copy(tot, LB[:, 0, :]))
            for l in range(1, DEPTH):
                k.settle()
                k.link(dve.tensor_tensor(tot, tot, LB[:, l, :], ALU.add))
            k.settle()
            k.link(dve.reciprocal(tot, tot))
            k.settle()
            k.link(dve.tensor_tensor(LB[:, :, :], LB[:, :, :], tot.unsqueeze(1).broadcast_to([P, DEPTH, H]), ALU.mult))
            k.settle()
            k.link(dve.tensor_copy(top, LB[:, 0, :]))
            for l in range(1, DEPTH):
                k.settle()
                k.link(dve.tensor_tensor(LB[:, l, :], LB[:, l, :], LB[:, l - 1, :], ALU.add))
            k.settle()
            k.link(dve.tensor_tensor(LB[:, :, :], LB[:, :, :], top.unsqueeze(1).broadcast_to([P, DEPTH, H]),
                                     ALU.subtract))
            k.settle()

    def clear():
        for s in sems.values():
            nc.sync.sem_clear(s)
        nc.all_engine_barrier()

    clear()

    with nc.Fori(0, DEPTH) as l:
        with nc.Block() as block:
            @block.sync
            def _(sp):
                k = Counts(sp, None)
                sp.dma_start(PR[:, :], params_in[l]).then_inc(sig("params_landed"), 16)
                sp.dma_start(CONV0[:, :, :], conv_in[l]).then_inc(sig("conv_landed"), 16)
                for i in range(2 * KD // ADG):
                    if i >= 3:
                        sp.wait_ge(sig("ada_group_used"), i - 2)
                    sp.dma_start(ada_group[i % 3], w_ada[l, i * ADG:(i + 1) * ADG].rearrange("n p k -> p n k")
                                 ).then_inc(sig(f"ada_group_landed_{i}"), 16)


                def load_states(n):
                    if n == 0:
                        sp.wait_ge(sig("stored_x"), 16)
                        sp.wait_ge(sig("modulation_ready"), 1)
                    else:
                        sp.wait_ge(sig("stored_sample"), 16 * H * n)
                    for h in range(H):
                        sp.dma_start(S8[:, h], (s_gdn, s_ret, s_hg)[n][l, :, h].rearrange("b k v -> k b v")
                                     ).then_inc(sig("states_landed"), 16)

                def store_states(n):
                    s_out, p_out = ((gdn_s, gdn_p), (ret_s, ret_p), (hg_s, hg_p))[n]
                    k.next(sig("prompt_state_done"))
                    sp.dma_start(p_out[l].rearrange("h k v -> k h v"), ST[:, :, :]).then_inc(sig("stored_prompt"), 16)
                    for h in range(H):
                        k.next(sig("sample_state_done"))
                        sp.dma_start(s_out[l, :, h].rearrange("b k v -> k b v"), S8[:, h]
                                     ).then_inc(sig("stored_sample"), 16)

                sp.dma_start(y_out[:, :, :], X[:, :, :]).then_inc(sig("stored_x"), 16)
                for seg in stream:
                    def load_slab(n, i, g):
                        odd = (n - base[seg[0]]) % 2 == 1
                        words = seg[2] * P
                        if n >= 2:
                            sp.wait_ge(split_done, n - 1 if g is None else n - 1 + 2 * g)
                        sp.dma_start(raw[:, n % 2, 0:words], source(seg[0], l, i, odd)).then_inc(landed[n % 2], 16)
                        if seg[0] in ADA_FIRST:
                            j = (n - base[seg[0]]) % 2
                            k.next(sig(f"ada_slot_{j}_free"))
                            sp.dma_start(ada_slot[j], w_ada[l, i + ADA_FIRST[seg[0]]]).then_inc(sig(f"ada_landed_{j}"), 16)

                    if seg[0] in ADA_FIRST:
                        each_slab(sp, seg[0], load_slab, k, {sig("ada_slot_0_free"): 1, sig("ada_slot_1_free"): 1})
                        for j in range(2):
                            k.skip(sig(f"ada_slot_{j}_free"))
                    else:
                        each_slab(sp, seg[0], load_slab)
                    if seg[0] in ("first", "ret", "hg"):
                        n = ("first", "ret", "hg").index(seg[0])
                        load_states(n)
                        store_states(n)
                    if seg[0] == "hg":
                        sp.wait_ge(sig("stored_sample"), 16 * H * 3)
                        sp.dma_start(X[:, :, :], y_out[:, :, :]).then_inc(sig("x_back"), 16)
                sp.wait_ge(sig("conv_saved"), 1)
                sp.dma_start(conv_out[l], CONV1[:, :, :]).then_inc(sig("stored_conv"), 16)
                sp.wait_ge(sig("stored_conv"), 16)
                sp.wait_ge(sig("stored_prompt"), 16 * 3)

            @block.gpsimd
            def _(pool):
                for seg in stream:
                    def split(n, i, g):
                        words = seg[2] * P

                        def at(v, per):
                            return v if g is None else v + per * g
                        if n >= 2:
                            pool.wait_ge(tile_done, at(n - 1, 2))
                        pool.wait_ge(landed[n % 2], at(16 * (n // 2 + 1), 16))
                        src, hi, lo = raw[:, n % 2, 0:words], whl[:, n % 2, 0, 0:words], whl[:, n % 2, 1, 0:words]
                        pool.tensor_tensor(hi, src, ones[:, 0:1].broadcast_to([P, words]), ALU.mult).then_inc(hi_done, 1)
                        pool.wait_ge(hi_done, at(n + 1, 2))
                        pool.tensor_tensor(lo, src, hi.bitcast(F32), ALU.subtract).then_inc(split_done, 1)

                    each_slab(pool, seg[0], split)
                    if seg[0] in ("first", "ret", "hg"):
                        n = ("first", "ret", "hg").index(seg[0])
                        pool.wait_ge(sig("values_ready"), n + 1)
                        val = US if n == 0 else small["v"][0:SW]
                        for h in range(H // 2, H):
                            pool.tensor_tensor(UM[0:SW, h], val[:, h].unsqueeze(1).broadcast_to([SW, NS, P]), seqs,
                                               ALU.mult).then_inc(sig("masked_values_pool"), 1)

            @block.tensor
            def _(pe):
                k = Counts(pe, own["tensor"])
                pe.nop().then_inc(sig("square_slot_free"), 2)

                def acquire(b):
                    k.next(free[b])

                def ada(weights, out):
                    w = weights.rearrange("p (k m) -> p k m", k=KD)
                    for kk in range(KD):
                        mm = pe.matmul(out, w[:, kk, :], CS[:, kk, :], start=kk == 0, stop=kk == KD - 1)
                    return mm


                def products(slot, buf, ks, rhs, first=True, last=True, fresh=False):
                    for kw, kr in ks:
                        if fresh:
                            k.next(sig("h_ready"))
                        for p, (a, b) in enumerate(((0, 0), (0, 1), (1, 0))):
                            for h in range(2):
                                mm = pe.matmul(GP[:, 2 * buf + h, 0:HALF], whl[:, slot, a, kw * P:(kw + 1) * P],
                                               rhs[:, b, kr, h * HALF:(h + 1) * HALF],
                                               start=first and (kw, kr) == ks[0] and p == 0,
                                               stop=last and (kw, kr) == ks[-1] and p == 2)
                    return mm

                def weights(n, g):
                    pe.wait_ge(split_done, n + 1 if g is None else n + 1 + 2 * g)

                def buffer(n, g):
                    if n >= 2:
                        pe.wait_ge(buf_free[n % 2], n // 2 if g is None else n // 2 + g)

                def gemm(n, g, kt, rhs, fresh=False):
                    weights(n, g)
                    buffer(n, g)
                    products(n % 2, n % 2, [(i, i) for i in range(kt)], rhs, fresh=fresh).then_inc(tile_done, 1)

                def segment(name, rhs, kt, fresh=False):
                    _, count, _ = next(s for s in stream if s[0] == name)
                    first = 2 if fresh else 0
                    for j in range(first):
                        gemm(base[name] + j, None, kt, rhs, j == 0)
                    slab_pairs(pe, name, first, count - first, lambda n, i, g: gemm(n, g, kt, rhs))

                def segment_with_ada(name):
                    def tile(n, i, g):
                        j = (n - base[name]) % 2
                        k.next(sig(f"ada_landed_{j}"), 16)
                        ada(ada_slot[j], B[:, 0, bass.ds(i * (1 + NS), 1 + NS)]).then_inc(sig(f"ada_slot_{j}_free"), 1)
                        gemm(n, g, KD, HH)
                    acquire(0)
                    each_slab(pe, name, tile, k, {sig("ada_landed_0"): 16, sig("ada_landed_1"): 16})
                    pe.wait_ge(sig("ada_slot_1_free"), KD + 1 if name == "ret" else 2 * (KD + 1))
                    pe.nop().then_inc(full[0], 1)

                def merge_segment(name):
                    def tile(n, i, g):
                        weights(n, g)
                        if (n - base[name]) % 2 == 0:
                            buffer(n, g)
                            products(n % 2, n % 2, [(i, i) for i in range(6)], HH, last=False).then_inc(tile_done, 1)
                            return
                        products(n % 2, (n - 1) % 2, [(0, 6), (1, 7)], HH, first=False).then_inc(sig("gate_product"), 1)
                        buffer(n, g)
                        products(n % 2, n % 2, [(2 + i, i) for i in range(4)], OH).then_inc(tile_done, 1)
                    each_slab(pe, name, tile)

                def feature_sums(count, lhs, rows, sq):
                    acquire(0)
                    acquire(1)
                    for i in range(count):
                        k.next(sig("square_ready"))
                        for h in range(2):
                            mm = pe.matmul(B[0:rows, h, 0:HALF], lhs(i), sq[i % 2][:, h * HALF:(h + 1) * HALF],
                                           start=i == 0, stop=i == count - 1)
                        mm.then_inc(sig("square_slot_free"), 1)

                def spread(rows, count):
                    k.next(sig("rows_ready"))
                    for i in range(count):
                        for h in range(2):
                            b = 2 * (i % 2) + h
                            acquire(b)
                            pe.matmul(B[:, b, 0:HALF], sel[0:8, i, :], rows[0:8, h * HALF:(h + 1) * HALF],
                                      start=True, stop=True).then_inc(full[b], 1)

                def operands(c):
                    if c < NCH:
                        return P, [[brt[:, g * H + h, cols(c)] for h in range(H)] for g in range(3)]
                    return SW, [[SMP[:, g * H + h, :] for h in range(H)] for g in range(3)]

                def hcol(bank, w, h, parts=P):
                    return psum(bank)[0:parts, h * w:(h + 1) * w]

                def per_head(bank, product):
                    acquire(bank)
                    for h in range(H):
                        mm = product(h)
                    mm.then_inc(full[bank], 1)

                def turn(bank, tiles, w):
                    per_head(bank, lambda h: pe.transpose(hcol(bank, P, h, w), tiles[h], ident))

                def out_and_state(t, val, b0=0):
                    acquire(b0 + 2)
                    for h in range(H):
                        pe.matmul(hcol(b0 + 2, P, h), ST[:, h, :], t["qg"][:, h, :], start=True, stop=False)
                        mm = pe.matmul(hcol(b0 + 2, P, h), val[:, h, :], t["sc"][:, h, :], start=False, stop=True)
                    mm.then_inc(full[b0 + 2], 1)
                    per_head(b0 + 3, lambda h: pe.matmul(hcol(b0 + 3, P, h), t["kend"][:, h, :], val[:, h, :],
                                                         start=True, stop=True))

                def sample_heads(delta):
                    t = small
                    k.next(sig("states_landed"), 16 * H)

                    def with_state(bank, h, val, mat, w):
                        o = h * SW
                        pe.matmul(B[:, bank, o:o + SW], val, mat, start=True, stop=False, skip_group_check=True)
                        for b in range(NS):
                            mm = pe.matmul(B[:, bank, o + b * LS:o + (b + 1) * LS], S8[:, h, b, :],
                                           w[:, h, b * LS:(b + 1) * LS], start=False, stop=b == NS - 1,
                                           skip_group_check=True)
                        return mm

                    val = t["v"][0:SW]
                    if delta:
                        per_head(1, lambda h: with_state(1, h, val[:, h, :], t["u"][0:SW, h, :], t["w"]))
                        k.next(sig("ut_copied"))
                        per_head(1, lambda h: pe.transpose(B[0:SW, 1, h * P:(h + 1) * P], t["ut"][:, h, :], ident))
                        k.peek(free[1])
                        val = US
                    per_head(2, lambda h: with_state(2, h, val[:, h, :], t["sc"][0:SW, h, :], t["qg"]))
                    for h in range(H):
                        k.next(sig("masked_values" if h < H // 2 else "masked_values_pool"))
                        for half, bank in enumerate(((0, 3), (1, 2))[h % 2]):
                            acquire(bank)
                            pe.matmul(B[:, bank, :], t["kend"][0:SW, h, :], UM[0:SW, h, 4 * half:4 * half + 4, :],
                                      start=True, stop=True).then_inc(full[bank], 1)

                def gdn_start(c):
                    w, (q, kk, v) = operands(c)
                    b0 = banks_of(c)
                    turn(b0, kk, w)
                    turn(b0 + 1, v, w)
                    for bank, r in ((b0 + 2, kk), (b0 + 3, q)):
                        per_head(bank, lambda h: pe.matmul(hcol(bank, w, h, w), kk[h], r[h], start=True, stop=True))
                    rows = ROWS if c == NCH else ROW[:, cols(c)]
                    for bank, p0, m in ((b0, 0, P), (b0 + 1, 32, w)):
                        per_head(bank, lambda h: pe.matmul(hcol(bank, w, h, m), sel[p0:p0 + H, h, 0:m],
                                                           rows[p0:p0 + H, :], start=True, stop=True))

                def gdn_level(chunks, lv):
                    last = lv == (S_LEVELS if chunks[0] == NCH else LEVELS) - 1
                    for c in chunks:
                        w, t, b0 = (SW, small, 0) if c == NCH else (P, sets[c % 2], banks_of(c))
                        k.next(sig(f"level_ready_{c % 2}"))
                        if lv > 1:
                            k.peek(free[b0 + 1])
                        al = t["l0" if lv % 2 else "l1"]
                        per_head(b0, lambda h: pe.matmul(hcol(b0, w, h, w), al[0:w, h, :],
                                                         ident[0:w, 0:w] if lv == 1 else t["t"][0:w, h, :],
                                                         start=True, stop=True))
                    for c in chunks:
                        w, t, b0 = (SW, small, 0) if c == NCH else (P, sets[c % 2], banks_of(c))
                        xs = t["x"]
                        uu = [ident[0:w, 0:w] if lv == 1 else t["u"][0:w, h, :] for h in range(H)]
                        k.peek(free[b0])
                        if lv > 1:
                            k.peek(free[b0 + 2])
                        if not last:
                            per_head(b0 + 1, lambda h: pe.matmul(hcol(b0 + 1, w, h, w), uu[h], xs[0:w, h, :],
                                                                 start=True, stop=True))
                        per_head(b0 + 2, lambda h: pe.matmul(hcol(b0 + 2, w, h, w), xs[0:w, h, :], uu[h],
                                                             start=True, stop=True))

                def gdn_w(c):
                    w, t, b0 = (SW, small, 0) if c == NCH else (P, sets[c % 2], banks_of(c))
                    k.peek(free[b0 + 2])
                    per_head(b0, lambda h: pe.matmul(hcol(b0, w, h), t["bgk"][0:w, h, :], t["u"][0:w, h, :],
                                                     start=True, stop=True))

                def gdn_finish(c):
                    t, b0 = (small, 0) if c == NCH else (sets[c % 2], banks_of(c))
                    k.peek(free[b0])
                    k.next(sig("gated_q_ready"))
                    if c == NCH:
                        sample_heads(True)
                        return
                    if c:
                        k.peek(free[banks_of(c - 1) + 3])
                    acquire(b0 + 1)
                    for h in range(H):
                        pe.matmul(hcol(b0 + 1, P, h), t["u"][:, h, :], t["v"][:, h, :], start=True, stop=False)
                        mm = pe.matmul(hcol(b0 + 1, P, h), t["w"][:, h, :], ST[:, h, :], start=False, stop=True)
                    mm.then_inc(full[b0 + 1], 1)
                    k.peek(free[b0 + 1])
                    out_and_state(t, t["uv"], b0)

                def gdn():
                    for n in range(2):
                        buffer(base["merge0"] + n, None)
                    for chunks in CHUNKS:
                        for c in chunks:
                            gdn_start(c)
                        for lv in range(1, S_LEVELS if chunks[0] == NCH else LEVELS):
                            gdn_level(chunks, lv)
                        for c in chunks:
                            gdn_w(c)
                        for c in chunks:
                            gdn_finish(c)

                def ret(c):
                    w, (q, kk, v) = operands(c)
                    turn(0, kk, w)
                    turn(1, v, w)
                    per_head(3, lambda h: pe.matmul(hcol(3, w, h, w), kk[h], q[h], start=True, stop=True))
                    k.next(sig("chunk_ready"))
                    if c == NCH:
                        sample_heads(False)
                    else:
                        k.peek(free[3])
                        out_and_state(big, big["v"])

                def hg(c):
                    w, (q, kk, v) = operands(c)
                    t = small if c == NCH else hgb
                    levels = S_LEVELS if c == NCH else LEVELS
                    k.next(sig("kend_ready"))
                    turn(0, [t["ked"][:, h, :] for h in range(H)], w)
                    turn(1, v, w)
                    k.next(sig("levels_ready"))
                    for h in range(H):
                        for lv in range(levels):
                            bank = 2 + lv // 4
                            if lv % 4 == 0:
                                acquire(bank)
                            a, b = (kk[h], q[h]) if lv == 0 else (t["xl"][:, lv - 1, h, :],) * 2
                            mm = pe.matmul(hcol(bank, P, lv % 4, w)[:, 0:w], a, b, start=True, stop=True)
                            if lv % 4 == 3 or lv == levels - 1:
                                mm.then_inc(full[bank], 1)
                    k.next(sig("chunk_ready"))
                    if c == NCH:
                        sample_heads(False)
                    else:
                        k.peek(free[3])
                        out_and_state(t, t["v"])

                def out_norm(n):
                    if n == 1:
                        k.next(sig("outputs_ready"))
                        for i in range(H):
                            for h in range(2):
                                b = 2 * (i % 2) + h
                                acquire(b)
                                pe.matmul(B[:, b, 0:HALF], ones, brt[:, i, h * HALF:(h + 1) * HALF],
                                          start=True, stop=True).then_inc(full[b], 1)
                    feature_sums(H, lambda i: hot[:, i, :], 8, sq_o)
                    spread(RWO, H)

                feature_sums(KD, lambda i: ones, P, sq_m)
                acquire(2)
                for i in range(2 * KD // ADG):
                    k.next(sig(f"ada_group_landed_{i}"), 16)
                    for j in range(ADG):
                        mm = ada(ada_group[i % 3][:, j, :], B[:, 2, (i * ADG + j) * (1 + NS):(i * ADG + j + 1) * (1 + NS)])
                    mm.then_inc(sig("ada_group_used"), 1)
                for n in range(3):
                    gemm(n, None, KD, HH, n == 0)
                slab_pairs(pe, "first", 3, 10, lambda n, i, g: gemm(n, g, KD, HH))
                acquire(0)
                acquire(1)
                k.next(sig("square_ready"), 2 * H)
                for i in range(2 * H):
                    for h in range(2):
                        mm = pe.matmul(B[0:8, h, 0:HALF], hot[:, i, :], SQ8[:, i, h * HALF:(h + 1) * HALF],
                                       start=i == 0, stop=i == 2 * H - 1)
                mm.then_inc(sig("l2_sums"), 1)
                slab_pairs(pe, "first", 13, 4, lambda n, i, g: gemm(n, g, KD, HH))
                spread(RW, 2 * H)
                k.next(sig("gate_rows_ready"))
                per_head(0, lambda c: pe.transpose(B[:, 0, c * P:(c + 1) * P], ROW[:, cols(c)], ident))
                acquire(1)
                pe.transpose(B[0:SW, 1, 0:P], ROWS, ident).then_inc(full[1], 1)
                for n, (name, mixer) in enumerate((("first", gdn), ("ret", ret), ("hg", hg))):
                    if n:
                        segment_with_ada(name)
                    k.next(sig("branch_ready"))
                    if n == 0:
                        gdn()
                    else:
                        for c in range(NCH + 1):
                            mixer(c)
                    out_norm(n)
                    k.next(sig("o_ready"))
                    merge_segment(f"merge{n}")
                segment("out", HH, 8, fresh=True)
                feature_sums(KD, lambda i: ones, P, sq_m)
                for f in range(2):
                    segment(f"gu{f}", HH, 8, fresh=f == 0)
                    k.next(sig("act_ready"))
                    segment(f"dn{f}", AH, KF)

            @block.vector
            def _(dve):
                k = Counts(dve, own["vector"])

                def release(*banks):
                    k.settle()
                    for b in banks:
                        dve.nop().then_inc(free[b], 1)

                def say(name):
                    k.settle()
                    dve.nop().then_inc(sig(name), 1)

                def bc(ap, shape):
                    return ap.broadcast_to(shape)

                def norm():
                    k.next(sig("root_ready"))
                    release(0, 1)
                    k.link(dve.reciprocal(RSTD, RSTD))
                    k.settle()
                    for i in range(KD):
                        k.link(dve.tensor_tensor(TN[:, i, :], X[:, i, :], RSTD, ALU.mult))

                def modulate(shift, scale, gain):
                    k.link(dve.scalar_tensor_tensor(
                        out=SCG[:, :, :], in0=MOD[:, scale:scale + KD, :], scalar=1.0,
                        in1=bc(PR[:, gain:gain + KD].unsqueeze(2), [P, KD, 1 + NS]), op0=ALU.add, op1=ALU.mult))
                    say("modulation_ready")
                    sc, sh = (x.rearrange("p i (a b) -> p i a b", a=2) for x in (SCG[:, :, 1:], MOD[:, shift:shift + KD, 1:]))
                    ys = [YS[:, a].rearrange("p i (b t) -> p i b t", b=4) for a in range(2)]

                    def columns(x, a):
                        return x[:, :, a * HALF + PH:(a + 1) * HALF]

                    def both(op):
                        for a in range(2):
                            k.link(op(a))
                        k.settle()

                    both(lambda a: dve.tensor_tensor(ys[a], columns(TN, a).rearrange("p i (b t) -> p i b t", b=4),
                                                     bc(sc[:, :, a].unsqueeze(3), [P, KD, 4, LS]), ALU.mult))
                    both(lambda a: dve.tensor_tensor(ys[a], ys[a], bc(sh[:, :, a].unsqueeze(3), [P, KD, 4, LS]), ALU.add))
                    both(lambda a: dve.tensor_copy(columns(HH[:, 0], a), YS[:, a]))
                    both(lambda a: dve.tensor_tensor(columns(HH[:, 1], a), YS[:, a], columns(HH[:, 0], a).bitcast(F32),
                                                     ALU.subtract))

                    def whole(i):
                        k.link(dve.tensor_scalar(prompt(YP[i % 2]), prompt(TN[:, i, :]), SCG[:, i, 0:1],
                                                 MOD[:, shift + i, 0:1], ALU.mult, ALU.add))

                    whole(0)
                    for i in range(KD):
                        k.settle()
                        if i + 1 < KD:
                            if i:
                                dve.wait_ge(sig("h_ready"), h_base[0] + i)
                            whole(i + 1)
                        k.next(sig("h_hi"))
                        dve.tensor_tensor(prompt(HH[:, 1, i, :]), prompt(YP[i % 2]), prompt(HH[:, 0, i, :]).bitcast(F32),
                                          ALU.subtract).then_inc(sig("h_ready"), 1)
                    h_base[0] += KD

                h_base = [0]

                def pairs(name, first, count, body, per):
                    n0 = base[name] + first
                    with dve.Fori(0, count // 2) as g:
                        k.begin(g, per)
                        for j in range(2):
                            body(n0 + j, g, j)
                        k.end(count // 2)

                def wait_tile(n, g):
                    dve.wait_ge(tile_done, n + 1 if g is None else n + 1 + 2 * g)

                def gp(n):
                    return GP[:, n % 2 * 2:n % 2 * 2 + 2, 0:HALF]

                def add_gated(name, gate):
                    def body(n, g, j):
                        wait_tile(n, g)
                        xi = X[:, 2 * g + j, :]
                        src, tmp = gp(n), SCT[:, :]
                        g4 = GTB[:, 2 * g + j, :].rearrange("p (a b) -> p a b", a=2)
                        k.link(dve.tensor_tensor(tmp.rearrange("p (a b t) -> p a b t", a=2, b=4),
                                                 by_seq(src[:, :, PH:HALF]), bc(g4.unsqueeze(3), [P, 2, 4, LS]), ALU.mult))
                        k.settle()
                        k.link(dve.tensor_tensor(sample(xi), sample(xi), tmp.rearrange("p (a b) -> p a b", a=2), ALU.add))
                        k.link(dve.scalar_tensor_tensor(
                            out=prompt(xi), in0=src[:, :, 0:PH], scalar=GTP[:, bass.ds(2 * g + j, 1)],
                            in1=prompt(xi), op0=ALU.mult, op1=ALU.add))
                        k.settle()
                        dve.nop().then_inc(buf_free[n % 2], 1)
                    k.link(dve.tensor_copy(GTB[:, :, :], MOD[:, gate:gate + KD, 1:]))
                    k.link(dve.tensor_copy(GTP[:, :], MOD[:, gate:gate + KD, 0]))
                    k.settle()
                    pairs(name, 0, 8, body, {own["vector"]: 6})

                for b in range(8):
                    dve.nop().then_inc(free[b], 1)
                dve.wait_ge(sig("params_landed"), 16)
                k.link(dve.tensor_copy(LBC[:, 0, :], LB[:, l, :]))
                k.settle()
                k.link(dve.tensor_scalar(LBC[:, 1, :], LBC[:, 0, :], -1.0, 1.0, ALU.mult, ALU.add))
                k.next(sig("a_exp"))
                k.link(dve.tensor_scalar(neg_a, neg_a, -1.0, None, ALU.mult))
                for i in range(2):
                    k.link(dve.memset(XP[i][:, 0:3], 0.0))

                def modulation(bank, first):
                    k.link(dve.tensor_tensor(
                        MOD[:, first:first + 2 * KD, :],
                        B[:, bank, 0:2 * KD * (1 + NS)].rearrange("p (i j) -> p i j", j=1 + NS),
                        bc(PR[:, P_BADA + first:P_BADA + first + 2 * KD].unsqueeze(2), [P, 2 * KD, 1 + NS]), ALU.add))
                    release(bank)

                norm()
                dve.wait_ge(sig("ada_group_used"), 2 * KD // ADG)
                modulation(2, 0)
                modulate(0, KD, P_NMIX)

                wait_tile(0, None)
                dve.tensor_copy(halves(ABROW), GP[0:64, 0:2, 0:HALF]).then_inc(buf_free[0], 1)
                dve.wait_ge(sig("conv_landed"), 16)

                def conv(n, g, j):
                    i = n - 1 if g is None else 2 * g + (n - 1)
                    xp = XP[n % 2]
                    xs = xp[:, 3 + SEQ:].rearrange("p (b t) -> p b t", b=NS)
                    cs = CSMP[n % 2].rearrange("p (b t) -> p b t", b=NS)
                    wait_tile(n, g)
                    k.link(dve.tensor_copy(halves(xp[:, 3:3 + SEQ]), gp(n)[:, :, 0:PH]))
                    dve.tensor_copy(xs[:, :, 3:].rearrange("p (a b) t -> p a b t", a=2),
                                    by_seq(gp(n)[:, :, PH:HALF])).then_inc(buf_free[n % 2], 1)
                    c0 = CONV0[:, i, :].rearrange("p (b t) -> p b t", b=NS)
                    k.link(dve.tensor_copy(xs[:, :, 0:3], c0))
                    k.settle()
                    c1 = CONV1[:, i, :]
                    k.link(dve.tensor_copy(c1[:, 0:3], xp[:, SEQ:SEQ + 3]))
                    k.link(dve.tensor_copy(c1[:, 3:].rearrange("p (b t) -> p b t", b=NS), xs[:, :, 4:7]))
                    k.next(sig("conv_slot_free"))
                    out = prompt(brt[:, i, :])
                    for tap in range(CONV_W):
                        wt = PR[:, bass.ds(i * CONV_W + tap, 1)]
                        xin = halves(xp[:, tap:tap + SEQ])
                        if tap == 0:
                            k.link(dve.tensor_scalar(out, xin, wt, None, ALU.mult))
                            k.link(dve.tensor_scalar(cs, xs[:, :, 0:LS], wt, None, ALU.mult))
                            k.settle()
                            continue
                        k.link(dve.scalar_tensor_tensor(out=out, in0=xin, scalar=wt, in1=out, op0=ALU.mult, op1=ALU.add))
                        ins = dve.scalar_tensor_tensor(out=cs, in0=xs[:, :, tap:tap + LS], scalar=wt, in1=cs,
                                                       op0=ALU.mult, op1=ALU.add)
                        if tap < CONV_W - 1:
                            k.link(ins)
                            k.settle()
                        else:
                            ins.then_inc(sig("conv_done"), 1)
                            k.settle()

                for n in (1, 2):
                    conv(n, None, n - 1)
                pairs("first", 3, 10, conv, {own["vector"]: 2 * 11, sig("conv_slot_free"): 2})
                say("conv_saved")

                def rows_of(rw, scale_q):
                    k.next(sig("root_ready"))
                    release(0, 1)
                    k.link(dve.reciprocal(rw[0:8, :], rw[0:8, :]))
                    if scale_q:
                        k.settle()
                        k.link(dve.tensor_scalar(rw[0:H, :], rw[0:H, :], float(P) ** -0.5, None, ALU.mult))
                    say("rows_ready")

                def bank_pair(i):
                    b = 2 * (i % 2)
                    k.next(full[b])
                    k.next(full[b + 1])
                    return B[:, b:b + 2, 0:HALF], b

                a1, a2 = wide[1][0:H, :], wide[2][0:H, :]
                k.next(sig("conv_slot_free"), 2)
                k.link(dve.memset(ROW, 0.0))
                k.link(dve.memset(COL[:, NCH, :], 0.0))
                k.link(dve.tensor_scalar(a1, ABROW[0:H, :], PR[0:H, P_DT:P_DT + 1], None, ALU.add))
                k.settle()
                k.link(dve.tensor_scalar(a2, a1, -1.0, None, ALU.mult))
                k.settle()
                k.link(dve.tensor_tensor(a2, a1, a2, ALU.min))
                say("gate_args")
                k.next(sig("gate_logs"))
                k.link(dve.scalar_tensor_tensor(out=a1, in0=a1, scalar=0.0, in1=a2, op0=ALU.max, op1=ALU.add))
                k.settle()
                k.link(dve.tensor_scalar(a1, a1, neg_a, None, ALU.mult))
                k.settle()
                k.link(dve.tensor_tensor_scan(ROW[0:H, :], reset[0:H, :], a1, 0.0, ALU.mult, ALU.add))
                k.settle()
                k.link(dve.tensor_copy(ROW[32:32 + H, :], wide[3][32:32 + H, :]))
                g4 = prompt(ROW[0:H, :]).rearrange("p a (c t) -> p a c t", c=2)
                e4 = prompt(ROW[64:64 + H, :]).rearrange("p a (c t) -> p a c t", c=2)
                k.link(dve.tensor_tensor(e4, bc(g4[:, :, :, P - 1:P], [H, 2, 2, P]), g4, ALU.subtract))
                g4, e4 = by_seq(sample(ROW[0:H, :])), by_seq(sample(ROW[64:64 + H, :]))
                k.link(dve.tensor_tensor(e4, bc(g4[:, :, :, LS - 1:LS], [H, 2, 4, LS]), g4, ALU.subtract))
                k.settle()
                k.link(dve.tensor_copy(halves(ROWS), sample(ROW)))
                say("gate_rows_ready")
                rows_of(RW, True)
                for i in range(2 * H):
                    src, b = bank_pair(i)
                    k.link(dve.tensor_tensor(halves(brt[:, i, :]), src, halves(brt[:, i, :]), ALU.mult))
                    release(b, b + 1)
                k.next(full[0])
                k.link(dve.tensor_copy(COL[:, 0:NCH, :], B[:, 0, :].rearrange("p (c j) -> p c j", c=NCH)[:, :, 0:96]))
                release(0)
                k.next(full[1])
                k.link(dve.tensor_copy(COL[0:SW, NCH, :], B[0:SW, 1, 0:96]))
                release(1)
                say("gate_cols")
                k.next(sig("gate_exps"))
                k.link(dve.tensor_tensor(CE[:, :, 8:12], CE[:, :, 0:4], COL[:, :, 32:36], ALU.mult))

                def start_branch(tiles):
                    for i in range(0, tiles, H):
                        src = 16 if i == 12 else i
                        k.settle()
                        k.link(dve.tensor_copy(SMP[:, i:i + H, :].rearrange("p i (a b) -> p i a b", a=2),
                                               brt[:, src:src + H, :].rearrange("p i (a b) -> p i a b", a=2)[:, :, :, PH:]))
                    k.link(dve.memset(ST[:, :, :], 0.0))
                    say("branch_ready")

                def bank4(b, w=P, parts=P, inner=P):
                    return psum(b)[0:parts, 0:H * w].rearrange("p (h t) -> p h t", h=H)[:, :, 0:inner]

                def by_token(col, parts, w=P):
                    return bc(col.unsqueeze(2), [parts, H, w])

                def finish_chunk(decay, c, b0=0):
                    k.next(full[b0 + 2])
                    k.link(dve.tensor_copy(brt[:, 0:H, cols(c)], bank4(b0 + 2)))
                    release(b0 + 2)
                    k.next(full[b0 + 3])
                    for h in range(H):
                        k.link(dve.scalar_tensor_tensor(out=ST[:, h, :], in0=ST[:, h, :], scalar=decay(h),
                                                        in1=bank4(b0 + 3)[:, h, :], op0=ALU.mult, op1=ALU.add))
                    release(b0 + 3)
                    if c == NCH - 1:
                        dve.nop().then_inc(sig("prompt_state_done"), 1)

                def sample_heads(delta, eg):
                    val = small["v"][0:SW]
                    if delta:
                        k.next(full[1], 2)
                        k.link(dve.tensor_copy(US, bank4(1, P, SW)))
                        release(1)
                        val = US
                    say("values_ready")
                    for h in range(H // 2):
                        k.link(dve.tensor_tensor(UM[0:SW, h], bc(val[:, h].unsqueeze(1), [SW, NS, P]), seqs, ALU.mult))
                        say("masked_values")
                    k.next(full[2])
                    k.link(dve.tensor_copy(brt[:, 0:H, :].rearrange("p i (a b) -> p i a b", a=2)[:, :, :, PH:],
                                           B[:, 2, 0:H * SW].rearrange("p (i a b) -> p i a b", i=H, a=2)))
                    release(2)
                    k.next(sig("states_landed"), 16 * H)
                    for h in range(H):
                        for half, bank in enumerate(((0, 3), (1, 2))[h % 2]):
                            k.next(full[bank])
                            for b in range(4 * half, 4 * half + 4):
                                k.link(dve.scalar_tensor_tensor(
                                    out=S8[:, h, b, :], in0=S8[:, h, b, :], scalar=eg[:, h, b * LS + LS - 1:b * LS + LS],
                                    in1=B[:, bank, b % 4 * P:(b % 4 + 1) * P], op0=ALU.mult, op1=ALU.add))
                            release(bank)
                        say("sample_state_done")

                def gdn_start(c):
                    sm = c == NCH
                    w, t, b0 = (SW, small, 0) if sm else (P, sets[c % 2], banks_of(c))
                    q = SMP[:, 0:H, :] if sm else brt[:, 0:H, cols(c)]
                    incl = C[0:w, C_INCLS:C_INCLS + SW] if sm else C[:, C_INCL:C_INCL + P]
                    k.next(full[b0])
                    k.link(dve.tensor_tensor(t["bgk"][0:w], bank4(b0, P, w), by_token(CE[0:w, c, 8:12], w), ALU.mult))
                    k.link(dve.tensor_tensor(t["kend"][0:w], bank4(b0, P, w), by_token(CE[0:w, c, 4:8], w), ALU.mult))
                    release(b0)
                    k.next(full[b0 + 1])
                    k.link(dve.tensor_tensor(t["v"][0:w], bank4(b0 + 1, P, w), by_token(COL[0:w, c, 32:36], w), ALU.mult))
                    release(b0 + 1)
                    k.next(sig("eg_ready"))
                    k.next(full[b0])
                    k.link(dve.tensor_tensor(t["dt"][0:w], bank4(b0, w, w, w), by_token(COL[0:w, c, 0:4], w, w), ALU.subtract))
                    release(b0)
                    k.link(dve.tensor_scalar(t["dt"][0:w], t["dt"][0:w], 0.0, None, ALU.min))
                    say("decay_args")
                    if not sm:
                        k.link(dve.tensor_copy(EGE[:, c % 2, :], t["eg"][:, :, P - 1]))
                        k.settle()
                    k.link(dve.tensor_tensor(t["qg"], q, t["eg"], ALU.mult))
                    say("gated_q_ready")
                    k.next(sig("decay_ready"))
                    k.link(dve.tensor_tensor(t["dt"][0:w], t["dt"][0:w], bc(incl.unsqueeze(1), [w, H, w]), ALU.mult))
                    k.settle()
                    k.next(full[b0 + 2])
                    k.link(dve.tensor_tensor(t["a"][0:w], bank4(b0 + 2, w, w, w), t["dt"][0:w], ALU.mult))
                    release(b0 + 2)
                    k.next(full[b0 + 1])
                    k.link(dve.tensor_tensor(t["a"][0:w], bank4(b0 + 1, w, w, w), t["a"][0:w], ALU.mult))
                    release(b0 + 1)
                    k.next(full[b0 + 3])
                    k.link(dve.tensor_tensor(t["sc"][0:w], bank4(b0 + 3, w, w, w), t["dt"][0:w], ALU.mult))
                    release(b0 + 3)
                    level_mask(c, 1)

                def level_mask(c, lv):
                    w, t = (SW, small) if c == NCH else (P, sets[c % 2])
                    m = bc(mask[0:w, lv, 0:w].unsqueeze(1), [w, H, w])
                    k.link(dve.tensor_tensor(t["l0" if lv % 2 else "l1"][0:w], t["a"][0:w], m, ALU.mult))
                    say(f"level_ready_{c % 2}")

                def gdn_level(c, lv):
                    w, t, b0 = (SW, small, 0) if c == NCH else (P, sets[c % 2], banks_of(c))
                    levels = S_LEVELS if c == NCH else LEVELS
                    if lv + 1 < levels:
                        level_mask(c, lv + 1)
                    for bank, name in ((1, "t"), (2, "u")):
                        if bank == 1 and lv == levels - 1:
                            continue
                        k.next(full[b0 + bank])
                        old = bc(ident[0:w, 0:w].unsqueeze(1), [w, H, w]) if lv == 1 else t[name][0:w]
                        k.link(dve.tensor_tensor(t[name][0:w], old, bank4(b0 + bank, w, w, w), ALU.subtract))
                        release(b0 + bank)

                def gdn():
                    for chunks in CHUNKS:
                        levels = S_LEVELS if chunks[0] == NCH else LEVELS
                        for c in chunks:
                            gdn_start(c)
                        for lv in range(1, levels):
                            for c in chunks:
                                gdn_level(c, lv)
                        for c in chunks:
                            b0 = banks_of(c)
                            k.skip(full[b0], levels)
                            if c == NCH:
                                sample_heads(True, small["eg"])
                            else:
                                k.skip(full[b0 + 1])
                                finish_chunk(lambda h: EGE[:, c % 2, h:h + 1], c, b0)

                def ret(c):
                    sm = c == NCH
                    w, t = (SW, small) if sm else (P, big)
                    q = SMP[:, 0:H, :] if sm else brt[:, 0:H, cols(c)]
                    heads_of = lambda o, w: C[:, o:o + H * w].rearrange("p (h t) -> p h t", h=H)
                    dec = heads_of(C_DRETS if sm else C_DRET, w)
                    inner = heads_of(C_IRETS if sm else C_IRET, w)
                    ends = C[0:w, C_ENDS:C_ENDS + H] if sm else C[:, C_END:C_END + H]
                    k.next(full[0])
                    k.link(dve.tensor_tensor(t["kend"][0:w], bank4(0, P, w), by_token(ends, w), ALU.mult))
                    release(0)
                    k.next(full[1])
                    k.link(dve.tensor_copy(t["v"][0:w], bank4(1, P, w)))
                    release(1)
                    k.link(dve.tensor_tensor(t["qg"], q, inner, ALU.mult))
                    k.next(full[3])
                    k.link(dve.tensor_tensor(t["sc"][0:w], bank4(3, w, w, w), dec[0:w], ALU.mult))
                    release(3)
                    say("chunk_ready")
                    if sm:
                        sample_heads(False, inner)
                    else:
                        finish_chunk(lambda h: inner[:, h, P - 1:P], c)

                def hg_args(c):
                    sm = c == NCH
                    w, t = (SW, small) if sm else (P, hgb)
                    acc = SMP[:, 12:16, :] if sm else brt[:, 16:20, cols(c)]
                    levels = S_LEVELS if sm else LEVELS
                    blk = LS if sm else P
                    nb = w // blk
                    a4, d4 = (x.rearrange("p h (n t) -> p h n t", n=nb) for x in (acc, t["ked"]))
                    if nb == 1:
                        k.link(dve.tensor_tensor(t["ked"], bc(acc[:, :, P - 1:P], [P, H, P]), acc, ALU.subtract))
                    else:
                        k.link(dve.tensor_tensor(d4, bc(a4[:, :, :, blk - 1:blk], [P, H, nb, blk]), a4, ALU.subtract))
                    say("kend_args")
                    for lv in range(1, levels):
                        m = 1 << (lv - 1)
                        a5, x5 = (x.rearrange("p h (n u t) -> p h n u t", u=2, t=m) for x in (acc, t["xl"][:, lv - 1]))
                        mid = bc(a5[:, :, :, 0, m - 1:m], [P, H, w // (2 * m), m])
                        k.link(dve.tensor_tensor(x5[:, :, :, 0, :], mid, a5[:, :, :, 0, :], ALU.subtract))
                        k.link(dve.tensor_tensor(x5[:, :, :, 1, :], a5[:, :, :, 1, :], mid, ALU.subtract))
                    say("level_args")

                def hg(c):
                    sm = c == NCH
                    w, t = (SW, small) if sm else (P, hgb)
                    q, kk = ((SMP[:, i:i + H, :] for i in (0, 4)) if sm else
                             (brt[:, i:i + H, cols(c)] for i in (0, 4)))
                    levels = S_LEVELS if sm else LEVELS
                    k.next(sig("kend_exps"))
                    if not sm:
                        k.link(dve.tensor_copy(EGE[:, 0, :], t["eg"][:, :, P - 1]))
                    k.link(dve.tensor_tensor(t["ked"], t["ked"], kk, ALU.mult))
                    say("kend_ready")
                    k.link(dve.tensor_tensor(t["qg"], q, t["eg"], ALU.mult))
                    k.next(full[0])
                    k.link(dve.tensor_copy(t["kend"][0:w], bank4(0, P, w)))
                    release(0)
                    k.next(full[1])
                    k.link(dve.tensor_copy(t["v"][0:w], bank4(1, P, w)))
                    release(1)
                    k.next(sig("level_exps"))
                    for lv in range(1, levels):
                        m = 1 << (lv - 1)
                        q5, k5, x5 = (x.rearrange("p h (n u t) -> p h n u t", u=2, t=m) for x in (q, kk, t["xl"][:, lv - 1]))
                        k.link(dve.tensor_tensor(x5[:, :, :, 0, :], x5[:, :, :, 0, :], k5[:, :, :, 0, :], ALU.mult))
                        k.link(dve.tensor_tensor(x5[:, :, :, 1, :], x5[:, :, :, 1, :], q5[:, :, :, 1, :], ALU.mult))
                    say("levels_ready")
                    prod = t["prod"]
                    for h in range(H):
                        for b in range((levels + 3) // 4):
                            n = min(4, levels - 4 * b)
                            k.next(full[2 + b])
                            k.link(dve.tensor_tensor(
                                prod[0:w, 4 * b:4 * b + n, 0:w],
                                B[0:w, 2 + b, :].rearrange("p (l t) -> p l t", l=4)[:, 0:n, 0:w],
                                mask[0:w, 4 * b:4 * b + n, 0:w], ALU.mult))
                            release(2 + b)
                        k.link(dve.tensor_reduce(t["sc"][0:w, h, :], prod[0:w].rearrange("p l t -> p t l"), AX.X, ALU.add))
                        k.settle()
                    say("chunk_ready")
                    if sm:
                        sample_heads(False, t["eg"])
                    else:
                        hg_args(c + 1)
                        finish_chunk(lambda h: EGE[:, 0, h:h + 1], c)

                def out_norm(n):
                    k.settle()
                    if n == 1:
                        say("outputs_ready")
                        for i in range(H):
                            src, b = bank_pair(i)
                            o = halves(brt[:, i, :])
                            k.link(dve.scalar_tensor_tensor(out=o, in0=src, scalar=-1.0 / P, in1=o, op0=ALU.mult, op1=ALU.add))
                            release(b, b + 1)
                    say("outputs_final")
                    for i in range(H):
                        k.link(dve.tensor_tensor(brt[:, 12 + i, :], brt[:, 12 + i, :], brt[:, i, :], ALU.mult))
                    rows_of(RWO, False)
                    gain = {0: PR[:, P_GNORM:P_GNORM + 1], 1: 1.0, 2: PR[:, P_HNORM:P_HNORM + 1]}[n]
                    for i in range(H):
                        src, b = bank_pair(i)
                        k.settle()
                        k.link(dve.scalar_tensor_tensor(out=halves(VAL), in0=src, scalar=gain,
                                                        in1=halves(brt[:, 12 + i, :]), op0=ALU.mult, op1=ALU.mult))
                        release(b, b + 1)
                        k.link(dve.tensor_copy(OH[:, 0, i, :], VAL))
                        k.settle()
                        k.link(dve.tensor_tensor(OH[:, 1, i, :], VAL, OH[:, 0, i, :].bitcast(F32), ALU.subtract))
                    say("o_ready")

                def merge(n):
                    def body(s, g, j):
                        if j == 0:
                            k.next(sig("merge_gate"))
                            dve.nop().then_inc(buf_free[s % 2], 1)
                            return
                        wait_tile(s, g)
                        dst = MG[:, g, :] if n == 0 else VAL
                        k.link(dve.tensor_tensor(halves(dst), gp(s), halves(SG), ALU.mult))
                        k.settle()
                        dve.nop().then_inc(buf_free[s % 2], 1)
                        dve.nop().then_inc(sig("merge_slot_free"), 1)
                        if n:
                            k.link(dve.tensor_tensor(MG[:, g, :], MG[:, g, :], VAL, ALU.add))
                            k.settle()
                    pairs(f"merge{n}", 0, 16, body, {own["vector"]: 2 if n else 1, sig("merge_gate"): 1})

                def copy_tiles(name, first, count, dst):
                    def body(n, g, j):
                        wait_tile(n, g)
                        dve.tensor_copy(halves(brt[:, 2 * g + j + dst, :]), gp(n)).then_inc(buf_free[n % 2], 1)
                    pairs(name, first, count, body, {})

                def rope(n, g, j):
                    k.next(sig("swapped"))
                    out = brt[:, 2 * g + j, :]
                    dve.tensor_tensor(halves(out), gp(n), halves(C[:, C_COS:C_SIN]), ALU.mult).then_inc(buf_free[n % 2], 1)
                    k.link(dve.tensor_tensor(wide[j], wide[j], C[:, C_SIN:C_DRET], ALU.mult))
                    k.settle()
                    k.link(dve.tensor_tensor(out, out, wide[j], ALU.add))
                    say("rope_slot_free")

                def forget(n, g, j):
                    k.next(sig("sigmoids"))
                    dve.nop().then_inc(buf_free[n % 2], 1)
                    i = 2 * g + j
                    f, kk = brt[:, i + 16, :], brt[:, i + 4, :]
                    k.link(dve.scalar_tensor_tensor(out=f, in0=kk, scalar=LBC[:, 0, bass.ds(i, 1)], in1=f,
                                                    op0=ALU.mult, op1=ALU.add))
                    k.settle()
                    k.link(dve.tensor_scalar(kk, kk, LBC[:, 1, bass.ds(i, 1)], None, ALU.mult))

                start_branch(12)
                gdn()
                out_norm(0)
                dve.nop().then_inc(sig("merge_slot_free"), 1)
                merge(0)

                for j in range(2):
                    dve.nop().then_inc(sig(f"ada_slot_{j}_free"), 1)
                dve.nop().then_inc(sig("rope_slot_free"), 2)
                pairs("ret", 0, 8, rope, {own["vector"]: 4, sig("swapped"): 2})
                copy_tiles("ret", 8, 4, 8)
                k.next(full[0])
                modulation(0, 2 * KD)
                k.next(sig("gates_in"))
                dve.wait_ge(sig("stored_prompt"), 16)
                start_branch(12)
                for c in range(NCH + 1):
                    ret(c)
                out_norm(1)
                merge(1)

                for j in range(2):
                    dve.nop().then_inc(sig(f"ada_slot_{j}_free"), 1)
                copy_tiles("hg", 0, 4, 0)
                pairs("hg", 4, 4, forget, {own["vector"]: 4, sig("sigmoids"): 2})
                f4 = BR[:, 16 * T:20 * T]
                k.settle()
                k.link(dve.tensor_scalar(LN1, f4, LN_CUT, None, ALU.max))
                k.link(dve.tensor_scalar(LN2, f4, F_TINY, LN_CUT, ALU.max, ALU.min))
                say("log_args")
                copy_tiles("hg", 8, 4, 8)
                k.next(sig("logs"))
                k.link(dve.tensor_tensor(LN1, LN1, LN2, ALU.add))
                k.settle()
                for h in range(H):
                    k.link(dve.tensor_tensor_scan(brt[:, 16 + h, :], reset, LN1[:, h * T:(h + 1) * T], 0.0,
                                                  ALU.mult, ALU.add))
                k.next(full[0])
                modulation(0, 4 * KD)
                k.next(sig("gates_in"))
                dve.wait_ge(sig("stored_prompt"), 32)
                start_branch(16)
                hg_args(0)
                for c in range(NCH + 1):
                    hg(c)
                out_norm(2)
                merge(2)

                dve.wait_ge(tile_done, base["out"])
                for i in range(KD):
                    k.link(dve.tensor_copy(HH[:, 0, i, :], MG[:, i, :]))
                k.settle()
                for i in range(KD):
                    dve.tensor_tensor(HH[:, 1, i, :], MG[:, i, :], HH[:, 0, i, :].bitcast(F32), ALU.subtract
                                      ).then_inc(sig("h_ready"), 1)
                h_base[0] += KD
                dve.wait_ge(sig("x_back"), 16)
                add_gated("out", 2 * KD)
                say("x_ready")

                dve.wait_ge(tile_done, base["gu0"])
                norm()
                modulate(3 * KD, 4 * KD, P_NFFN)
                dve.nop().then_inc(sig("ffn_slot_free"), 1)
                for f in range(2):
                    def act_tile(s, g, j):
                        if j == 0:
                            k.next(sig("ffn_gate"))
                            dve.nop().then_inc(buf_free[s % 2], 1)
                            return
                        wait_tile(s, g)
                        k.link(dve.tensor_tensor(halves(FT[:, 1, :]), gp(s), halves(FT[:, 0, :]), ALU.mult))
                        k.settle()
                        dve.nop().then_inc(buf_free[s % 2], 1)
                        dve.nop().then_inc(sig("ffn_slot_free"), 1)
                        k.link(dve.tensor_copy(AH[:, 0, g, :], FT[:, 1, :]))
                        k.settle()
                        k.link(dve.tensor_tensor(AH[:, 1, g, :], FT[:, 1, :], AH[:, 0, g, :].bitcast(F32), ALU.subtract))
                        k.settle()
                    pairs(f"gu{f}", 0, 22, act_tile, {own["vector"]: 3, sig("ffn_gate"): 1})
                    say("act_ready")
                    add_gated(f"dn{f}", 5 * KD)

            @block.scalar
            def _(act):
                k = Counts(act, own["scalar"])

                def f(out, in_, func, **kw):
                    return act.activation(out, in_, func, **kw)

                def pairs(name, first, count, body, per):
                    n0 = base[name] + first
                    with act.Fori(0, count // 2) as g:
                        k.begin(g, per)
                        for j in range(2):
                            body(n0 + j, g, j)
                        k.end(count // 2)

                def wait_tile(n, g):
                    act.wait_ge(tile_done, n + 1 if g is None else n + 1 + 2 * g)

                def gp(n, p0=0, p1=P):
                    return GP[p0:p1, n % 2 * 2:n % 2 * 2 + 2, 0:HALF]

                def squares(tiles, sq, rows, out, scale):
                    for i, tile in enumerate(tiles):
                        k.next(sig("square_slot_free"))
                        f(sq[i % 2], tile, ACT.Square).then_inc(sig("square_ready"), 1)
                    k.peek(sig("square_slot_free"), 2)
                    f(halves(out[0:rows, :]), B[0:rows, 0:2, 0:HALF], ACT.Sqrt, scale=scale, bias=epsc[0:rows, :]
                      ).then_inc(sig("root_ready"), 1)

                def high_parts(shift):
                    k.next(sig("modulation_ready"))
                    for i in range(KD):
                        f(prompt(HH[:, 0, i, :]), prompt(TN[:, i, :]), ACT.Identity, scale=SCG[:, i, 0:1],
                          bias=MOD[:, shift + i, 0:1]).then_inc(sig("h_hi"), 1)

                act.wait_ge(sig("params_landed"), 16)
                f(neg_a, PR[0:H, P_ALOG:P_ALOG + 1], ACT.Exp).then_inc(sig("a_exp"), 1)
                squares([X[:, i, :] for i in range(KD)], sq_m, P, RSTD, 1.0 / D)
                high_parts(0)

                act.nop().then_inc(sig("conv_slot_free"), 2)

                def conv(n, g, j):
                    i = n - 1 if g is None else 2 * g + (n - 1)
                    k.next(sig("conv_done"))
                    tile = brt[:, i, :]
                    k.link(f(prompt(tile), prompt(tile), ACT.Silu))
                    k.link(f(sample(tile), halves(CSMP[n % 2]), ACT.Silu))
                    k.settle()
                    act.nop().then_inc(sig("conv_slot_free"), 1)
                    return tile, i

                def conv_square(n, g, j):
                    tile, i = conv(n, g, j)
                    f(SQ8[:, i, :], tile, ACT.Square).then_inc(sig("square_ready"), 1)

                for n in (1, 2):
                    conv_square(n, None, n - 1)
                pairs("first", 3, 6, conv_square, {own["scalar"]: 4, sig("conv_done"): 2})
                pairs("first", 9, 4, conv, {own["scalar"]: 4, sig("conv_done"): 2})

                def gate_tiles(name, first, func):
                    def body(n, g, j):
                        wait_tile(n, g)
                        k.link(f(halves(brt[:, 2 * g + j + 12, :]), gp(n), func))
                        k.settle()
                        act.nop().then_inc(buf_free[n % 2], 1)
                    pairs(name, first, 4, body, {own["scalar"]: 2})

                a2 = wide[2][0:H, :]
                k.next(sig("gate_args"))
                k.link(f(a2, a2, ACT.Exp))
                k.settle()
                k.link(f(a2, a2, ACT.Ln, bias=onec[0:H, :]))
                k.settle()
                f(wide[3][32:32 + H, :], ABROW[32:32 + H, :], ACT.Sigmoid).then_inc(sig("gate_logs"), 1)
                k.next(sig("l2_sums"))
                f(halves(RW[0:8, :]), B[0:8, 0:2, 0:HALF], ACT.Sqrt, bias=epsc[0:8, :]).then_inc(sig("root_ready"), 1)
                gate_tiles("first", 13, ACT.Silu)
                k.next(sig("gate_cols"))
                k.link(f(CE[:, :, 0:4], COL[:, :, 0:4], ACT.Exp))
                f(CE[:, :, 4:8], COL[:, :, 64:68], ACT.Exp).then_inc(sig("gate_exps"), 1)

                def bank4(b, w=P, parts=P, inner=P):
                    return psum(b)[0:parts, 0:H * w].rearrange("p (h t) -> p h t", h=H)[:, :, 0:inner]

                fills = {b: 0 for b in range(8)}

                def filled(b, n=1):
                    fills[b] += n
                    act.wait_ge(full[b], fills[b])

                def skip(b, n=1):
                    fills[b] += n

                for b in range(4):
                    skip(b, H)
                skip(0)
                skip(1)

                def gdn_start(c):
                    w, t, b0 = (SW, small, 0) if c == NCH else (P, sets[c % 2], banks_of(c))
                    skip(b0)
                    filled(b0)
                    f(t["eg"], bank4(b0, w, P, w), ACT.Exp).then_inc(sig("eg_ready"), 1)
                    k.next(sig("decay_args"))
                    f(t["dt"][0:w], t["dt"][0:w], ACT.Exp).then_inc(sig("decay_ready"), 1)

                for chunks in CHUNKS:
                    levels = S_LEVELS if chunks[0] == NCH else LEVELS
                    for c in chunks:
                        gdn_start(c)
                    for lv in range(1, levels + 1):
                        for c in chunks:
                            w, t, b0 = (SW, small, 0) if c == NCH else (P, sets[c % 2], banks_of(c))
                            filled(b0)
                            if lv < levels:
                                f(t["x"][0:w], bank4(b0, w, w, w), ACT.Copy).then_inc(free[b0], 1)
                            else:
                                f(t["w"], bank4(b0, w, P, w), ACT.Copy, scale=-1.0).then_inc(free[b0], 1)
                    for c in chunks:
                        b0 = banks_of(c)
                        skip(b0 + 1, levels)
                        filled(b0 + 1)
                        if c < NCH:
                            f(sets[c % 2]["uv"], bank4(b0 + 1), ACT.Copy).then_inc(free[b0 + 1], 1)
                            continue
                        k.link(f(small["ut"], bank4(1, SW, P, SW), ACT.Copy))
                        k.settle()
                        act.nop().then_inc(free[1], 1)
                        act.nop().then_inc(sig("ut_copied"), 1)

                def out_norm():
                    k.next(sig("outputs_final"))
                    squares([brt[:, i, :] for i in range(H)], sq_o, 8, RWO, 1.0 / P)

                def merge(n):
                    def body(s, g, j):
                        if j == 0:
                            k.next(sig("merge_slot_free"))
                            k.next(sig("gate_product"))
                            f(halves(SG), gp(s), ACT.Sigmoid).then_inc(sig("merge_gate"), 1)
                    pairs(f"merge{n}", 0, 16, body, {sig("merge_slot_free"): 1, sig("gate_product"): 1})

                out_norm()
                merge(0)

                def swap(n, g, j):
                    k.next(sig("rope_slot_free"))
                    wait_tile(n, g)
                    k.link(f(halves(wide[j][0:64, :]), gp(n, 64, P), ACT.Copy))
                    f(halves(wide[j][64:P, :]), gp(n, 0, 64), ACT.Copy).then_inc(sig("swapped"), 1)

                pairs("ret", 0, 8, swap, {own["scalar"]: 2, sig("rope_slot_free"): 2})
                gate_tiles("ret", 12, ACT.Silu)
                act.nop().then_inc(sig("gates_in"), 1)
                out_norm()
                merge(1)

                def forget(n, g, j):
                    wait_tile(n, g)
                    k.link(f(halves(brt[:, 2 * g + j + 16, :]), gp(n), ACT.Sigmoid))
                    f(halves(brt[:, 2 * g + j + 4, :]), gp(n), ACT.Sigmoid, scale=-1.0).then_inc(sig("sigmoids"), 1)

                pairs("hg", 4, 4, forget, {own["scalar"]: 2})
                k.next(sig("log_args"))
                k.link(f(LN1, LN1, ACT.Ln))
                f(LN2, LN2, ACT.Ln, scale=1.0 / LN_CUT).then_inc(sig("logs"), 1)
                gate_tiles("hg", 12, ACT.Sigmoid)
                act.nop().then_inc(sig("gates_in"), 1)
                for c in range(NCH + 1):
                    t = small if c == NCH else hgb
                    acc = SMP[:, 12:16, :] if c == NCH else brt[:, 16:20, cols(c)]
                    k.next(sig("kend_args"))
                    k.link(f(t["eg"], acc, ACT.Exp))
                    f(t["ked"], t["ked"], ACT.Exp).then_inc(sig("kend_exps"), 1)
                    k.next(sig("level_args"))
                    f(t["xl"], t["xl"], ACT.Exp).then_inc(sig("level_exps"), 1)
                out_norm()
                merge(2)

                k.next(sig("x_ready"))
                squares([X[:, i, :] for i in range(KD)], sq_m, P, RSTD, 1.0 / D)
                high_parts(3 * KD)
                for half in range(2):
                    def gate(s, g, j):
                        if j == 0:
                            k.next(sig("ffn_slot_free"))
                            wait_tile(s, g)
                            f(halves(FT[:, 0, :]), gp(s), ACT.Silu).then_inc(sig("ffn_gate"), 1)
                    pairs(f"gu{half}", 0, 22, gate, {sig("ffn_slot_free"): 1})
        clear()

    with nc.Block() as block:
        @block.scalar
        def _(act):
            for i in range(KD):
                if i >= 2:
                    act.wait_ge(sig("square_slot_free"), i - 1)
                act.activation(sq_m[i % 2], X[:, i, :], ACT.Square).then_inc(sig("square_ready"), 1)
            act.wait_ge(sig("square_slot_free"), KD)
            act.activation(halves(wide[0]), B[:, 0:2, 0:HALF], ACT.Sqrt, scale=1.0 / D, bias=epsc
                           ).then_inc(sig("root_ready"), 1)

        @block.tensor
        def _(pe):
            for i in range(KD):
                pe.wait_ge(sig("square_ready"), i + 1)
                for h in range(2):
                    mm = pe.matmul(B[:, h, 0:HALF], ones, sq_m[i % 2][:, h * HALF:(h + 1) * HALF],
                                   start=i == 0, stop=i == KD - 1)
                mm.then_inc(sig("square_slot_free"), 1)

        @block.vector
        def _(dve):
            k = Counts(dve, own["vector"])
            dve.wait_ge(sig("root_ready"), 1)
            k.link(dve.reciprocal(wide[0], wide[0]))
            k.settle()
            for i in range(KD):
                dve.scalar_tensor_tensor(out=X[:, i, :], in0=X[:, i, :], scalar=FN[:, i:i + 1], in1=wide[0],
                                         op0=ALU.mult, op1=ALU.mult).then_inc(sig("y_ready"), 1)

        @block.sync
        def _(sp):
            for i in range(KD):
                sp.wait_ge(sig("y_ready"), i + 1)
                sp.dma_start(y_out[:, i, :], X[:, i, :]).then_inc(sig("stored_y"), 16)
            sp.wait_ge(sig("stored_y"), 16 * KD)

    ctx.close()


def _halves(prompt, sample):
    s = sample.reshape((SW,) + sample.shape[2:])
    return np.concatenate([prompt[:PH], s[:SH], prompt[PH:], s[SH:]])


def _tiles(w):
    L, K, N = w.shape
    return np.ascontiguousarray(w.reshape(L, K // P, P, N // P, P).transpose(0, 3, 2, 1, 4)).reshape(L, N // P, P, K)


def _cols(a):
    return np.swapaxes(a.reshape(a.shape[:-1] + (-1, P)), -1, -2)


def kernel(**inputs):
    import concourse.bacc as bacc
    from concourse.bass_utils import run_bass_kernel_spmd

    i = {n: np.asarray(a) for n, a in inputs.items()}
    f = np.float32
    arrays = {"consts": constants()}
    x = _halves(i["x_prompt"][0], i["x_sample"])
    arrays["x"] = np.ascontiguousarray(x.reshape(T, KD, P).transpose(2, 1, 0))
    cc = np.concatenate([i["c_prompt"], i["c_sample"]])
    arrays["c"] = np.ascontiguousarray(cc.reshape(1 + NS, KD, P).transpose(2, 1, 0))
    par = np.zeros((DEPTH, P, P_W), f)
    par[:, :, P_CONV:P_NMIX] = i["conv_w"].reshape(DEPTH, CONV_W, NCQ, P).transpose(0, 3, 2, 1).reshape(DEPTH, P, -1)
    par[:, :, P_NMIX:P_NFFN] = _cols(i["norm_mix"])
    par[:, :, P_NFFN:P_BADA] = _cols(i["norm_ffn"])
    par[:, :, P_BADA:P_GNORM] = _cols(i["b_ada"])
    par[:, :, P_GNORM] = i["gdn_norm"]
    par[:, :, P_HNORM] = i["hgrn_norm"]
    par[:, 0:H, P_ALOG] = i["gdn_a_log"]
    par[:, 0:H, P_DT] = i["gdn_dt_bias"]
    arrays["params"] = par
    arrays["fnorm"] = np.ascontiguousarray(_cols(i["final_norm"]))
    arrays["lb"] = np.ascontiguousarray(_cols(i["hgrn_lb"]).transpose(1, 0, 2))
    arrays["conv"] = np.ascontiguousarray(
        i["state_gdn_conv"].reshape(DEPTH, NS, 3, NCQ, P).transpose(0, 4, 3, 1, 2)).reshape(DEPTH, P, NCQ, NS * 3)
    w = i["w_in"]
    mk = H * P
    ab = np.zeros((DEPTH, D, P), f)
    ab[:, :, 0:H] = w[:, :, 4 * mk:4 * mk + H]
    ab[:, :, 32:32 + H] = w[:, :, 4 * mk + H:4 * mk + 2 * H]
    o = 4 * mk + 2 * H
    arrays["w_first"] = _tiles(np.concatenate([ab, w[:, :, :4 * mk]], 2))
    arrays["w_ret"] = _tiles(w[:, :, o:o + 4 * mk])
    arrays["w_hg"] = _tiles(w[:, :, o + 4 * mk:o + 8 * mk])
    gate = _tiles(w[:, :, o + 8 * mk:]).reshape(DEPTH, 3, KD, P, D)
    branch = _tiles(i["w_branch"].reshape(DEPTH * 3, mk, D)).reshape(DEPTH, 3, KD, P, mk)
    both = np.concatenate([gate, branch], -1).reshape(DEPTH, 3, KD, P, 2, -1)
    arrays["w_merge"] = np.ascontiguousarray(both.transpose(0, 1, 2, 4, 3, 5))
    arrays["w_out"] = _tiles(i["w_out"])
    gu = _tiles(i["w_gate_up"]).reshape(DEPTH, 2, 2, KF, P, D)
    arrays["w_gu"] = np.ascontiguousarray(gu.transpose(0, 2, 3, 1, 4, 5)).reshape(DEPTH, 2, 2 * KF, P, D)
    dn = _tiles(i["w_down"]).reshape(DEPTH, KD, P, 2, KF * P)
    arrays["w_dn"] = np.ascontiguousarray(dn.transpose(0, 3, 1, 2, 4))
    arrays["w_ada"] = _tiles(i["w_ada"])
    for n, s in (("s_gdn", "state_gdn"), ("s_ret", "state_ret"), ("s_hg", "state_hgrn")):
        arrays[n] = np.ascontiguousarray(i[s])

    outs = {"y": (P, KD, T), "gdn_p": (DEPTH, H, P, P), "conv_new_": (DEPTH, P, NCQ, 3 + NS * 3), "ret_p": (DEPTH, H, P, P),
            "hg_p": (DEPTH, H, P, P), "gdn_s": (DEPTH, NS, H, P, P), "ret_s": (DEPTH, NS, H, P, P),
            "hg_s": (DEPTH, NS, H, P, P)}
    nc = bacc.Bacc("TRN2", target_bir_lowering=False, num_devices=1)
    args = [nc.dram_tensor(f"in_{n}", a.shape, F32, kind="ExternalInput").ap() for n, a in arrays.items()]
    args += [nc.dram_tensor(f"out_{n}", s, F32, kind="ExternalOutput").ap() for n, s in outs.items()]
    trunk(nc, *args)
    r = run_bass_kernel_spmd(nc, [{f"in_{n}": a for n, a in arrays.items()}], core_ids=[0])
    got = {n: np.asarray(r.results[0][f"out_{n}"]) for n in outs}
    y = got["y"].transpose(2, 1, 0).reshape(2, HALF, D)
    y_prompt = np.ascontiguousarray(y[:, :PH]).reshape(1, SEQ, D)
    y_sample = np.ascontiguousarray(y[:, PH:]).reshape(NS, LS, D)
    cv = got["conv_new_"].transpose(0, 3, 2, 1).reshape(DEPTH, 3 + NS * 3, NCQ * P)
    conv_p = np.ascontiguousarray(cv[:, :3]).reshape(DEPTH, 1, 3, NCQ * P)
    conv_s = np.ascontiguousarray(cv[:, 3:]).reshape(DEPTH, NS, 3, NCQ * P)
    one = {n: got[n].reshape(DEPTH, 1, H, P, P) for n in ("gdn_p", "ret_p", "hg_p")}
    return (y_prompt, y_sample, one["gdn_p"], conv_p, one["ret_p"], one["hg_p"],
            got["gdn_s"], conv_s, got["ret_s"], got["hg_s"])
```

```python
from contextlib import ExitStack

import numpy as np

import concourse.bass as bass
from concourse import mybir

F32 = mybir.dt.float32
F32R = mybir.dt.float32r
ALU = mybir.AluOpType
ACT = mybir.ActivationFunctionType
AX = mybir.AxisListType

P = 128
D = 1024
DEPTH = 2
SEQ = 512
NS, LS = 8, 4
H = 4
DFF = 2816
CONV_W = 4
PAST = 4096
EPS = 1e-6
F_TINY = 1e-30
LN_CUT = 2.0 ** -50
KD = D // P
HALF, PH, SH = 272, 256, 16
T = 2 * HALF
NCH = SEQ // P
SW = NS * LS
LEVELS = 8
S_LEVELS = 3
KF = 11
SLAB = KF * P
NCQ = 12

P_CONV = 0
P_NMIX = P_CONV + NCQ * CONV_W
P_NFFN = P_NMIX + KD
P_BADA = P_NFFN + KD
P_GNORM = P_BADA + 6 * KD
P_HNORM = P_GNORM + 1
P_ALOG = P_HNORM + 1
P_DT = P_ALOG + 1
P_W = P_DT + 1

C_ID = 0
C_MASK = C_ID + P
C_COS = C_MASK + LEVELS * P
C_SIN = C_COS + T
C_DRET = C_SIN + T
C_IRET = C_DRET + H * P
C_DRETS = C_IRET + H * P
C_IRETS = C_DRETS + H * SW
C_END = C_IRETS + H * SW
C_ENDS = C_END + H
C_RESET = C_ENDS + H
C_INCL = C_RESET + T
C_INCLS = C_INCL + P
C_SEQ = C_INCLS + SW
C_HOT = C_SEQ + NS
C_SEL = C_HOT + 64
C_ONE = C_SEL + 8 * P
C_W = C_ONE + P


def constants():
    f = np.float32
    c = np.zeros((P, C_W), f)
    c[:, C_ID:C_ID + P] = np.eye(P)
    s, t = np.arange(P)[:, None], np.arange(P)[None, :]
    masks = [s == t] + [(s // (2 * m) == t // (2 * m)) & (s // m % 2 == 0) & (t // m % 2 == 1)
                        for m in (1 << i for i in range(LEVELS - 1))]
    c[:, C_MASK:C_COS] = np.stack(masks, 1).reshape(P, -1)
    pos = np.concatenate([np.concatenate([np.arange(h * PH, (h + 1) * PH), PAST + np.tile(np.arange(LS), NS // 2)])
                          for h in range(2)]).astype(f)
    half = P // 2
    inv = (10000.0 ** (-np.arange(half) / half)).astype(f)
    ang = (inv[:, None] * pos[None, :]).astype(f)
    c[:, C_COS:C_SIN] = np.tile(np.cos(ang), (2, 1))
    c[:, C_SIN:C_DRET] = np.concatenate([-np.sin(ang), np.sin(ang)])
    lg = np.log1p(-np.exp2(-5.0 - np.arange(H)))
    scale = P ** -0.5
    for h in range(H):
        decay = np.where(s <= t, np.exp(lg[h] * (t - s)), 0.0) * scale
        c[:, C_DRET + h * P:C_DRET + (h + 1) * P] = decay
        c[:SW, C_DRETS + h * SW:C_DRETS + (h + 1) * SW] = (decay * (s // LS == t // LS))[:SW, :SW]
        c[:, C_IRET + h * P:C_IRET + (h + 1) * P] = np.exp(lg[h] * (t + 1))
        c[:, C_IRETS + h * SW:C_IRETS + (h + 1) * SW] = np.exp(lg[h] * (t[:, :SW] % LS + 1))
        c[:, C_END + h] = np.exp(lg[h] * (P - 1 - s[:, 0])) * scale
        c[:, C_ENDS + h] = np.exp(lg[h] * (LS - 1 - s[:, 0] % LS)) * scale
    reset = np.ones(T)
    for h in range(2):
        reset[[h * HALF, h * HALF + P]] = 0
        reset[h * HALF + PH:(h + 1) * HALF:LS] = 0
    c[:, C_RESET:C_INCL] = reset
    c[:, C_INCL:C_INCLS] = s <= t
    c[:SW, C_INCLS:C_SEQ] = ((s <= t) & (s // LS == t // LS))[:SW, :SW]
    c[:, C_SEQ:C_HOT] = s // LS == np.arange(NS)
    for i in range(8):
        c[:, C_HOT + 8 * i + i] = 1
        c[i, C_SEL + i * P:C_SEL + (i + 1) * P] = 1
        c[32 + i, C_SEL + i * P:C_SEL + (i + 1) * P] = 1
    c[:, C_ONE:C_W] = 1
    return c


class Counts:

    def __init__(self, eng, own):
        self.eng, self.own, self.n = eng, own, {}
        self.reg, self.per, self.before = None, {}, {}

    def value(self, sem, n):
        return n if self.reg is None else n + self.reg * self.per[sem]

    def next(self, sem, n=1):
        self.n[sem] = self.n.get(sem, 0) + n
        self.eng.wait_ge(sem, self.value(sem, self.n[sem]))

    def peek(self, sem, ahead=1):
        self.eng.wait_ge(sem, self.value(sem, self.n.get(sem, 0) + ahead))

    def skip(self, sem, n=1):
        self.n[sem] = self.n.get(sem, 0) + n

    def link(self, ins):
        self.n[self.own] = self.n.get(self.own, 0) + 1
        ins.then_inc(self.own, 1)

    def settle(self):
        self.eng.wait_ge(self.own, self.value(self.own, self.n[self.own]))

    def begin(self, reg, per):
        self.reg, self.per, self.before = reg, per, dict(self.n)

    def end(self, passes):
        for sem, k in self.per.items():
            got = self.n.get(sem, 0) - self.before.get(sem, 0)
            assert got == k, (sem, got, k)
            self.n[sem] += k * (passes - 1)
        assert all(self.n[s] == self.before.get(s, 0) for s in self.n if s not in self.per)
        self.reg, self.per = None, {}


def trunk(nc, consts_in, x_in, c_in, params_in, fnorm_in, lb_in, conv_in, w_first, w_ret, w_hg, w_merge, w_out,
          w_gu, w_dn, w_ada_first, w_ada, s_gdn, s_ret, s_hg, y_out, gdn_p, conv_out, ret_p, hg_p, gdn_s, ret_s, hg_s):
    ctx = ExitStack()

    def sb(name, shape, dt=F32):
        return ctx.enter_context(nc.sbuf_tensor(name, shape, dt))

    sems = {}

    def sig(name):
        if name not in sems:
            sems[name] = ctx.enter_context(nc.semaphore(name))
        return sems[name]

    X = sb("x", [P, KD, T])
    HH = sb("h_hi_lo", [P, 2, KD, T], F32R)
    raw = sb("w_raw", [P, 2, SLAB])
    whl = sb("w_hi_lo", [P, 2, 2, SLAB], F32R)
    C = sb("consts", [P, C_W])
    PR = sb("params", [P, P_W])
    MOD = sb("mod", [P, 6 * KD, 1 + NS])
    LB = sb("lb", [P, DEPTH, H])
    LBC = sb("lb_layer", [P, 2, H])
    CS = sb("silu_c", [P, KD, 1 + NS])
    CONV0 = sb("conv_state", [P, NCQ, NS * 3])
    CONV1 = sb("conv_new", [P, NCQ, 3 + NS * 3])
    ST = sb("state", [P, H, P])
    FN = sb("final_norm", [P, KD])
    MISC = sb("misc", [P, 64])
    GTB = sb("gate_sample", [P, KD, NS])
    GTP = sb("gate_prompt", [P, KD])
    SCT = sb("gated_sample", [P, SW])
    SCG = sb("scale_gain", [P, KD, 1 + NS])
    SMP = sb("sample_cols", [P, 16, SW])
    CSM = sb("conv_sample", [P, SW])

    M1W = 7680
    XPW = 3 + SEQ + NS * (3 + LS)
    BRW = 20 * T
    with ExitStack() as mix:
        M1 = mix.enter_context(nc.sbuf_tensor("mix_temps", [P, M1W], F32))
        BR = mix.enter_context(nc.sbuf_tensor("branch", [P, BRW], F32))
        MG = mix.enter_context(nc.sbuf_tensor("merged", [P, KD, T], F32))
    X_flat = X[:, :, :].rearrange("p k t -> p (k t)")
    MG_flat = MG[:, :, :].rearrange("p k t -> p (k t)")
    with ExitStack() as mix:
        OH = mix.enter_context(nc.sbuf_tensor("o_hi_lo", [P, 2, H, T], F32R))
        OT = mix.enter_context(nc.sbuf_tensor("o_temps", [P, M1W - 2 * H * T], F32))
    with ExitStack() as ffn:
        AH = ffn.enter_context(nc.sbuf_tensor("ffn_hi_lo", [P, 2, KF, T], F32R))
        FT = ffn.enter_context(nc.sbuf_tensor("ffn_temps", [P, 2, T], F32))
    GP = ctx.enter_context(nc.psum_tensor("gemm_psum", [P, 4, 512], F32))
    B = ctx.enter_context(nc.psum_tensor("mix_psum", [P, 4, 512], F32))

    brt = BR[:, :].rearrange("p (i t) -> p i t", t=T)

    def halves(ap):
        return ap.rearrange("p (a b) -> p a b", a=2)

    def prompt(ap):
        return halves(ap)[:, :, 0:PH]

    def sample(ap):
        return halves(ap)[:, :, PH:HALF]

    def by_seq(ap):
        return ap.rearrange("p a (b t) -> p a b t", t=LS)

    def cols(c):
        o = c // 2 * HALF + c % 2 * P
        return slice(o, o + P)

    ident = C[:, C_ID:C_ID + P]
    mask = C[:, C_MASK:C_COS].rearrange("p (l t) -> p l t", l=LEVELS)
    hot = C[:, C_HOT:C_SEL].rearrange("p (i j) -> p i j", i=8)
    sel = C[:, C_SEL:C_ONE].rearrange("p (i j) -> p i j", i=8)
    ones = C[:, C_ONE:C_W]
    seqs = C[0:SW, C_SEQ:C_SEQ + NS].unsqueeze(2).broadcast_to([SW, NS, P])
    reset = C[:, C_RESET:C_INCL]
    neg_a = MISC[0:H, 1:2]
    epsc = MISC[:, 2:3]
    onec = MISC[:, 3:4]
    EGE = MISC[:, 16:16 + 2 * H].rearrange("p (c h) -> p c h", c=2)

    def heads(o, w):
        return M1[:, o:o + H * w].rearrange("p (h t) -> p h t", h=H)

    BLK = H * P
    order = ("bgk", "kend", "v", "qg", "sc", "a", "t", "u", "x", "l0", "l1")
    flat = [(M1[:, :], i * BLK) for i in range(15)] + [(MG_flat, i * BLK) for i in range(7)]
    sets = []
    for p in range(2):
        where = flat[p * len(order):(p + 1) * len(order)]
        t = {n: m[:, a:a + BLK].rearrange("p (h t) -> p h t", h=H) for n, (m, a) in zip(order, where)}
        t.update(eg=t["qg"], dt=t["x"], w=t["l1"], uv=t["x"])
        sets.append(t)
    rsets = [{n: sets[0][n] for n in ("kend", "v", "qg", "sc")},
             dict({n: sets[1][n] for n in ("kend", "v", "qg")}, sc=sets[1]["bgk"])]
    hgb = {n: heads((9 + i) * BLK, P) for i, n in enumerate(("qg", "ked", "eg", "kend", "v", "sc"))}
    hgb["xl"] = M1[:, 0:7 * BLK].rearrange("p (l h t) -> p l h t", l=LEVELS - 1, h=H)
    hgb["prod"] = M1[:, 7 * BLK:9 * BLK].rearrange("p (l t) -> p l t", l=LEVELS)
    NAR = H * SW
    names = ("eg", "dt", "sc", "a", "l0", "l1", "t", "u", "zero", "x", "w", "qg", "ut", "oq", "ked")
    small = {n: heads(i * NAR, SW) for i, n in enumerate(names)}
    small["xl"] = M1[:, 3 * NAR:5 * NAR].rearrange("p (l h t) -> p l h t", l=S_LEVELS - 1, h=H)
    small["prod"] = M1[:, 6 * NAR:6 * NAR + S_LEVELS * SW].rearrange("p (l t) -> p l t", l=S_LEVELS)
    o = len(names) * NAR
    for i, n in enumerate(("bgk", "kend", "v")):
        small[n] = heads(o + i * BLK, P)
    o += 3 * BLK
    UM = M1[:, o:o + H * NS * P].rearrange("p (h b v) -> p h b v", h=H, b=NS)

    def pair_of(name):
        a = names.index(name) * NAR
        return M1[:, a:a + 2 * NAR].rearrange("p (u h t) -> p u h t", u=2, h=H)

    US = small["bgk"][0:SW]
    S8 = X_flat[:, 0:H * NS * P].rearrange("p (h b v) -> p h b v", h=H, b=NS)
    sq_m = [M1[:, i * T:(i + 1) * T] for i in range(2)]
    wide = [M1[:, i * T:(i + 1) * T] for i in range(2, 8)]
    sq_o = [BR[:, i * T:(i + 1) * T] for i in (16, 17)]
    RWO = BR[:, 18 * T:19 * T]
    VALS = [OT[:, i * T:(i + 1) * T] for i in (2, 3)]
    VAL, SG = VALS[1], OT[:, 4 * T:5 * T]
    RW = wide[0]
    RSTD = wide[0]
    TN = M1[:, 3 * T:11 * T].rearrange("p (i t) -> p i t", i=KD)
    YP = [M1[:, i * T:(i + 1) * T] for i in (11, 12)]
    YS = M1[:, 13 * T:13 * T + KD * SW].rearrange("p (a i t) -> p a i t", a=2, i=KD)
    SQ8 = M1[:, 6 * T:14 * T].rearrange("p (i t) -> p i t", i=8)
    LN1, LN2 = (M1[:, i * H * T:(i + 1) * H * T] for i in range(2))

    o = 16 * T
    XP = [BR[:, o + i * XPW:o + (i + 1) * XPW] for i in range(2)]
    ROW = BR[:, o:o + T]
    ROWS = BR[:, o + T:o + T + SW]
    o += T + SW
    COL = BR[:, o:o + 5 * 96].rearrange("p (c j) -> p c j", c=5)
    o += 5 * 96
    CE = BR[:, o:o + 5 * 12].rearrange("p (c j) -> p c j", c=5)
    CSMP = [MISC[:, 32:64], CSM[:, :]]
    ABROW = MG[0:64, 0, :]
    ADG = 4
    ada_group = [x[:, o:o + ADG * D] for x, o in ((BR, 0), (BR, ADG * D), (MG_flat, 0))]
    ADR = BR[0:1 + NS, 2 * ADG * D:2 * ADG * D + 2 * D]
    ada_slot = [M1[:, M1W - (i + 1) * D:M1W - i * D] for i in range(2)]

    CHUNKS = [(c, c + 1) for c in range(0, NCH, 2)] + [(NCH,)]
    POOL_LEVELS = range(5, LEVELS)

    stream = [("first", 17, 8)]
    for n in range(3):
        if n:
            stream.append(("ret" if n == 1 else "hg", 16, 8))
        stream.append((f"merge{n}", 16, 6))
    stream += [("out", 8, 8)]
    for f in range(2):
        stream += [(f"gu{f}", 22, 8), (f"dn{f}", 8, KF)]
    ADA_FIRST = {"ret": 0, "hg": 2 * KD}
    base, at = {}, 0
    for name, count, _ in stream:
        base[name] = at
        at += count

    def source(name, l, i, odd):
        if name == "first":
            return w_first[l, i]
        if name.startswith("merge"):
            return w_merge[l, int(name[-1]), i, int(odd)]
        if name in ("ret", "hg"):
            return {"ret": w_ret, "hg": w_hg}[name][l, i]
        if name == "out":
            return w_out[l, i]
        return {"gu": w_gu, "dn": w_dn}[name[:2]][l, int(name[-1]), i]

    landed = [sig("slab_landed_0"), sig("slab_landed_1")]
    hi_done, split_done, tile_done = sig("weights_hi"), sig("weights_split"), sig("gemm_tile_done")
    buf_free = [sig("gemm_buffer_0_free"), sig("gemm_buffer_1_free")]
    full = [sig(f"bank_{i}_full") for i in range(8)]
    free = [sig(f"bank_{i}_free") for i in range(8)]

    def psum(b):
        return (B if b < 4 else GP)[:, b % 4, :]

    def banks_of(c):
        return 4 * (c % 2) if c < NCH else 0

    own = {e: sig(f"{e}_steps") for e in ("vector", "scalar", "gpsimd", "tensor")}

    def slab_pairs(eng, name, first, count, body, k=None, per=None):
        with eng.Fori(0, count // 2) as g:
            if k:
                k.begin(g, per)
            for j in range(2):
                body(base[name] + first + j, g + first // 2 if name.startswith("merge") else 2 * g + first + j, g)
            if k:
                k.end(count // 2)

    def each_slab(eng, name, body, k=None, per=None):
        _, count, _ = next(s for s in stream if s[0] == name)
        first = 3 if count % 2 else 0
        for n in range(first):
            body(base[name] + n, n, None)
        slab_pairs(eng, name, first, count - first, body, k, per)

    with nc.Block() as block:
        @block.sync
        def _(sp):
            sp.dma_start(LB[:, :, :], lb_in[:, :, :]).then_inc(sig("lb_landed"), 16)
            sp.dma_start(CS[:, :, :], c_in[:, :, :]).then_inc(sig("c_landed"), 16)
            sp.dma_start(FN[:, :], fnorm_in[:, :]).then_inc(sig("fnorm_landed"), 16)
            sp.dma_start(C[:, :], consts_in[:, :]).then_inc(sig("consts_landed"), 16)
            sp.dma_start(X[:, :, :], x_in[:, :, :]).then_inc(sig("x_landed"), 16)
            for s in ("consts_landed", "x_landed", "fnorm_landed"):
                sp.wait_ge(sig(s), 16)

        @block.scalar
        def _(act):
            act.wait_ge(sig("c_landed"), 16)
            act.activation(CS[:, :, :], CS[:, :, :], ACT.Silu)
            act.wait_ge(sig("lb_shifted"), 1)
            act.activation(LB[:, :, :], LB[:, :, :], ACT.Exp).then_inc(sig("lb_exp"), 1)

        @block.vector
        def _(dve):
            k = Counts(dve, own["vector"])
            k.link(dve.memset(MISC[:, :], 0.0))
            k.settle()
            k.link(dve.memset(epsc, EPS))
            k.link(dve.memset(onec, 1.0))
            dve.wait_ge(sig("lb_landed"), 16)
            top, tot = MISC[:, 8:8 + H], MISC[:, 12:12 + H]
            k.settle()
            k.link(dve.tensor_copy(top, LB[:, 0, :]))
            for l in range(1, DEPTH):
                k.settle()
                k.link(dve.tensor_tensor(top, top, LB[:, l, :], ALU.max))
            k.settle()
            dve.tensor_tensor(LB[:, :, :], LB[:, :, :], top.unsqueeze(1).broadcast_to([P, DEPTH, H]),
                              ALU.subtract).then_inc(sig("lb_shifted"), 1)
            dve.wait_ge(sig("lb_exp"), 1)
            k.link(dve.tensor_copy(tot, LB[:, 0, :]))
            for l in range(1, DEPTH):
                k.settle()
                k.link(dve.tensor_tensor(tot, tot, LB[:, l, :], ALU.add))
            k.settle()
            k.link(dve.reciprocal(tot, tot))
            k.settle()
            k.link(dve.tensor_tensor(LB[:, :, :], LB[:, :, :], tot.unsqueeze(1).broadcast_to([P, DEPTH, H]), ALU.mult))
            k.settle()
            k.link(dve.tensor_copy(top, LB[:, 0, :]))
            for l in range(1, DEPTH):
                k.settle()
                k.link(dve.tensor_tensor(LB[:, l, :], LB[:, l, :], LB[:, l - 1, :], ALU.add))
            k.settle()
            k.link(dve.tensor_tensor(LB[:, :, :], LB[:, :, :], top.unsqueeze(1).broadcast_to([P, DEPTH, H]),
                                     ALU.subtract))
            k.settle()

    def clear():
        for s in sems.values():
            nc.sync.sem_clear(s)
        nc.all_engine_barrier()

    clear()

    with nc.Fori(0, DEPTH) as l:
        with nc.Block() as block:
            @block.sync
            def _(sp):
                k = Counts(sp, None)
                sp.dma_start(PR[:, :], params_in[l]).then_inc(sig("params_landed"), 16)
                sp.dma_start(CONV0[:, :, :], conv_in[l]).then_inc(sig("conv_landed"), 16)
                for i in range(2 * KD // ADG):
                    if i >= 3:
                        sp.wait_ge(sig("ada_group_used"), i - 2)
                    sp.dma_start(ada_group[i % 3], w_ada_first[l, i]).then_inc(sig(f"ada_group_landed_{i}"), 16)


                def load_states(n):
                    if n == 0:
                        sp.wait_ge(sig("stored_x"), 16)
                        sp.wait_ge(sig("modulation_ready"), 1)
                    else:
                        sp.wait_ge(sig("stored_sample"), 16 * H * n)
                    for h in range(H):
                        sp.dma_start(S8[:, h], (s_gdn, s_ret, s_hg)[n][l, :, h].rearrange("b k v -> k b v")
                                     ).then_inc(sig("states_landed"), 16)

                def store_states(n):
                    s_out, p_out = ((gdn_s, gdn_p), (ret_s, ret_p), (hg_s, hg_p))[n]
                    k.next(sig("prompt_state_done"))
                    sp.dma_start(p_out[l].rearrange("h k v -> k h v"), ST[:, :, :]).then_inc(sig("stored_prompt"), 16)
                    for h in range(H):
                        k.next(sig("sample_state_done"))
                        sp.dma_start(s_out[l, :, h].rearrange("b k v -> k b v"), S8[:, h]
                                     ).then_inc(sig("stored_sample"), 16)

                sp.dma_start(y_out[:, :, :], X[:, :, :]).then_inc(sig("stored_x"), 16)
                for seg in stream:
                    def load_slab(n, i, g):
                        name, _, kt = next(x for x in reversed(stream) if base[x[0]] <= n)
                        odd = (n - base[name]) % 2 == 1
                        words = kt * P
                        if n >= 2:
                            sp.wait_ge(split_done, n - 1 if g is None else n - 1 + 2 * g)
                        sp.dma_start(raw[:, n % 2, 0:words], source(name, l, i, odd)).then_inc(landed[n % 2], 16)
                        if name in ADA_FIRST:
                            j = (n - base[name]) % 2
                            k.next(sig(f"ada_slot_{j}_free"))
                            sp.dma_start(ada_slot[j], w_ada[l, i + ADA_FIRST[name]]).then_inc(sig(f"ada_landed_{j}"), 16)

                    if seg[0] in ADA_FIRST:
                        each_slab(sp, seg[0], load_slab, k, {sig("ada_slot_0_free"): 1, sig("ada_slot_1_free"): 1})
                        for j in range(2):
                            k.skip(sig(f"ada_slot_{j}_free"))
                    elif seg[0].startswith("merge"):
                        slab_pairs(sp, seg[0], 2, 14, load_slab)
                    else:
                        each_slab(sp, seg[0], load_slab)
                    if seg[0] in ("first", "ret", "hg"):
                        n = ("first", "ret", "hg").index(seg[0])
                        load_states(n)
                        for j in range(2):
                            load_slab(base[f"merge{n}"] + j, 0, None)
                        store_states(n)
                    if seg[0] == "hg":
                        sp.wait_ge(sig("stored_sample"), 16 * H * 3)
                        sp.dma_start(X[:, :, :], y_out[:, :, :]).then_inc(sig("x_back"), 16)
                sp.wait_ge(sig("conv_saved"), 1)
                sp.dma_start(conv_out[l], CONV1[:, :, :]).then_inc(sig("stored_conv"), 16)
                sp.wait_ge(sig("stored_conv"), 16)
                sp.wait_ge(sig("stored_prompt"), 16 * 3)

            @block.gpsimd
            def _(pool):
                def level_factors(c):
                    q, kk, acc = (brt[:, i:i + H, cols(c)] for i in (0, 4, 16))

                    def split_blocks(x, m):
                        return x.rearrange("p h (n u t) -> p h n u t", u=2, t=m)

                    pool.wait_ge(sig("xl_free"), c + 1)
                    for lv in POOL_LEVELS:
                        m = 1 << (lv - 1)
                        a5, x5 = split_blocks(acc, m), split_blocks(hgb["xl"][:, lv - 1], m)
                        mid = a5[:, :, :, 0, m - 1:m].broadcast_to([P, H, P // (2 * m), m])
                        pool.tensor_tensor(x5[:, :, :, 0, :], mid, a5[:, :, :, 0, :], ALU.subtract
                                           ).then_inc(sig("level_args_pool"), 1)
                        pool.tensor_tensor(x5[:, :, :, 1, :], a5[:, :, :, 1, :], mid, ALU.subtract
                                           ).then_inc(sig("level_args_pool"), 1)
                    pool.wait_ge(sig("level_exps_pool"), c + 1)
                    for lv in POOL_LEVELS:
                        m = 1 << (lv - 1)
                        q5, k5, x5 = (split_blocks(x, m) for x in (q, kk, hgb["xl"][:, lv - 1]))
                        for u, y5 in enumerate((k5, q5)):
                            pool.tensor_tensor(x5[:, :, :, u, :], x5[:, :, :, u, :], y5[:, :, :, u, :], ALU.mult
                                               ).then_inc(sig("levels_ready_pool"), 1)

                for seg in stream:
                    def split(n, i, g):
                        words = next(x for x in reversed(stream) if base[x[0]] <= n)[2] * P

                        def at(v, per):
                            return v if g is None else v + per * g
                        if n >= 2:
                            pool.wait_ge(tile_done, at(n - 1, 2))
                        pool.wait_ge(landed[n % 2], at(16 * (n // 2 + 1), 16))
                        src, hi, lo = raw[:, n % 2, 0:words], whl[:, n % 2, 0, 0:words], whl[:, n % 2, 1, 0:words]
                        pool.tensor_tensor(hi, src, ones[:, 0:1].broadcast_to([P, words]), ALU.mult).then_inc(hi_done, 1)
                        pool.wait_ge(hi_done, at(n + 1, 2))
                        pool.tensor_tensor(lo, src, hi.bitcast(F32), ALU.subtract).then_inc(split_done, 1)

                    if seg[0].startswith("merge"):
                        slab_pairs(pool, seg[0], 2, 14, split)
                    else:
                        each_slab(pool, seg[0], split)
                    if seg[0] in ("first", "ret", "hg"):
                        n = ("first", "ret", "hg").index(seg[0])
                        for j in range(2):
                            split(base[f"merge{n}"] + j, 0, None)
                        if seg[0] == "hg":
                            for c in range(NCH):
                                level_factors(c)
                        pool.wait_ge(sig("values_ready"), n + 1)
                        val = US if n == 0 else small["v"][0:SW]
                        for h in range(H // 2, H):
                            pool.tensor_tensor(UM[0:SW, h], val[:, h].unsqueeze(1).broadcast_to([SW, NS, P]), seqs,
                                               ALU.mult).then_inc(sig("masked_values_pool"), 1)

            @block.tensor
            def _(pe):
                k = Counts(pe, own["tensor"])
                pe.nop().then_inc(sig("square_slot_free"), 2)

                def acquire(b):
                    k.next(free[b])

                def ada(weights, out):
                    w = weights.rearrange("p (k m) -> p k m", k=KD)
                    for kk in range(KD):
                        mm = pe.matmul(out, w[:, kk, :], CS[:, kk, :], start=kk == 0, stop=kk == KD - 1)
                    return mm

                def products(slot, buf, ks, rhs, first=True, last=True, fresh=None):
                    for kw, kr in ks:
                        if fresh:
                            k.next(fresh)
                        for p, (a, b) in enumerate(((0, 0), (0, 1), (1, 0))):
                            for h in range(2):
                                mm = pe.matmul(GP[:, 2 * buf + h, 0:HALF], whl[:, slot, a, kw * P:(kw + 1) * P],
                                               rhs[:, b, kr, h * HALF:(h + 1) * HALF],
                                               start=first and (kw, kr) == ks[0] and p == 0,
                                               stop=last and (kw, kr) == ks[-1] and p == 2)
                    return mm

                def weights(n, g):
                    pe.wait_ge(split_done, n + 1 if g is None else n + 1 + 2 * g)

                def buffer(n, g):
                    if n >= 2:
                        pe.wait_ge(buf_free[n % 2], n // 2 if g is None else n // 2 + g)

                def gemm(n, g, kt, rhs, fresh=None):
                    weights(n, g)
                    buffer(n, g)
                    products(n % 2, n % 2, [(i, i) for i in range(kt)], rhs, fresh=fresh).then_inc(tile_done, 1)

                def segment(name, rhs, kt, fresh=False):
                    _, count, _ = next(s for s in stream if s[0] == name)
                    first = 2 if fresh else 0
                    for j in range(first):
                        gemm(base[name] + j, None, kt, rhs, sig("h_ready") if j == 0 else None)
                    slab_pairs(pe, name, first, count - first, lambda n, i, g: gemm(n, g, kt, rhs))

                def segment_with_ada(name):
                    def tile(n, i, g):
                        j = (n - base[name]) % 2
                        k.next(sig(f"ada_landed_{j}"), 16)
                        ada(ada_slot[j], B[:, 0, bass.ds(i * (1 + NS), 1 + NS)]).then_inc(sig(f"ada_slot_{j}_free"), 1)
                        gemm(n, g, KD, HH)
                    acquire(0)
                    each_slab(pe, name, tile, k, {sig("ada_landed_0"): 16, sig("ada_landed_1"): 16})
                    pe.wait_ge(sig("ada_slot_1_free"), KD + 1 if name == "ret" else 2 * (KD + 1))
                    pe.nop().then_inc(full[0], 1)

                def merge_gate_part(n, g):
                    weights(n, g)
                    if (n - base["merge0"]) % 2 == 0:
                        buffer(n, g)
                        products(n % 2, n % 2, [(i, i) for i in range(6)], HH, last=False).then_inc(tile_done, 1)
                    else:
                        products(n % 2, (n - 1) % 2, [(0, 6), (1, 7)], HH, first=False).then_inc(sig("gate_product"), 1)

                def merge_branch_part(n, g, fresh=None):
                    buffer(n, g)
                    products(n % 2, n % 2, [(2 + i, i) for i in range(4)], OH, fresh=fresh).then_inc(tile_done, 1)

                def merge_rest(name):
                    def tile(n, i, g):
                        merge_gate_part(n, g)
                        if (n - base[name]) % 2:
                            merge_branch_part(n, g)
                    merge_branch_part(base[name] + 1, None, sig("o_ready"))
                    slab_pairs(pe, name, 2, 14, tile)

                def feature_sums(count, lhs, rows, sq):
                    acquire(0)
                    acquire(1)
                    for i in range(count):
                        k.next(sig("square_ready"))
                        for h in range(2):
                            mm = pe.matmul(B[0:rows, h, 0:HALF], lhs(i), sq[i % 2][:, h * HALF:(h + 1) * HALF],
                                           start=i == 0, stop=i == count - 1)
                        mm.then_inc(sig("square_slot_free"), 1)

                def spread(rows, count):
                    k.next(sig("rows_ready"))
                    for i in range(count):
                        for h in range(2):
                            b = 2 * (i % 2) + h
                            acquire(b)
                            pe.matmul(B[:, b, 0:HALF], sel[0:8, i, :], rows[0:8, h * HALF:(h + 1) * HALF],
                                      start=True, stop=True).then_inc(full[b], 1)

                def operands(c):
                    if c < NCH:
                        return P, [[brt[:, g * H + h, cols(c)] for h in range(H)] for g in range(3)]
                    return SW, [[SMP[:, g * H + h, :] for h in range(H)] for g in range(3)]

                def hcol(bank, w, h, parts=P):
                    return psum(bank)[0:parts, h * w:(h + 1) * w]

                def per_head(bank, product, done=None):
                    acquire(bank)
                    for h in range(H):
                        mm = product(h)
                    mm.then_inc(done or full[bank], 1)

                def turn(bank, tiles, w, done=None):
                    per_head(bank, lambda h: pe.transpose(hcol(bank, P, h, w), tiles[h], ident), done)

                def out_and_state(t, val, b0=0):
                    acquire(b0 + 2)
                    for h in range(H):
                        pe.matmul(hcol(b0 + 2, P, h), ST[:, h, :], t["qg"][:, h, :], start=True, stop=False)
                        mm = pe.matmul(hcol(b0 + 2, P, h), val[:, h, :], t["sc"][:, h, :], start=False, stop=True)
                    mm.then_inc(full[b0 + 2], 1)
                    per_head(b0 + 3, lambda h: pe.matmul(hcol(b0 + 3, P, h), t["kend"][:, h, :], val[:, h, :],
                                                         start=True, stop=True))

                def sample_outputs(delta):
                    t = small
                    k.next(sig("states_landed"), 16 * H)

                    def with_state(bank, h, val, mat, w):
                        o = h * SW
                        pe.matmul(B[:, bank, o:o + SW], val, mat, start=True, stop=False, skip_group_check=True)
                        for b in range(NS):
                            mm = pe.matmul(B[:, bank, o + b * LS:o + (b + 1) * LS], S8[:, h, b, :],
                                           w[:, h, b * LS:(b + 1) * LS], start=False, stop=b == NS - 1,
                                           skip_group_check=True)
                        return mm

                    val = t["v"][0:SW]
                    if delta:
                        both = B[:, 1, 0:2 * H * SW].rearrange("p (u h t) -> p u h t", u=2, h=H)
                        wq = pair_of("w")

                        def u_and_q(h):
                            pe.matmul(both[:, :, h, :], val[:, h, :], pair_of("u")[0:SW, :, h, :], start=True,
                                      stop=False, skip_group_check=True)
                            for b in range(NS):
                                at = slice(b * LS, (b + 1) * LS)
                                mm = pe.matmul(both[:, :, h, at], S8[:, h, b, :], wq[:, :, h, at],
                                               start=False, stop=b == NS - 1, skip_group_check=True)
                            return mm

                        per_head(1, u_and_q)
                        k.next(sig("ut_copied"))
                        per_head(1, lambda h: pe.transpose(B[0:SW, 1, h * P:(h + 1) * P], t["ut"][:, h, :], ident))
                        k.peek(free[1])
                        per_head(2, lambda h: pe.matmul(hcol(2, SW, h), US[:, h, :], t["sc"][0:SW, h, :],
                                                        start=True, stop=True))
                    else:
                        per_head(2, lambda h: with_state(2, h, val[:, h, :], t["sc"][0:SW, h, :], t["qg"]))

                def sample_states(heads):
                    for h in heads:
                        k.next(sig("masked_values" if h < H // 2 else "masked_values_pool"))
                        for half in range(2):
                            acquire(2 + half)
                            pe.matmul(B[:, 2 + half, :], small["kend"][0:SW, h, :], UM[0:SW, h, 4 * half:4 * half + 4, :],
                                      start=True, stop=True).then_inc(full[2 + half], 1)

                def gdn_start(c):
                    w, (q, kk, v) = operands(c)
                    b0 = banks_of(c)
                    turn(b0, kk, w)
                    turn(b0 + 1, v, w)
                    for bank, r in ((b0 + 2, kk), (b0 + 3, q)):
                        per_head(bank, lambda h: pe.matmul(hcol(bank, w, h, w), kk[h], r[h], start=True, stop=True))
                    rows = ROWS if c == NCH else ROW[:, cols(c)]
                    for bank, p0, m in ((b0, 0, P), (b0 + 1, 32, w)):
                        per_head(bank, lambda h: pe.matmul(hcol(bank, w, h, m), sel[p0:p0 + H, h, 0:m],
                                                           rows[p0:p0 + H, :], start=True, stop=True))

                def gdn_level(chunks, lv):
                    last = lv == (S_LEVELS if chunks[0] == NCH else LEVELS) - 1
                    for c in chunks:
                        w, t, b0 = (SW, small, 0) if c == NCH else (P, sets[c % 2], banks_of(c))
                        k.next(sig(f"level_ready_{c % 2}"))
                        if lv > 1:
                            k.peek(free[b0 + 1])
                        al = t["l0" if lv % 2 else "l1"]
                        per_head(b0, lambda h: pe.matmul(hcol(b0, w, h, w), al[0:w, h, :],
                                                         ident[0:w, 0:w] if lv == 1 else t["t"][0:w, h, :],
                                                         start=True, stop=True))
                    for c in chunks:
                        w, t, b0 = (SW, small, 0) if c == NCH else (P, sets[c % 2], banks_of(c))
                        xs = t["x"]
                        uu = [ident[0:w, 0:w] if lv == 1 else t["u"][0:w, h, :] for h in range(H)]
                        k.peek(free[b0])
                        if lv > 1:
                            k.peek(free[b0 + 2])
                        if not last:
                            per_head(b0 + 1, lambda h: pe.matmul(hcol(b0 + 1, w, h, w), uu[h], xs[0:w, h, :],
                                                                 start=True, stop=True))
                        per_head(b0 + 2, lambda h: pe.matmul(hcol(b0 + 2, w, h, w), xs[0:w, h, :], uu[h],
                                                             start=True, stop=True))

                def gdn_w(c):
                    w, t, b0 = (SW, small, 0) if c == NCH else (P, sets[c % 2], banks_of(c))
                    k.peek(free[b0 + 2])
                    per_head(b0, lambda h: pe.matmul(hcol(b0, w, h), t["bgk"][0:w, h, :], t["u"][0:w, h, :],
                                                     start=True, stop=True))

                def gdn_finish(c):
                    t, b0 = (small, 0) if c == NCH else (sets[c % 2], banks_of(c))
                    k.peek(free[b0])
                    k.next(sig("gated_q_ready"))
                    if c == NCH:
                        sample_outputs(True)
                        return
                    acquire(b0 + 1)
                    for h in range(H):
                        pe.matmul(hcol(b0 + 1, P, h), t["u"][:, h, :], t["v"][:, h, :], start=True, stop=False)
                        mm = pe.matmul(hcol(b0 + 1, P, h), t["w"][:, h, :], ST[:, h, :], start=False, stop=True)
                    mm.then_inc(full[b0 + 1], 1)
                    k.peek(free[b0 + 1])
                    out_and_state(t, t["uv"], b0)

                def in_turn(start, finish, chunks):
                    for c in chunks:
                        finish(c)
                        if c + 2 <= NCH:
                            start(c + 2)

                def gdn():
                    for c in CHUNKS[0]:
                        gdn_start(c)
                    for chunks in CHUNKS:
                        for lv in range(1, S_LEVELS if chunks[0] == NCH else LEVELS):
                            gdn_level(chunks, lv)
                        for c in chunks:
                            gdn_w(c)
                        in_turn(gdn_start, gdn_finish, chunks)

                def ret_start(c):
                    w, (q, kk, v) = operands(c)
                    b0 = banks_of(c)
                    turn(b0, kk, w)
                    turn(b0 + 1, v, w)
                    per_head(b0 + 3, lambda h: pe.matmul(hcol(b0 + 3, w, h, w), kk[h], q[h], start=True, stop=True))

                def ret_finish(c):
                    k.next(sig("chunk_ready"))
                    if c == NCH:
                        sample_outputs(False)
                    else:
                        out_and_state(rsets[c % 2], rsets[c % 2]["v"], banks_of(c))

                def ret():
                    for c in CHUNKS[0]:
                        ret_start(c)
                    for chunks in CHUNKS:
                        in_turn(ret_start, ret_finish, chunks)

                def hg_chunk(c):
                    w, (q, kk, v) = operands(c)
                    t = small if c == NCH else hgb
                    levels = S_LEVELS if c == NCH else LEVELS
                    k.next(sig("kend_ready"))
                    turn(0, [t["ked"][:, h, :] for h in range(H)], w, sig("keys_turned"))
                    turn(1, v, w, sig("values_turned"))
                    k.next(sig("levels_ready"))
                    for h in range(H):
                        for lv in range(levels):
                            if h == 0 and lv == POOL_LEVELS[0] - 1:
                                k.next(sig("levels_ready_pool"), 2 * len(POOL_LEVELS))
                            bank = 4 * (h % 2) + 2 + lv // 4
                            if lv % 4 == 0:
                                acquire(bank)
                            a, b = (kk[h], q[h]) if lv == 0 else (t["xl"][:, lv - 1, h, :],) * 2
                            mm = pe.matmul(hcol(bank, P, lv % 4, w)[:, 0:w], a, b, start=True, stop=True)
                            if lv % 4 == 3 or lv == levels - 1:
                                mm.then_inc(full[bank], 1)
                    k.next(sig("chunk_ready"))
                    if c == NCH:
                        sample_outputs(False)
                    else:
                        k.peek(free[3])
                        out_and_state(t, t["v"])

                def hg():
                    for c in range(NCH + 1):
                        hg_chunk(c)

                def out_norm(n):
                    if n == 1:
                        k.next(sig("outputs_ready"))
                        for i in range(H):
                            for h in range(2):
                                b = 2 * (i % 2) + h
                                acquire(b)
                                pe.matmul(B[:, b, 0:HALF], ones, brt[:, i, h * HALF:(h + 1) * HALF],
                                          start=True, stop=True).then_inc(full[b], 1)
                    sample_states(range(H // 2))
                    feature_sums(H, lambda i: hot[:, i, :], 8, sq_o)
                    sample_states(range(H // 2, H))
                    for b in range(4, 8):
                        k.peek(free[b])
                    for j in range(2):
                        merge_gate_part(base[f"merge{n}"] + j, None)
                    spread(RWO, H)

                feature_sums(KD, lambda i: ones, P, sq_m)
                for i in range(2 * KD // ADG):
                    acquire(2 + i % 2)
                    k.next(sig(f"ada_group_landed_{i}"), 16)
                    w = ada_group[i % 3].rearrange("p (k m) -> p k m", k=KD)
                    for kk in range(KD):
                        mm = pe.matmul(B[0:1 + NS, 2 + i % 2, :], CS[:, kk, :], w[:, kk, :], start=kk == 0, stop=kk == KD - 1)
                    mm.then_inc(sig("ada_group_used"), 1)
                acquire(2)
                k.peek(free[3])
                for i in range(2 * KD):
                    mm = pe.transpose(B[:, 2, i * (1 + NS):(i + 1) * (1 + NS)], ADR[:, i * P:(i + 1) * P],
                                      ident[0:1 + NS, 0:1 + NS])
                mm.then_inc(sig("ada_turned"), 1)
                for n in range(3):
                    gemm(n, None, KD, HH, sig("h_ready") if n == 0 else None)
                slab_pairs(pe, "first", 3, 10, lambda n, i, g: gemm(n, g, KD, HH))
                acquire(0)
                acquire(1)
                k.next(sig("square_ready"), 2 * H)
                for i in range(2 * H):
                    for h in range(2):
                        mm = pe.matmul(B[0:8, h, 0:HALF], hot[:, i, :], SQ8[:, i, h * HALF:(h + 1) * HALF],
                                       start=i == 0, stop=i == 2 * H - 1)
                mm.then_inc(sig("l2_sums"), 1)
                slab_pairs(pe, "first", 13, 4, lambda n, i, g: gemm(n, g, KD, HH))
                spread(RW, 2 * H)
                k.next(sig("gate_rows_ready"))
                per_head(0, lambda c: pe.transpose(B[:, 0, c * P:(c + 1) * P], ROW[:, cols(c)], ident))
                acquire(1)
                pe.transpose(B[0:SW, 1, 0:P], ROWS, ident).then_inc(full[1], 1)
                for n, (name, mixer) in enumerate((("first", gdn), ("ret", ret), ("hg", hg))):
                    if n:
                        segment_with_ada(name)
                    k.next(sig("branch_ready"))
                    for j in range(2):
                        buffer(base[f"merge{n}"] + j, None)
                    mixer()
                    out_norm(n)
                    merge_rest(f"merge{n}")
                segment("out", HH, 8, fresh=True)
                acquire(0)
                acquire(1)
                k.next(sig("x_ready"))
                for h in range(2):
                    mm = pe.matmul(B[:, h, 0:HALF], ones, sq_m[0][:, h * HALF:(h + 1) * HALF], start=True, stop=True)
                mm.then_inc(sig("x_sums"), 1)
                for f in range(2):
                    segment(f"gu{f}", HH, 8, fresh=f == 0)
                    k.next(sig("act_ready"))
                    segment(f"dn{f}", AH, KF)

            @block.vector
            def _(dve):
                k = Counts(dve, own["vector"])

                def release(*banks):
                    k.settle()
                    for b in banks:
                        dve.nop().then_inc(free[b], 1)

                def say(name):
                    k.settle()
                    dve.nop().then_inc(sig(name), 1)

                def bc(ap, shape):
                    return ap.broadcast_to(shape)

                def norm():
                    k.next(sig("root_ready"))
                    release(0, 1)
                    k.link(dve.reciprocal(RSTD, RSTD))
                    k.settle()
                    for i in range(KD):
                        k.link(dve.tensor_tensor(TN[:, i, :], X[:, i, :], RSTD, ALU.mult))

                def modulate(shift, scale, gain):
                    k.link(dve.scalar_tensor_tensor(
                        out=SCG[:, :, :], in0=MOD[:, scale:scale + KD, :], scalar=1.0,
                        in1=bc(PR[:, gain:gain + KD].unsqueeze(2), [P, KD, 1 + NS]), op0=ALU.add, op1=ALU.mult))
                    say("modulation_ready")
                    sc, sh = (x.rearrange("p i (a b) -> p i a b", a=2) for x in (SCG[:, :, 1:], MOD[:, shift:shift + KD, 1:]))
                    ys = [YS[:, a].rearrange("p i (b t) -> p i b t", b=4) for a in range(2)]

                    def columns(x, a):
                        return x[:, :, a * HALF + PH:(a + 1) * HALF]

                    def both(op):
                        for a in range(2):
                            k.link(op(a))
                        k.settle()

                    both(lambda a: dve.tensor_tensor(ys[a], columns(TN, a).rearrange("p i (b t) -> p i b t", b=4),
                                                     bc(sc[:, :, a].unsqueeze(3), [P, KD, 4, LS]), ALU.mult))
                    both(lambda a: dve.tensor_tensor(ys[a], ys[a], bc(sh[:, :, a].unsqueeze(3), [P, KD, 4, LS]), ALU.add))
                    both(lambda a: dve.tensor_copy(columns(HH[:, 0], a), YS[:, a]))
                    both(lambda a: dve.tensor_tensor(columns(HH[:, 1], a), YS[:, a], columns(HH[:, 0], a).bitcast(F32),
                                                     ALU.subtract))

                    def whole(i):
                        k.link(dve.tensor_scalar(prompt(YP[i % 2]), prompt(TN[:, i, :]), SCG[:, i, 0:1],
                                                 MOD[:, shift + i, 0:1], ALU.mult, ALU.add))

                    whole(0)
                    for i in range(KD):
                        k.settle()
                        if i + 1 < KD:
                            if i:
                                dve.wait_ge(sig("h_ready"), h_base[0] + i)
                            whole(i + 1)
                        k.next(sig("h_hi"))
                        dve.tensor_tensor(prompt(HH[:, 1, i, :]), prompt(YP[i % 2]), prompt(HH[:, 0, i, :]).bitcast(F32),
                                          ALU.subtract).then_inc(sig("h_ready"), 1)
                    h_base[0] += KD

                h_base = [0]

                def pairs(name, first, count, body, per):
                    n0 = base[name] + first
                    with dve.Fori(0, count // 2) as g:
                        k.begin(g, per)
                        for j in range(2):
                            body(n0 + j, g, j)
                        k.end(count // 2)

                def wait_tile(n, g):
                    dve.wait_ge(tile_done, n + 1 if g is None else n + 1 + 2 * g)

                def gp(n):
                    return GP[:, n % 2 * 2:n % 2 * 2 + 2, 0:HALF]

                def add_gated(name, gate, squares=False):
                    def body(n, g, j):
                        wait_tile(n, g)
                        xi = X[:, 2 * g + j, :]
                        src, tmp = gp(n), SCT[:, :]
                        g4 = GTB[:, 2 * g + j, :].rearrange("p (a b) -> p a b", a=2)
                        k.link(dve.tensor_tensor(tmp.rearrange("p (a b t) -> p a b t", a=2, b=4),
                                                 by_seq(src[:, :, PH:HALF]), bc(g4.unsqueeze(3), [P, 2, 4, LS]), ALU.mult))
                        k.settle()
                        k.link(dve.tensor_tensor(sample(xi), sample(xi), tmp.rearrange("p (a b) -> p a b", a=2), ALU.add))
                        k.link(dve.scalar_tensor_tensor(
                            out=prompt(xi), in0=src[:, :, 0:PH], scalar=GTP[:, bass.ds(2 * g + j, 1)],
                            in1=prompt(xi), op0=ALU.mult, op1=ALU.add))
                        k.settle()
                        dve.nop().then_inc(buf_free[n % 2], 1)
                        if squares:
                            k.link(dve.tensor_tensor(sq_m[1], xi, xi, ALU.mult))
                            k.settle()
                            k.link(dve.tensor_tensor(sq_m[0], sq_m[0], sq_m[1], ALU.add))
                            k.settle()
                    if squares:
                        k.link(dve.memset(sq_m[0], 0.0))
                    k.link(dve.tensor_copy(GTB[:, :, :], MOD[:, gate:gate + KD, 1:]))
                    k.link(dve.tensor_copy(GTP[:, :], MOD[:, gate:gate + KD, 0]))
                    k.settle()
                    pairs(name, 0, 8, body, {own["vector"]: 10 if squares else 6})

                for b in range(8):
                    dve.nop().then_inc(free[b], 1)
                dve.wait_ge(sig("params_landed"), 16)
                k.link(dve.tensor_copy(LBC[:, 0, :], LB[:, l, :]))
                k.settle()
                k.link(dve.tensor_scalar(LBC[:, 1, :], LBC[:, 0, :], -1.0, 1.0, ALU.mult, ALU.add))
                k.next(sig("a_exp"))
                k.link(dve.tensor_scalar(neg_a, neg_a, -1.0, None, ALU.mult))

                def modulation(bank, first):
                    k.link(dve.tensor_tensor(
                        MOD[:, first:first + 2 * KD, :],
                        B[:, bank, 0:2 * KD * (1 + NS)].rearrange("p (i j) -> p i j", j=1 + NS),
                        bc(PR[:, P_BADA + first:P_BADA + first + 2 * KD].unsqueeze(2), [P, 2 * KD, 1 + NS]), ALU.add))
                    release(bank)

                norm()
                k.next(sig("ada_turned"))
                modulation(2, 0)
                for i in range(2):
                    k.link(dve.memset(XP[i][:, 0:3], 0.0))
                modulate(0, KD, P_NMIX)

                wait_tile(0, None)
                dve.tensor_copy(halves(ABROW), GP[0:64, 0:2, 0:HALF]).then_inc(buf_free[0], 1)
                dve.wait_ge(sig("conv_landed"), 16)

                def conv(n, g, j):
                    i = n - 1 if g is None else 2 * g + (n - 1)
                    xp = XP[n % 2]
                    xs = xp[:, 3 + SEQ:].rearrange("p (b t) -> p b t", b=NS)
                    cs = CSMP[n % 2].rearrange("p (b t) -> p b t", b=NS)
                    wait_tile(n, g)
                    k.link(dve.tensor_copy(halves(xp[:, 3:3 + SEQ]), gp(n)[:, :, 0:PH]))
                    dve.tensor_copy(xs[:, :, 3:].rearrange("p (a b) t -> p a b t", a=2),
                                    by_seq(gp(n)[:, :, PH:HALF])).then_inc(buf_free[n % 2], 1)
                    c0 = CONV0[:, i, :].rearrange("p (b t) -> p b t", b=NS)
                    k.link(dve.tensor_copy(xs[:, :, 0:3], c0))
                    k.settle()
                    c1 = CONV1[:, i, :]
                    k.link(dve.tensor_copy(c1[:, 0:3], xp[:, SEQ:SEQ + 3]))
                    k.link(dve.tensor_copy(c1[:, 3:].rearrange("p (b t) -> p b t", b=NS), xs[:, :, 4:7]))
                    k.next(sig("conv_slot_free"))
                    out = prompt(brt[:, i, :])
                    for tap in range(CONV_W):
                        wt = PR[:, bass.ds(i * CONV_W + tap, 1)]
                        xin = halves(xp[:, tap:tap + SEQ])
                        if tap == 0:
                            k.link(dve.tensor_scalar(out, xin, wt, None, ALU.mult))
                            k.link(dve.tensor_scalar(cs, xs[:, :, 0:LS], wt, None, ALU.mult))
                            k.settle()
                            continue
                        k.link(dve.scalar_tensor_tensor(out=out, in0=xin, scalar=wt, in1=out, op0=ALU.mult, op1=ALU.add))
                        ins = dve.scalar_tensor_tensor(out=cs, in0=xs[:, :, tap:tap + LS], scalar=wt, in1=cs,
                                                       op0=ALU.mult, op1=ALU.add)
                        if tap < CONV_W - 1:
                            k.link(ins)
                            k.settle()
                        else:
                            ins.then_inc(sig("conv_done"), 1)
                            k.settle()

                for n in (1, 2):
                    conv(n, None, n - 1)
                pairs("first", 3, 10, conv, {own["vector"]: 2 * 11, sig("conv_slot_free"): 2})
                say("conv_saved")

                def rows_of(rw, scale_q):
                    k.next(sig("root_ready"))
                    release(0, 1)
                    k.link(dve.reciprocal(rw[0:8, :], rw[0:8, :]))
                    if scale_q:
                        k.settle()
                        k.link(dve.tensor_scalar(rw[0:H, :], rw[0:H, :], float(P) ** -0.5, None, ALU.mult))
                    say("rows_ready")

                def bank_pair(i):
                    b = 2 * (i % 2)
                    k.next(full[b])
                    k.next(full[b + 1])
                    return B[:, b:b + 2, 0:HALF], b

                a1, a2 = wide[1][0:H, :], wide[2][0:H, :]
                k.next(sig("conv_slot_free"), 2)
                k.link(dve.memset(ROW, 0.0))
                k.link(dve.memset(COL[:, NCH, :], 0.0))
                k.link(dve.tensor_scalar(a1, ABROW[0:H, :], PR[0:H, P_DT:P_DT + 1], None, ALU.add))
                k.settle()
                k.link(dve.tensor_scalar(a2, a1, -1.0, None, ALU.mult))
                k.settle()
                k.link(dve.tensor_tensor(a2, a1, a2, ALU.min))
                say("gate_args")
                k.next(sig("gate_logs"))
                k.link(dve.scalar_tensor_tensor(out=a1, in0=a1, scalar=0.0, in1=a2, op0=ALU.max, op1=ALU.add))
                k.settle()
                k.link(dve.tensor_scalar(a1, a1, neg_a, None, ALU.mult))
                k.settle()
                k.link(dve.tensor_tensor_scan(ROW[0:H, :], reset[0:H, :], a1, 0.0, ALU.mult, ALU.add))
                k.settle()
                k.link(dve.tensor_copy(ROW[32:32 + H, :], wide[3][32:32 + H, :]))
                g4 = prompt(ROW[0:H, :]).rearrange("p a (c t) -> p a c t", c=2)
                e4 = prompt(ROW[64:64 + H, :]).rearrange("p a (c t) -> p a c t", c=2)
                k.link(dve.tensor_tensor(e4, bc(g4[:, :, :, P - 1:P], [H, 2, 2, P]), g4, ALU.subtract))
                g4, e4 = by_seq(sample(ROW[0:H, :])), by_seq(sample(ROW[64:64 + H, :]))
                k.link(dve.tensor_tensor(e4, bc(g4[:, :, :, LS - 1:LS], [H, 2, 4, LS]), g4, ALU.subtract))
                k.settle()
                k.link(dve.tensor_copy(halves(ROWS), sample(ROW)))
                say("gate_rows_ready")
                rows_of(RW, True)
                for i in range(2 * H):
                    src, b = bank_pair(i)
                    k.link(dve.tensor_tensor(halves(brt[:, i, :]), src, halves(brt[:, i, :]), ALU.mult))
                    release(b, b + 1)
                k.next(full[0])
                k.link(dve.tensor_copy(COL[:, 0:NCH, :], B[:, 0, :].rearrange("p (c j) -> p c j", c=NCH)[:, :, 0:96]))
                release(0)
                k.next(full[1])
                k.link(dve.tensor_copy(COL[0:SW, NCH, :], B[0:SW, 1, 0:96]))
                release(1)
                say("gate_cols")
                k.next(sig("gate_exps"))
                k.link(dve.tensor_tensor(CE[:, :, 8:12], CE[:, :, 0:4], COL[:, :, 32:36], ALU.mult))

                def start_branch(tiles):
                    for i in range(0, tiles, H):
                        src = 16 if i == 12 else i
                        k.settle()
                        k.link(dve.tensor_copy(SMP[:, i:i + H, :].rearrange("p i (a b) -> p i a b", a=2),
                                               brt[:, src:src + H, :].rearrange("p i (a b) -> p i a b", a=2)[:, :, :, PH:]))
                    k.link(dve.memset(ST[:, :, :], 0.0))
                    say("branch_ready")

                def bank4(b, w=P, parts=P, inner=P):
                    return psum(b)[0:parts, 0:H * w].rearrange("p (h t) -> p h t", h=H)[:, :, 0:inner]

                def by_token(col, parts, w=P):
                    return bc(col.unsqueeze(2), [parts, H, w])

                def finish_chunk(decay, c, b0=0):
                    k.next(full[b0 + 2])
                    k.link(dve.tensor_copy(brt[:, 0:H, cols(c)], bank4(b0 + 2)))
                    release(b0 + 2)
                    k.next(full[b0 + 3])
                    for h in range(H):
                        k.link(dve.scalar_tensor_tensor(out=ST[:, h, :], in0=ST[:, h, :], scalar=decay(h),
                                                        in1=bank4(b0 + 3)[:, h, :], op0=ALU.mult, op1=ALU.add))
                    release(b0 + 3)
                    if c == NCH - 1:
                        dve.nop().then_inc(sig("prompt_state_done"), 1)

                def sample_outputs(delta):
                    val = small["v"][0:SW]
                    if delta:
                        k.next(full[1], 2)
                        k.link(dve.tensor_copy(US, bank4(1, P, SW)))
                        release(1)
                        val = US
                    say("values_ready")
                    for h in range(H // 2):
                        k.link(dve.tensor_tensor(UM[0:SW, h], bc(val[:, h].unsqueeze(1), [SW, NS, P]), seqs, ALU.mult))
                        say("masked_values")
                    k.next(full[2])
                    out = brt[:, 0:H, :].rearrange("p i (a b) -> p i a b", a=2)[:, :, :, PH:]
                    o_t = B[:, 2, 0:H * SW].rearrange("p (i a b) -> p i a b", i=H, a=2)
                    if delta:
                        k.link(dve.tensor_tensor(out, o_t, small["oq"].rearrange("p i (a b) -> p i a b", a=2), ALU.add))
                    else:
                        k.link(dve.tensor_copy(out, o_t))
                    release(2)

                def sample_states(eg):
                    k.next(sig("states_landed"), 16 * H)
                    for h in range(H):
                        for half, bank in enumerate((2, 3)):
                            k.next(full[bank])
                            for b in range(4 * half, 4 * half + 4):
                                k.link(dve.scalar_tensor_tensor(
                                    out=S8[:, h, b, :], in0=S8[:, h, b, :], scalar=eg[:, h, b * LS + LS - 1:b * LS + LS],
                                    in1=B[:, bank, b % 4 * P:(b % 4 + 1) * P], op0=ALU.mult, op1=ALU.add))
                            release(bank)
                        say("sample_state_done")

                def gdn_start(c):
                    sm = c == NCH
                    w, t, b0 = (SW, small, 0) if sm else (P, sets[c % 2], banks_of(c))
                    q = SMP[:, 0:H, :] if sm else brt[:, 0:H, cols(c)]
                    incl = C[0:w, C_INCLS:C_INCLS + SW] if sm else C[:, C_INCL:C_INCL + P]
                    k.next(full[b0])
                    k.link(dve.tensor_tensor(t["bgk"][0:w], bank4(b0, P, w), by_token(CE[0:w, c, 8:12], w), ALU.mult))
                    k.link(dve.tensor_tensor(t["kend"][0:w], bank4(b0, P, w), by_token(CE[0:w, c, 4:8], w), ALU.mult))
                    release(b0)
                    k.next(full[b0 + 1])
                    k.link(dve.tensor_tensor(t["v"][0:w], bank4(b0 + 1, P, w), by_token(COL[0:w, c, 32:36], w), ALU.mult))
                    release(b0 + 1)
                    k.next(sig("eg_ready"))
                    k.next(full[b0])
                    k.link(dve.tensor_tensor(t["dt"][0:w], bank4(b0, w, w, w), by_token(COL[0:w, c, 0:4], w, w), ALU.subtract))
                    release(b0)
                    k.link(dve.tensor_scalar(t["dt"][0:w], t["dt"][0:w], 0.0, None, ALU.min))
                    say("decay_args")
                    if not sm:
                        k.link(dve.tensor_copy(EGE[:, c % 2, :], t["eg"][:, :, P - 1]))
                        k.settle()
                    k.link(dve.tensor_tensor(t["qg"], q, t["eg"], ALU.mult))
                    say("gated_q_ready")
                    k.next(sig("decay_ready"))
                    k.link(dve.tensor_tensor(t["dt"][0:w], t["dt"][0:w], bc(incl.unsqueeze(1), [w, H, w]), ALU.mult))
                    k.settle()
                    k.next(full[b0 + 2])
                    k.link(dve.tensor_tensor(t["a"][0:w], bank4(b0 + 2, w, w, w), t["dt"][0:w], ALU.mult))
                    release(b0 + 2)
                    k.next(full[b0 + 1])
                    k.link(dve.tensor_tensor(t["a"][0:w], bank4(b0 + 1, w, w, w), t["a"][0:w], ALU.mult))
                    release(b0 + 1)
                    k.next(full[b0 + 3])
                    k.link(dve.tensor_tensor(t["sc"][0:w], bank4(b0 + 3, w, w, w), t["dt"][0:w], ALU.mult))
                    release(b0 + 3)
                    if sm:
                        k.link(dve.memset(t["zero"], 0.0))
                    level_mask(c, 1)

                def level_mask(c, lv):
                    w, t = (SW, small) if c == NCH else (P, sets[c % 2])
                    m = bc(mask[0:w, lv, 0:w].unsqueeze(1), [w, H, w])
                    k.link(dve.tensor_tensor(t["l0" if lv % 2 else "l1"][0:w], t["a"][0:w], m, ALU.mult))
                    say(f"level_ready_{c % 2}")

                def gdn_level(c, lv):
                    w, t, b0 = (SW, small, 0) if c == NCH else (P, sets[c % 2], banks_of(c))
                    levels = S_LEVELS if c == NCH else LEVELS
                    if lv + 1 < levels:
                        level_mask(c, lv + 1)
                    for bank, name in ((1, "t"), (2, "u")):
                        if bank == 1 and lv == levels - 1:
                            continue
                        k.next(full[b0 + bank])
                        old = bc(ident[0:w, 0:w].unsqueeze(1), [w, H, w]) if lv == 1 else t[name][0:w]
                        k.link(dve.tensor_tensor(t[name][0:w], old, bank4(b0 + bank, w, w, w), ALU.subtract))
                        release(b0 + bank)

                def in_turn(start, finish, chunks):
                    for c in chunks:
                        finish(c)
                        if c + 2 <= NCH:
                            start(c + 2)

                def gdn_finish(c):
                    b0 = banks_of(c)
                    k.skip(full[b0], S_LEVELS if c == NCH else LEVELS)
                    if c == NCH:
                        sample_outputs(True)
                    else:
                        k.skip(full[b0 + 1])
                        finish_chunk(lambda h: EGE[:, c % 2, h:h + 1], c, b0)

                def gdn():
                    for c in CHUNKS[0]:
                        gdn_start(c)
                    for chunks in CHUNKS:
                        for lv in range(1, S_LEVELS if chunks[0] == NCH else LEVELS):
                            for c in chunks:
                                gdn_level(c, lv)
                        in_turn(gdn_start, gdn_finish, chunks)

                def ret_tables(c):
                    sm = c == NCH
                    w = SW if sm else P
                    dec, inner = (C[:, o:o + H * w].rearrange("p (h t) -> p h t", h=H)
                                  for o in ((C_DRETS, C_IRETS) if sm else (C_DRET, C_IRET)))
                    return dec, inner, C[0:w, C_ENDS:C_ENDS + H] if sm else C[:, C_END:C_END + H]

                def ret_start(c):
                    sm = c == NCH
                    w, t, b0 = (SW, small, 0) if sm else (P, rsets[c % 2], banks_of(c))
                    q = SMP[:, 0:H, :] if sm else brt[:, 0:H, cols(c)]
                    dec, inner, ends = ret_tables(c)
                    k.next(full[b0])
                    k.link(dve.tensor_tensor(t["kend"][0:w], bank4(b0, P, w), by_token(ends, w), ALU.mult))
                    release(b0)
                    k.next(full[b0 + 1])
                    k.link(dve.tensor_copy(t["v"][0:w], bank4(b0 + 1, P, w)))
                    release(b0 + 1)
                    k.link(dve.tensor_tensor(t["qg"], q, inner, ALU.mult))
                    k.next(full[b0 + 3])
                    k.link(dve.tensor_tensor(t["sc"][0:w], bank4(b0 + 3, w, w, w), dec[0:w], ALU.mult))
                    release(b0 + 3)
                    say("chunk_ready")

                def ret_finish(c):
                    if c == NCH:
                        sample_outputs(False)
                    else:
                        finish_chunk(lambda h: ret_tables(c)[1][:, h, P - 1:P], c, banks_of(c))

                def ret():
                    for c in CHUNKS[0]:
                        ret_start(c)
                    for chunks in CHUNKS:
                        in_turn(ret_start, ret_finish, chunks)

                def hg_args(c):
                    sm = c == NCH
                    w, t = (SW, small) if sm else (P, hgb)
                    acc = SMP[:, 12:16, :] if sm else brt[:, 16:20, cols(c)]
                    levels = S_LEVELS if sm else LEVELS
                    if not sm:
                        say("xl_free")
                    blk = LS if sm else P
                    nb = w // blk
                    a4, d4 = (x.rearrange("p h (n t) -> p h n t", n=nb) for x in (acc, t["ked"]))
                    if nb == 1:
                        k.link(dve.tensor_tensor(t["ked"], bc(acc[:, :, P - 1:P], [P, H, P]), acc, ALU.subtract))
                    else:
                        k.link(dve.tensor_tensor(d4, bc(a4[:, :, :, blk - 1:blk], [P, H, nb, blk]), a4, ALU.subtract))
                    say("kend_args")
                    for lv in range(1, levels if sm else POOL_LEVELS[0]):
                        m = 1 << (lv - 1)
                        a5, x5 = (x.rearrange("p h (n u t) -> p h n u t", u=2, t=m) for x in (acc, t["xl"][:, lv - 1]))
                        mid = bc(a5[:, :, :, 0, m - 1:m], [P, H, w // (2 * m), m])
                        k.link(dve.tensor_tensor(x5[:, :, :, 0, :], mid, a5[:, :, :, 0, :], ALU.subtract))
                        k.link(dve.tensor_tensor(x5[:, :, :, 1, :], a5[:, :, :, 1, :], mid, ALU.subtract))
                    say("level_args")

                def hg(c):
                    sm = c == NCH
                    w, t = (SW, small) if sm else (P, hgb)
                    q, kk = ((SMP[:, i:i + H, :] for i in (0, 4)) if sm else
                             (brt[:, i:i + H, cols(c)] for i in (0, 4)))
                    levels = S_LEVELS if sm else LEVELS
                    k.next(sig("kend_exps"))
                    if not sm:
                        k.link(dve.tensor_copy(EGE[:, 0, :], t["eg"][:, :, P - 1]))
                    k.link(dve.tensor_tensor(t["ked"], t["ked"], kk, ALU.mult))
                    say("kend_ready")
                    k.link(dve.tensor_tensor(t["qg"], q, t["eg"], ALU.mult))
                    k.next(sig("level_exps"))
                    for lv in range(1, levels if sm else POOL_LEVELS[0]):
                        m = 1 << (lv - 1)
                        q5, k5, x5 = (x.rearrange("p h (n u t) -> p h n u t", u=2, t=m) for x in (q, kk, t["xl"][:, lv - 1]))
                        k.link(dve.tensor_tensor(x5[:, :, :, 0, :], x5[:, :, :, 0, :], k5[:, :, :, 0, :], ALU.mult))
                        k.link(dve.tensor_tensor(x5[:, :, :, 1, :], x5[:, :, :, 1, :], q5[:, :, :, 1, :], ALU.mult))
                    say("levels_ready")
                    prod = t["prod"]
                    for h in range(H):
                        for b in range((levels + 3) // 4):
                            n = min(4, levels - 4 * b)
                            bank = 4 * (h % 2) + 2 + b
                            k.next(full[bank])
                            k.link(dve.tensor_tensor(
                                prod[0:w, 4 * b:4 * b + n, 0:w],
                                psum(bank)[0:w].rearrange("p (l t) -> p l t", l=4)[:, 0:n, 0:w],
                                mask[0:w, 4 * b:4 * b + n, 0:w], ALU.mult))
                            release(bank)
                        k.link(dve.tensor_reduce(t["sc"][0:w, h, :], prod[0:w].rearrange("p l t -> p t l"), AX.X, ALU.add))
                        k.settle()
                    k.next(sig("kv_copied"))
                    say("chunk_ready")
                    if sm:
                        sample_outputs(False)
                    else:
                        hg_args(c + 1)
                        finish_chunk(lambda h: EGE[:, 0, h:h + 1], c)

                def out_norm(n):
                    k.settle()
                    if n == 1:
                        say("outputs_ready")
                        for i in range(H):
                            src, b = bank_pair(i)
                            o = halves(brt[:, i, :])
                            k.link(dve.scalar_tensor_tensor(out=o, in0=src, scalar=-1.0 / P, in1=o, op0=ALU.mult, op1=ALU.add))
                            release(b, b + 1)
                    say("outputs_final")
                    for i in range(H):
                        k.link(dve.tensor_tensor(brt[:, 12 + i, :], brt[:, 12 + i, :], brt[:, i, :], ALU.mult))
                    sample_states(ret_tables(NCH)[1] if n == 1 else small["eg"])
                    rows_of(RWO, False)
                    gain = {0: PR[:, P_GNORM:P_GNORM + 1], 1: 1.0, 2: PR[:, P_HNORM:P_HNORM + 1]}[n]

                    def value(i):
                        src, b = bank_pair(i)
                        k.link(dve.scalar_tensor_tensor(out=halves(VALS[i % 2]), in0=src, scalar=gain,
                                                        in1=halves(brt[:, 12 + i, :]), op0=ALU.mult, op1=ALU.mult))
                        release(b, b + 1)
                        dve.nop().then_inc(sig("o_value"), 1)

                    value(0)
                    for i in range(H):
                        if i + 1 < H:
                            if i:
                                dve.wait_ge(sig("o_ready"), H * n + i)
                            value(i + 1)
                        k.next(sig("o_hi"))
                        dve.tensor_tensor(OH[:, 1, i, :], VALS[i % 2], OH[:, 0, i, :].bitcast(F32), ALU.subtract
                                          ).then_inc(sig("o_ready"), 1)
                    dve.wait_ge(sig("o_ready"), H * (n + 1))

                def merge(n):
                    def body(s, g, j):
                        if j == 0:
                            k.next(sig("merge_gate"))
                            dve.nop().then_inc(buf_free[s % 2], 1)
                            return
                        wait_tile(s, g)
                        dst = MG[:, g, :] if n == 0 else VAL
                        k.link(dve.tensor_tensor(halves(dst), gp(s), halves(SG), ALU.mult))
                        k.settle()
                        dve.nop().then_inc(buf_free[s % 2], 1)
                        dve.nop().then_inc(sig("merge_slot_free"), 1)
                        if n:
                            k.link(dve.tensor_tensor(MG[:, g, :], MG[:, g, :], VAL, ALU.add))
                            k.settle()
                    pairs(f"merge{n}", 0, 16, body, {own["vector"]: 2 if n else 1, sig("merge_gate"): 1})

                def copy_tiles(name, first, count, dst):
                    def body(n, g, j):
                        wait_tile(n, g)
                        dve.tensor_copy(halves(brt[:, 2 * g + j + dst, :]), gp(n)).then_inc(buf_free[n % 2], 1)
                    pairs(name, first, count, body, {})

                def rope(n, g, j):
                    k.next(sig("swapped"))
                    out = brt[:, 2 * g + j, :]
                    dve.tensor_tensor(halves(out), gp(n), halves(C[:, C_COS:C_SIN]), ALU.mult).then_inc(buf_free[n % 2], 1)
                    k.link(dve.tensor_tensor(wide[j], wide[j], C[:, C_SIN:C_DRET], ALU.mult))
                    k.settle()
                    k.link(dve.tensor_tensor(out, out, wide[j], ALU.add))
                    say("rope_slot_free")

                def forget(n, g, j):
                    k.next(sig("sigmoids"))
                    dve.nop().then_inc(buf_free[n % 2], 1)
                    i = 2 * g + j
                    f, kk = brt[:, i + 16, :], brt[:, i + 4, :]
                    k.link(dve.scalar_tensor_tensor(out=f, in0=kk, scalar=LBC[:, 0, bass.ds(i, 1)], in1=f,
                                                    op0=ALU.mult, op1=ALU.add))
                    k.settle()
                    k.link(dve.tensor_scalar(kk, kk, LBC[:, 1, bass.ds(i, 1)], None, ALU.mult))

                start_branch(12)
                gdn()
                out_norm(0)
                dve.nop().then_inc(sig("merge_slot_free"), 1)
                merge(0)

                for j in range(2):
                    dve.nop().then_inc(sig(f"ada_slot_{j}_free"), 1)
                dve.nop().then_inc(sig("rope_slot_free"), 2)
                pairs("ret", 0, 8, rope, {own["vector"]: 4, sig("swapped"): 2})
                copy_tiles("ret", 8, 4, 8)
                k.next(full[0])
                modulation(0, 2 * KD)
                k.next(sig("gates_in"))
                dve.wait_ge(sig("stored_prompt"), 16)
                start_branch(12)
                ret()
                out_norm(1)
                merge(1)

                for j in range(2):
                    dve.nop().then_inc(sig(f"ada_slot_{j}_free"), 1)
                copy_tiles("hg", 0, 4, 0)
                pairs("hg", 4, 4, forget, {own["vector"]: 4, sig("sigmoids"): 2})
                f4 = BR[:, 16 * T:20 * T]
                k.settle()
                k.link(dve.tensor_scalar(LN1, f4, LN_CUT, None, ALU.max))
                k.link(dve.tensor_scalar(LN2, f4, F_TINY, LN_CUT, ALU.max, ALU.min))
                say("log_args")
                copy_tiles("hg", 8, 4, 8)
                k.next(sig("logs"))
                k.link(dve.tensor_tensor(LN1, LN1, LN2, ALU.add))
                k.settle()
                for h in range(H):
                    k.link(dve.tensor_tensor_scan(brt[:, 16 + h, :], reset, LN1[:, h * T:(h + 1) * T], 0.0,
                                                  ALU.mult, ALU.add))
                k.next(full[0])
                modulation(0, 4 * KD)
                k.next(sig("gates_in"))
                dve.wait_ge(sig("stored_prompt"), 32)
                start_branch(16)
                hg_args(0)
                for c in range(NCH + 1):
                    hg(c)
                out_norm(2)
                merge(2)

                dve.wait_ge(tile_done, base["out"])
                for i in range(KD):
                    k.link(dve.tensor_copy(HH[:, 0, i, :], MG[:, i, :]))
                k.settle()
                for i in range(KD):
                    dve.tensor_tensor(HH[:, 1, i, :], MG[:, i, :], HH[:, 0, i, :].bitcast(F32), ALU.subtract
                                      ).then_inc(sig("h_ready"), 1)
                h_base[0] += KD
                dve.wait_ge(sig("x_back"), 16)
                add_gated("out", 2 * KD, squares=True)
                say("x_ready")

                dve.wait_ge(tile_done, base["gu0"])
                norm()
                modulate(3 * KD, 4 * KD, P_NFFN)
                dve.nop().then_inc(sig("ffn_slot_free"), 1)
                for f in range(2):
                    def act_tile(s, g, j):
                        if j == 0:
                            k.next(sig("ffn_gate"))
                            dve.nop().then_inc(buf_free[s % 2], 1)
                            return
                        wait_tile(s, g)
                        k.link(dve.tensor_tensor(halves(FT[:, 1, :]), gp(s), halves(FT[:, 0, :]), ALU.mult))
                        k.settle()
                        dve.nop().then_inc(buf_free[s % 2], 1)
                        dve.nop().then_inc(sig("ffn_slot_free"), 1)
                        k.link(dve.tensor_copy(AH[:, 0, g, :], FT[:, 1, :]))
                        k.settle()
                        k.link(dve.tensor_tensor(AH[:, 1, g, :], FT[:, 1, :], AH[:, 0, g, :].bitcast(F32), ALU.subtract))
                        k.settle()
                    pairs(f"gu{f}", 0, 22, act_tile, {own["vector"]: 3, sig("ffn_gate"): 1})
                    say("act_ready")
                    add_gated(f"dn{f}", 5 * KD)

            @block.scalar
            def _(act):
                k = Counts(act, own["scalar"])

                def f(out, in_, func, **kw):
                    return act.activation(out, in_, func, **kw)

                def pairs(name, first, count, body, per):
                    n0 = base[name] + first
                    with act.Fori(0, count // 2) as g:
                        k.begin(g, per)
                        for j in range(2):
                            body(n0 + j, g, j)
                        k.end(count // 2)

                def wait_tile(n, g):
                    act.wait_ge(tile_done, n + 1 if g is None else n + 1 + 2 * g)

                def gp(n, p0=0, p1=P):
                    return GP[p0:p1, n % 2 * 2:n % 2 * 2 + 2, 0:HALF]

                def squares(tiles, sq, rows, out, scale):
                    for i, tile in enumerate(tiles):
                        k.next(sig("square_slot_free"))
                        f(sq[i % 2], tile, ACT.Square).then_inc(sig("square_ready"), 1)
                    k.peek(sig("square_slot_free"), 2)
                    f(halves(out[0:rows, :]), B[0:rows, 0:2, 0:HALF], ACT.Sqrt, scale=scale, bias=epsc[0:rows, :]
                      ).then_inc(sig("root_ready"), 1)

                def high_parts(shift):
                    k.next(sig("modulation_ready"))
                    for i in range(KD):
                        f(prompt(HH[:, 0, i, :]), prompt(TN[:, i, :]), ACT.Identity, scale=SCG[:, i, 0:1],
                          bias=MOD[:, shift + i, 0:1]).then_inc(sig("h_hi"), 1)

                act.wait_ge(sig("params_landed"), 16)
                f(neg_a, PR[0:H, P_ALOG:P_ALOG + 1], ACT.Exp).then_inc(sig("a_exp"), 1)
                squares([X[:, i, :] for i in range(KD)], sq_m, P, RSTD, 1.0 / D)
                for i in range(2 * KD // ADG):
                    k.next(sig("ada_group_used"))
                    f(ADR[:, i * 4 * P:(i + 1) * 4 * P], B[0:1 + NS, 2 + i % 2, :], ACT.Copy).then_inc(free[2 + i % 2], 1)
                high_parts(0)

                act.nop().then_inc(sig("conv_slot_free"), 2)

                def conv(n, g, j):
                    i = n - 1 if g is None else 2 * g + (n - 1)
                    k.next(sig("conv_done"))
                    tile = brt[:, i, :]
                    k.link(f(prompt(tile), prompt(tile), ACT.Silu))
                    k.link(f(sample(tile), halves(CSMP[n % 2]), ACT.Silu))
                    k.settle()
                    act.nop().then_inc(sig("conv_slot_free"), 1)
                    return tile, i

                def conv_square(n, g, j):
                    tile, i = conv(n, g, j)
                    f(SQ8[:, i, :], tile, ACT.Square).then_inc(sig("square_ready"), 1)

                for n in (1, 2):
                    conv_square(n, None, n - 1)
                pairs("first", 3, 6, conv_square, {own["scalar"]: 4, sig("conv_done"): 2})
                pairs("first", 9, 4, conv, {own["scalar"]: 4, sig("conv_done"): 2})

                def gate_tiles(name, first, func):
                    def body(n, g, j):
                        wait_tile(n, g)
                        k.link(f(halves(brt[:, 2 * g + j + 12, :]), gp(n), func))
                        k.settle()
                        act.nop().then_inc(buf_free[n % 2], 1)
                    pairs(name, first, 4, body, {own["scalar"]: 2})

                a2 = wide[2][0:H, :]
                k.next(sig("gate_args"))
                k.link(f(a2, a2, ACT.Exp))
                k.settle()
                k.link(f(a2, a2, ACT.Ln, bias=onec[0:H, :]))
                k.settle()
                f(wide[3][32:32 + H, :], ABROW[32:32 + H, :], ACT.Sigmoid).then_inc(sig("gate_logs"), 1)
                k.next(sig("l2_sums"))
                f(halves(RW[0:8, :]), B[0:8, 0:2, 0:HALF], ACT.Sqrt, bias=epsc[0:8, :]).then_inc(sig("root_ready"), 1)
                gate_tiles("first", 13, ACT.Silu)
                k.next(sig("gate_cols"))
                k.link(f(CE[:, :, 0:4], COL[:, :, 0:4], ACT.Exp))
                f(CE[:, :, 4:8], COL[:, :, 64:68], ACT.Exp).then_inc(sig("gate_exps"), 1)

                def bank4(b, w=P, parts=P, inner=P):
                    return psum(b)[0:parts, 0:H * w].rearrange("p (h t) -> p h t", h=H)[:, :, 0:inner]

                fills = {b: 0 for b in range(8)}

                def filled(b, n=1):
                    fills[b] += n
                    act.wait_ge(full[b], fills[b])

                def skip(b, n=1):
                    fills[b] += n

                for b in range(4):
                    skip(b, H)
                skip(0)
                skip(1)

                def gdn_start(c):
                    w, t, b0 = (SW, small, 0) if c == NCH else (P, sets[c % 2], banks_of(c))
                    skip(b0)
                    filled(b0)
                    f(t["eg"], bank4(b0, w, P, w), ACT.Exp).then_inc(sig("eg_ready"), 1)
                    k.next(sig("decay_args"))
                    f(t["dt"][0:w], t["dt"][0:w], ACT.Exp).then_inc(sig("decay_ready"), 1)

                for c in CHUNKS[0]:
                    gdn_start(c)
                for chunks in CHUNKS:
                    levels = S_LEVELS if chunks[0] == NCH else LEVELS
                    for lv in range(1, levels + 1):
                        for c in chunks:
                            w, t, b0 = (SW, small, 0) if c == NCH else (P, sets[c % 2], banks_of(c))
                            filled(b0)
                            if lv < levels:
                                f(t["x"][0:w], bank4(b0, w, w, w), ACT.Copy).then_inc(free[b0], 1)
                            else:
                                f(t["w"], bank4(b0, w, P, w), ACT.Copy, scale=-1.0).then_inc(free[b0], 1)
                    for c in chunks:
                        b0 = banks_of(c)
                        skip(b0 + 1, levels)
                        filled(b0 + 1)
                        if c < NCH:
                            f(sets[c % 2]["uv"], bank4(b0 + 1), ACT.Copy).then_inc(free[b0 + 1], 1)
                        else:
                            k.link(f(pair_of("ut"), B[:, 1, 0:2 * H * SW].rearrange("p (u h t) -> p u h t", u=2, h=H),
                                     ACT.Copy))
                            k.settle()
                            act.nop().then_inc(free[1], 1)
                            act.nop().then_inc(sig("ut_copied"), 1)
                        if c + 2 <= NCH:
                            gdn_start(c + 2)

                def out_norm():
                    k.next(sig("outputs_final"))
                    squares([brt[:, i, :] for i in range(H)], sq_o, 8, RWO, 1.0 / P)
                    for i in range(H):
                        k.next(sig("o_value"))
                        f(OH[:, 0, i, :], VALS[i % 2], ACT.Copy).then_inc(sig("o_hi"), 1)

                def merge(n):
                    def body(s, g, j):
                        if j == 0:
                            k.next(sig("merge_slot_free"))
                            k.next(sig("gate_product"))
                            f(halves(SG), gp(s), ACT.Sigmoid).then_inc(sig("merge_gate"), 1)
                    pairs(f"merge{n}", 0, 16, body, {sig("merge_slot_free"): 1, sig("gate_product"): 1})

                out_norm()
                merge(0)

                def swap(n, g, j):
                    k.next(sig("rope_slot_free"))
                    wait_tile(n, g)
                    k.link(f(halves(wide[j][0:64, :]), gp(n, 64, P), ACT.Copy))
                    f(halves(wide[j][64:P, :]), gp(n, 0, 64), ACT.Copy).then_inc(sig("swapped"), 1)

                pairs("ret", 0, 8, swap, {own["scalar"]: 2, sig("rope_slot_free"): 2})
                gate_tiles("ret", 12, ACT.Silu)
                act.nop().then_inc(sig("gates_in"), 1)
                out_norm()
                merge(1)

                def forget(n, g, j):
                    wait_tile(n, g)
                    k.link(f(halves(brt[:, 2 * g + j + 16, :]), gp(n), ACT.Sigmoid))
                    f(halves(brt[:, 2 * g + j + 4, :]), gp(n), ACT.Sigmoid, scale=-1.0).then_inc(sig("sigmoids"), 1)

                pairs("hg", 4, 4, forget, {own["scalar"]: 2})
                k.next(sig("log_args"))
                k.link(f(LN1, LN1, ACT.Ln))
                f(LN2, LN2, ACT.Ln, scale=1.0 / LN_CUT).then_inc(sig("logs"), 1)
                gate_tiles("hg", 12, ACT.Sigmoid)
                act.nop().then_inc(sig("gates_in"), 1)
                for c in range(NCH + 1):
                    t = small if c == NCH else hgb
                    acc = SMP[:, 12:16, :] if c == NCH else brt[:, 16:20, cols(c)]
                    k.next(sig("kend_args"))
                    k.link(f(t["eg"], acc, ACT.Exp))
                    f(t["ked"], t["ked"], ACT.Exp).then_inc(sig("kend_exps"), 1)
                    k.next(sig("level_args"))
                    mine = t["xl"] if c == NCH else t["xl"][:, 0:POOL_LEVELS[0] - 1]
                    f(mine, mine, ACT.Exp).then_inc(sig("level_exps"), 1)
                    if c < NCH:
                        k.next(sig("level_args_pool"), 2 * len(POOL_LEVELS))
                        theirs = t["xl"][:, POOL_LEVELS[0] - 1:]
                        f(theirs, theirs, ACT.Exp).then_inc(sig("level_exps_pool"), 1)
                    w = SW if c == NCH else P
                    k.next(sig("keys_turned"))
                    k.link(f(t["kend"][0:w], bank4(0, P, w), ACT.Copy))
                    k.next(sig("values_turned"))
                    k.link(f(t["v"][0:w], bank4(1, P, w), ACT.Copy))
                    k.settle()
                    for what in (free[0], free[1], sig("kv_copied")):
                        act.nop().then_inc(what, 1)
                out_norm()
                merge(2)

                k.next(sig("x_sums"))
                f(halves(RSTD), B[:, 0:2, 0:HALF], ACT.Sqrt, scale=1.0 / D, bias=epsc).then_inc(sig("root_ready"), 1)
                high_parts(3 * KD)
                for half in range(2):
                    def gate(s, g, j):
                        if j == 0:
                            k.next(sig("ffn_slot_free"))
                            wait_tile(s, g)
                            f(halves(FT[:, 0, :]), gp(s), ACT.Silu).then_inc(sig("ffn_gate"), 1)
                    pairs(f"gu{half}", 0, 22, gate, {sig("ffn_slot_free"): 1})
        clear()

    with nc.Block() as block:
        @block.scalar
        def _(act):
            for i in range(KD):
                if i >= 2:
                    act.wait_ge(sig("square_slot_free"), i - 1)
                act.activation(sq_m[i % 2], X[:, i, :], ACT.Square).then_inc(sig("square_ready"), 1)
            act.wait_ge(sig("square_slot_free"), KD)
            act.activation(halves(wide[0]), B[:, 0:2, 0:HALF], ACT.Sqrt, scale=1.0 / D, bias=epsc
                           ).then_inc(sig("root_ready"), 1)

        @block.tensor
        def _(pe):
            for i in range(KD):
                pe.wait_ge(sig("square_ready"), i + 1)
                for h in range(2):
                    mm = pe.matmul(B[:, h, 0:HALF], ones, sq_m[i % 2][:, h * HALF:(h + 1) * HALF],
                                   start=i == 0, stop=i == KD - 1)
                mm.then_inc(sig("square_slot_free"), 1)

        @block.vector
        def _(dve):
            k = Counts(dve, own["vector"])
            dve.wait_ge(sig("root_ready"), 1)
            k.link(dve.reciprocal(wide[0], wide[0]))
            k.settle()
            for i in range(KD):
                dve.scalar_tensor_tensor(out=X[:, i, :], in0=X[:, i, :], scalar=FN[:, i:i + 1], in1=wide[0],
                                         op0=ALU.mult, op1=ALU.mult).then_inc(sig("y_ready"), 1)

        @block.sync
        def _(sp):
            for i in range(KD):
                sp.wait_ge(sig("y_ready"), i + 1)
                sp.dma_start(y_out[:, i, :], X[:, i, :]).then_inc(sig("stored_y"), 16)
            sp.wait_ge(sig("stored_y"), 16 * KD)

    ctx.close()


def _halves(prompt, sample):
    s = sample.reshape((SW,) + sample.shape[2:])
    return np.concatenate([prompt[:PH], s[:SH], prompt[PH:], s[SH:]])


def _tiles(w):
    L, K, N = w.shape
    return np.ascontiguousarray(w.reshape(L, K // P, P, N // P, P).transpose(0, 3, 2, 1, 4)).reshape(L, N // P, P, K)


def _cols(a):
    return np.swapaxes(a.reshape(a.shape[:-1] + (-1, P)), -1, -2)


def kernel(**inputs):
    import concourse.bacc as bacc
    from concourse.bass_utils import run_bass_kernel_spmd

    i = {n: np.asarray(a) for n, a in inputs.items()}
    f = np.float32
    arrays = {"consts": constants()}
    x = _halves(i["x_prompt"][0], i["x_sample"])
    arrays["x"] = np.ascontiguousarray(x.reshape(T, KD, P).transpose(2, 1, 0))
    cc = np.concatenate([i["c_prompt"], i["c_sample"]])
    arrays["c"] = np.ascontiguousarray(cc.reshape(1 + NS, KD, P).transpose(2, 1, 0))
    par = np.zeros((DEPTH, P, P_W), f)
    par[:, :, P_CONV:P_NMIX] = i["conv_w"].reshape(DEPTH, CONV_W, NCQ, P).transpose(0, 3, 2, 1).reshape(DEPTH, P, -1)
    par[:, :, P_NMIX:P_NFFN] = _cols(i["norm_mix"])
    par[:, :, P_NFFN:P_BADA] = _cols(i["norm_ffn"])
    par[:, :, P_BADA:P_GNORM] = _cols(i["b_ada"])
    par[:, :, P_GNORM] = i["gdn_norm"]
    par[:, :, P_HNORM] = i["hgrn_norm"]
    par[:, 0:H, P_ALOG] = i["gdn_a_log"]
    par[:, 0:H, P_DT] = i["gdn_dt_bias"]
    arrays["params"] = par
    arrays["fnorm"] = np.ascontiguousarray(_cols(i["final_norm"]))
    arrays["lb"] = np.ascontiguousarray(_cols(i["hgrn_lb"]).transpose(1, 0, 2))
    arrays["conv"] = np.ascontiguousarray(
        i["state_gdn_conv"].reshape(DEPTH, NS, 3, NCQ, P).transpose(0, 4, 3, 1, 2)).reshape(DEPTH, P, NCQ, NS * 3)
    w = i["w_in"]
    mk = H * P
    ab = np.zeros((DEPTH, D, P), f)
    ab[:, :, 0:H] = w[:, :, 4 * mk:4 * mk + H]
    ab[:, :, 32:32 + H] = w[:, :, 4 * mk + H:4 * mk + 2 * H]
    o = 4 * mk + 2 * H
    arrays["w_first"] = _tiles(np.concatenate([ab, w[:, :, :4 * mk]], 2))
    arrays["w_ret"] = _tiles(w[:, :, o:o + 4 * mk])
    arrays["w_hg"] = _tiles(w[:, :, o + 4 * mk:o + 8 * mk])
    gate = _tiles(w[:, :, o + 8 * mk:]).reshape(DEPTH, 3, KD, P, D)
    branch = _tiles(i["w_branch"].reshape(DEPTH * 3, mk, D)).reshape(DEPTH, 3, KD, P, mk)
    both = np.concatenate([gate, branch], -1).reshape(DEPTH, 3, KD, P, 2, -1)
    arrays["w_merge"] = np.ascontiguousarray(both.transpose(0, 1, 2, 4, 3, 5))
    arrays["w_out"] = _tiles(i["w_out"])
    gu = _tiles(i["w_gate_up"]).reshape(DEPTH, 2, 2, KF, P, D)
    arrays["w_gu"] = np.ascontiguousarray(gu.transpose(0, 2, 3, 1, 4, 5)).reshape(DEPTH, 2, 2 * KF, P, D)
    dn = _tiles(i["w_down"]).reshape(DEPTH, KD, P, 2, KF * P)
    arrays["w_dn"] = np.ascontiguousarray(dn.transpose(0, 3, 1, 2, 4))
    wa = i["w_ada"]
    arrays["w_ada_first"] = np.ascontiguousarray(
        wa[:, :, :2 * D].reshape(DEPTH, KD, P, 4, 4 * P).transpose(0, 3, 2, 1, 4)).reshape(DEPTH, 4, P, -1)
    arrays["w_ada"] = _tiles(wa[:, :, 2 * D:])
    for n, s in (("s_gdn", "state_gdn"), ("s_ret", "state_ret"), ("s_hg", "state_hgrn")):
        arrays[n] = np.ascontiguousarray(i[s])

    outs = {"y": (P, KD, T), "gdn_p": (DEPTH, H, P, P), "conv_new_": (DEPTH, P, NCQ, 3 + NS * 3), "ret_p": (DEPTH, H, P, P),
            "hg_p": (DEPTH, H, P, P), "gdn_s": (DEPTH, NS, H, P, P), "ret_s": (DEPTH, NS, H, P, P),
            "hg_s": (DEPTH, NS, H, P, P)}
    nc = bacc.Bacc("TRN2", target_bir_lowering=False, num_devices=1)
    args = [nc.dram_tensor(f"in_{n}", a.shape, F32, kind="ExternalInput").ap() for n, a in arrays.items()]
    args += [nc.dram_tensor(f"out_{n}", s, F32, kind="ExternalOutput").ap() for n, s in outs.items()]
    trunk(nc, *args)
    r = run_bass_kernel_spmd(nc, [{f"in_{n}": a for n, a in arrays.items()}], core_ids=[0])
    got = {n: np.asarray(r.results[0][f"out_{n}"]) for n in outs}
    y = got["y"].transpose(2, 1, 0).reshape(2, HALF, D)
    y_prompt = np.ascontiguousarray(y[:, :PH]).reshape(1, SEQ, D)
    y_sample = np.ascontiguousarray(y[:, PH:]).reshape(NS, LS, D)
    cv = got["conv_new_"].transpose(0, 3, 2, 1).reshape(DEPTH, 3 + NS * 3, NCQ * P)
    conv_p = np.ascontiguousarray(cv[:, :3]).reshape(DEPTH, 1, 3, NCQ * P)
    conv_s = np.ascontiguousarray(cv[:, 3:]).reshape(DEPTH, NS, 3, NCQ * P)
    one = {n: got[n].reshape(DEPTH, 1, H, P, P) for n in ("gdn_p", "ret_p", "hg_p")}
    return (y_prompt, y_sample, one["gdn_p"], conv_p, one["ret_p"], one["hg_p"],
            got["gdn_s"], conv_s, got["ret_s"], got["hg_s"])
```
